# Optimizing a Trainium2 kernel written in Bass

```python
import jax, jax.numpy as jnp
from jax import lax
import numpy as np

D_MODEL = 1024
BATCH = 1
SEQ = 256
DEPTH = 1

CTX_LEN = 256
GRID_W = 64
D_CONV = 1024
CONV_W = 3
N_Q_HEADS = 8
N_KV_HEADS = 2
HEAD_DIM = 128
GROUP = N_Q_HEADS // N_KV_HEADS
ROPE_THETA = 10000.0
D_FF = 2816
Q_BLOCK = 128
EPS = 1e-6
N_MOD = 9

Q_W = N_Q_HEADS * HEAD_DIM
KV_W = N_KV_HEADS * HEAD_DIM
PIECE_WIDTHS = (D_CONV, D_CONV, D_CONV, Q_W, KV_W, KV_W, 2 * D_MODEL)
D_IN = int(sum(PIECE_WIDTHS))
SPLITS = tuple(int(s) for s in np.cumsum(PIECE_WIDTHS)[:-1])


def rms_norm(x, g):
    xf = x.astype(jnp.float32)
    y = xf * lax.rsqrt(jnp.mean(xf * xf, axis=-1, keepdims=True) + EPS)
    return (y * g.astype(jnp.float32)).astype(x.dtype)

def modulate(h, shift, scale):
    return h * (1.0 + scale) + shift

def swiglu(h, w_in, w_out):
    a, b = jnp.split(h @ w_in, 2, axis=-1)
    return (jax.nn.silu(a) * b) @ w_out

def axial_rope_tables(n_tokens):
    rows = n_tokens // GRID_W
    row = jnp.repeat(jnp.arange(rows), GRID_W).astype(jnp.float32)
    col = jnp.tile(jnp.arange(GRID_W), rows).astype(jnp.float32)
    n_freq = HEAD_DIM // 4
    inv = ROPE_THETA ** (-jnp.arange(n_freq, dtype=jnp.float32) / n_freq)
    ang = jnp.stack([row[:, None] * inv, col[:, None] * inv], axis=1)
    return jnp.cos(ang), jnp.sin(ang)

def apply_axial_rope(x, cos, sin):
    xs = x.reshape(x.shape[:3] + (2, 2, HEAD_DIM // 4))
    x1, x2 = xs[..., 0, :], xs[..., 1, :]
    c = cos[None, :, None].astype(x.dtype)
    s = sin[None, :, None].astype(x.dtype)
    out = jnp.stack([x1 * c - x2 * s, x2 * c + x1 * s], axis=-2)
    return out.reshape(x.shape)

def short_conv(u, w):
    L = u.shape[1]
    pad = CONV_W // 2
    up = jnp.pad(u, ((0, 0), (pad, pad), (0, 0)))
    y = up[:, 0:L] * w[0]
    for j in range(1, CONV_W):
        y = y + up[:, j:j + L] * w[j]
    return y

def conv_branch(bg, cg, vc, conv_w):
    return bg * short_conv(cg * vc, conv_w)

def gqa_attend(q, k, v):
    s = jnp.einsum('btkgd,blkd->bkgtl', q, k, preferred_element_type=jnp.float32) * (HEAD_DIM ** -0.5)
    p = jax.nn.softmax(s, axis=-1).astype(v.dtype)
    return jnp.einsum('bkgtl,blkd->btkgd', p, v)

def latent_attention(q_lat, k_all, v_all):
    B, S = q_lat.shape[:2]
    nblk = S // Q_BLOCK
    qb = q_lat.reshape(B, nblk, Q_BLOCK, N_KV_HEADS, GROUP, HEAD_DIM).swapaxes(0, 1)
    ob = lax.map(lambda qi: gqa_attend(qi, k_all, v_all), qb)
    return ob.swapaxes(0, 1).reshape(B, S, Q_W)

def split_heads(q, k, v, q_g, k_g):
    B, L = q.shape[:2]
    q = rms_norm(q.reshape(B, L, N_Q_HEADS, HEAD_DIM), q_g)
    k = rms_norm(k.reshape(B, L, N_KV_HEADS, HEAD_DIM), k_g)
    v = v.reshape(B, L, N_KV_HEADS, HEAD_DIM)
    return q, k, v

def merge_branches(y_conv, o_attn, gate_logits, w_bc, w_ba, w_out):
    g_conv, g_attn = jnp.split(jax.nn.sigmoid(gate_logits), 2, axis=-1)
    return (g_conv * (y_conv @ w_bc) + g_attn * (o_attn @ w_ba)) @ w_out

def first_inputs(seed: int = 0) -> dict:
    key = jax.random.key(seed)
    ks = jax.random.split(key, 24)

    def nrm(k, shape, scale):
        return jax.random.normal(k, shape, jnp.float32) * scale

    def gain(k, shape):
        return 1.0 + 0.1 * jax.random.normal(k, shape, jnp.float32)

    L = DEPTH
    return {
        "x": nrm(ks[0], (BATCH, SEQ, D_MODEL), 1.0),
        "c": nrm(ks[1], (BATCH, D_MODEL), 1.0),
        "ctx": nrm(ks[2], (BATCH, CTX_LEN, D_MODEL), 1.0),
        "c_ctx": nrm(ks[3], (D_MODEL,), 1.0),
        "w_mod": nrm(ks[4], (L, D_MODEL, N_MOD * D_MODEL), 0.5 * D_MODEL ** -0.5),
        "b_mod": nrm(ks[5], (L, N_MOD * D_MODEL), 0.02),
        "norm1_g": gain(ks[6], (L, D_MODEL)),
        "norm2_g": gain(ks[7], (L, D_MODEL)),
        "norm3_g": gain(ks[8], (L, D_MODEL)),
        "ffn1_w_in": nrm(ks[9], (L, D_MODEL, 2 * D_FF), D_MODEL ** -0.5),
        "ffn1_w_out": nrm(ks[10], (L, D_FF, D_MODEL), D_FF ** -0.5),
        "w_in": nrm(ks[11], (L, D_MODEL, D_IN), D_MODEL ** -0.5),
        "conv_w": nrm(ks[12], (L, CONV_W, D_CONV), CONV_W ** -0.5),
        "q_norm_g": gain(ks[13], (L, HEAD_DIM)),
        "k_norm_g": gain(ks[14], (L, HEAD_DIM)),
        "w_branch_conv": nrm(ks[15], (L, D_CONV, D_MODEL), D_CONV ** -0.5),
        "w_branch_attn": nrm(ks[16], (L, Q_W, D_MODEL), Q_W ** -0.5),
        "w_out": nrm(ks[17], (L, D_MODEL, D_MODEL), D_MODEL ** -0.5),
        "ffn2_w_in": nrm(ks[18], (L, D_MODEL, 2 * D_FF), D_MODEL ** -0.5),
        "ffn2_w_out": nrm(ks[19], (L, D_FF, D_MODEL), D_FF ** -0.5),
        "final_g": gain(ks[20], (D_MODEL,)),
    }

def first_block(x, c, ctx, c_ctx, w_mod, b_mod, norm1_g, norm2_g, norm3_g,
              ffn1_w_in, ffn1_w_out, w_in, conv_w, q_norm_g, k_norm_g,
              w_branch_conv, w_branch_attn, w_out, ffn2_w_in, ffn2_w_out, final_g):
    B, S, _ = x.shape
    cos, sin = axial_rope_tables(S)
    cx = ctx
    for layer in range(DEPTH):
        last = layer == DEPTH - 1
        mod_lat = (jax.nn.silu(c) @ w_mod[layer] + b_mod[layer])[:, None, :]
        mod_ctx = (jax.nn.silu(c_ctx) @ w_mod[layer] + b_mod[layer])[None, None, :]
        ml = jnp.split(mod_lat, N_MOD, axis=-1)
        mc = jnp.split(mod_ctx, N_MOD, axis=-1)

        x = x + 0.5 * ml[2] * swiglu(modulate(rms_norm(x, norm1_g[layer]), ml[0], ml[1]),
                                      ffn1_w_in[layer], ffn1_w_out[layer])
        cx = cx + 0.5 * mc[2] * swiglu(modulate(rms_norm(cx, norm1_g[layer]), mc[0], mc[1]),
                                        ffn1_w_in[layer], ffn1_w_out[layer])

        hx = modulate(rms_norm(x, norm2_g[layer]), ml[3], ml[4])
        hc = modulate(rms_norm(cx, norm2_g[layer]), mc[3], mc[4])
        bg_l, cg_l, vc_l, q_l, k_l, v_l, gt_l = jnp.split(hx @ w_in[layer], SPLITS, axis=-1)
        bg_c, cg_c, vc_c, q_c, k_c, v_c, gt_c = jnp.split(hc @ w_in[layer], SPLITS, axis=-1)

        y_conv_l = conv_branch(bg_l, cg_l, vc_l, conv_w[layer])

        q_l, k_l, v_l = split_heads(q_l, k_l, v_l, q_norm_g[layer], k_norm_g[layer])
        q_c, k_c, v_c = split_heads(q_c, k_c, v_c, q_norm_g[layer], k_norm_g[layer])
        q_l = apply_axial_rope(q_l, cos, sin)
        k_l = apply_axial_rope(k_l, cos, sin)
        k_all = jnp.concatenate([k_c, k_l], axis=1)
        v_all = jnp.concatenate([v_c, v_l], axis=1)
        o_l = latent_attention(q_l, k_all, v_all)

        x = x + ml[5] * merge_branches(y_conv_l, o_l, gt_l, w_branch_conv[layer],
                                       w_branch_attn[layer], w_out[layer])

        if not last:
            y_conv_c = conv_branch(bg_c, cg_c, vc_c, conv_w[layer])
            o_c = gqa_attend(q_c.reshape(B, cx.shape[1], N_KV_HEADS, GROUP, HEAD_DIM), k_c, v_c)
            o_c = o_c.reshape(B, cx.shape[1], Q_W)
            cx = cx + mc[5] * merge_branches(y_conv_c, o_c, gt_c, w_branch_conv[layer],
                                             w_branch_attn[layer], w_out[layer])
            cx = cx + 0.5 * mc[8] * swiglu(modulate(rms_norm(cx, norm3_g[layer]), mc[6], mc[7]),
                                            ffn2_w_in[layer], ffn2_w_out[layer])

        x = x + 0.5 * ml[8] * swiglu(modulate(rms_norm(x, norm3_g[layer]), ml[6], ml[7]),
                                      ffn2_w_in[layer], ffn2_w_out[layer])
    return rms_norm(x, final_g)


N_HEADS = 8
HEAD_DIM_2 = 64
N_KV = 2
GROUP_2 = N_HEADS // N_KV
ROT_DIM = HEAD_DIM_2 // 4
ROPE_THETA_2 = 500000.0
CMP_BLOCK = 32
CMP_STRIDE = 16
CMP_HIDDEN = 4 * HEAD_DIM_2
SEL_BLOCK = 64
SEL_TOPK = 16
WINDOW = 512
N_NSA_BRANCHES = 3
ATTN_WIDTH = N_HEADS * HEAD_DIM_2
KV_WIDTH = N_KV * HEAD_DIM_2
POOL_WIDTH = 512
POOL_WINDOWS = (2, 4, 8, 16)
POOL_GROUP = POOL_WIDTH // len(POOL_WINDOWS)
D_FF_2 = 4 * D_MODEL
IN_SIZES = (ATTN_WIDTH, 6 * KV_WIDTH, N_NSA_BRANCHES * N_HEADS, POOL_WIDTH, 2 * D_MODEL)
IN_WIDTH = sum(IN_SIZES)
NEG_INF = -1e30
FORCE_SCORE = 1e4


def rms_norm_2(x, g):
    xf = x.astype(jnp.float32)
    y = xf * lax.rsqrt(jnp.mean(xf * xf, axis=-1, keepdims=True) + EPS)
    return (y * g.astype(jnp.float32)).astype(x.dtype)

def rope(x, pos):
    inv = ROPE_THETA_2 ** (-jnp.arange(0, ROT_DIM, 2, dtype=jnp.float32) / ROT_DIM)
    ang = pos.astype(jnp.float32)[:, None] * inv
    cos, sin = jnp.cos(ang), jnp.sin(ang)
    xr = x[..., :ROT_DIM].astype(jnp.float32)
    x1, x2 = xr[..., :ROT_DIM // 2], xr[..., ROT_DIM // 2:]
    rot = jnp.concatenate([x1 * cos - x2 * sin, x2 * cos + x1 * sin], axis=-1)
    return jnp.concatenate([rot.astype(x.dtype), x[..., ROT_DIM:]], axis=-1)

def masked_softmax(s, mask):
    s = jnp.where(mask, s.astype(jnp.float32), NEG_INF)
    e = jnp.exp(s - jnp.max(s, axis=-1, keepdims=True)) * mask
    return e / jnp.maximum(jnp.sum(e, axis=-1, keepdims=True), 1e-30)

def cmp_to_sel_matrix(S):
    n_cmp = (S - CMP_BLOCK) // CMP_STRIDE + 1
    n_sel = S // SEL_BLOCK
    cs = np.arange(n_cmp)[:, None] * CMP_STRIDE
    js = np.arange(n_sel)[None, :] * SEL_BLOCK
    ov = np.clip(np.minimum(cs + CMP_BLOCK, js + SEL_BLOCK) - np.maximum(cs, js), 0, None)
    return jnp.asarray((ov / CMP_STRIDE).astype(np.float32))

def compress_blocks(k, pe, w1, w2):
    B, G, S, dh = k.shape
    ratio = CMP_BLOCK // CMP_STRIDE
    chunks = k.reshape(B, G, S // CMP_STRIDE, CMP_STRIDE, dh)
    n_cmp = S // CMP_STRIDE - ratio + 1
    blocks = jnp.concatenate([chunks[:, :, j:j + n_cmp] for j in range(ratio)], axis=3)
    flat = (blocks + pe).reshape(B, G, n_cmp, CMP_BLOCK * dh)
    return jax.nn.gelu(flat @ w1) @ w2

def nsa_attention(q_flat, kv_flat, gate_logits, pe_k, pe_v, ck_w1, ck_w2, cv_w1, cv_w2):
    B, S, _ = q_flat.shape
    dt = q_flat.dtype
    scale = HEAD_DIM_2 ** -0.5
    t = jnp.arange(S)
    q = rope(q_flat.reshape(B, S, N_KV, GROUP_2, HEAD_DIM_2).transpose(0, 2, 3, 1, 4), t)

    def kv_heads(a):
        return a.reshape(B, S, N_KV, HEAD_DIM_2).transpose(0, 2, 1, 3)

    kc, vc, ks, vs, kw, vw = [kv_heads(a) for a in jnp.split(kv_flat, 6, axis=-1)]
    ks = rope(ks, t)
    kw = rope(kw, t)

    n_cmp = (S - CMP_BLOCK) // CMP_STRIDE + 1
    pos_c = jnp.arange(n_cmp) * CMP_STRIDE + CMP_BLOCK - 1
    k_cmp = rope(compress_blocks(kc, pe_k, ck_w1, ck_w2), pos_c)
    v_cmp = compress_blocks(vc, pe_v, cv_w1, cv_w2)
    s = jnp.einsum('bgrsd,bgcd->bgrsc', q, k_cmp) * scale
    p_cmp = masked_softmax(s, pos_c[None, :] <= t[:, None])
    o_cmp = jnp.einsum('bgrsc,bgcd->bgrsd', p_cmp.astype(dt), v_cmp)

    n_sel = S // SEL_BLOCK
    top = min(SEL_TOPK, n_sel)
    imp = jnp.einsum('bgrsc,cj->bgsj', p_cmp, cmp_to_sel_matrix(S))
    blk = jnp.arange(n_sel)[None, :]
    cur = (t // SEL_BLOCK)[:, None]
    imp = jnp.where(blk > cur, -FORCE_SCORE, imp)
    imp = jnp.where((blk == 0) | (blk == cur) | (blk == cur - 1), FORCE_SCORE, imp)
    _, sel_idx = lax.top_k(imp, top)

    nq = S // Q_BLOCK
    q_blocks = q.reshape(B, N_KV, GROUP_2, nq, Q_BLOCK, HEAD_DIM_2).transpose(3, 0, 1, 2, 4, 5)
    idx_blocks = sel_idx.reshape(B, N_KV, nq, Q_BLOCK, top).transpose(2, 0, 1, 3, 4)
    ks_blk = ks.reshape(B, N_KV, n_sel, SEL_BLOCK, HEAD_DIM_2)
    vs_blk = vs.reshape(B, N_KV, n_sel, SEL_BLOCK, HEAD_DIM_2)
    pad = ((0, 0), (0, 0), (WINDOW, 0), (0, 0))
    kw_pad = jnp.pad(kw, pad)
    vw_pad = jnp.pad(vw, pad)
    bi = jnp.arange(B)[:, None, None, None]
    gi = jnp.arange(N_KV)[None, :, None, None]
    offs = jnp.arange(SEL_BLOCK)
    band = WINDOW + Q_BLOCK

    def step(args):
        i, qb, ib = args
        qpos = i * Q_BLOCK + jnp.arange(Q_BLOCK)
        k_sel = ks_blk[bi, gi, ib].reshape(B, N_KV, Q_BLOCK, top * SEL_BLOCK, HEAD_DIM_2)
        v_sel = vs_blk[bi, gi, ib].reshape(B, N_KV, Q_BLOCK, top * SEL_BLOCK, HEAD_DIM_2)
        kpos = (ib[..., None] * SEL_BLOCK + offs).reshape(B, N_KV, Q_BLOCK, top * SEL_BLOCK)
        s_sel = jnp.einsum('bgrqd,bgqkd->bgrqk', qb, k_sel) * scale
        p_sel = masked_softmax(s_sel, (kpos <= qpos[:, None])[:, :, None])
        o_sel = jnp.einsum('bgrqk,bgqkd->bgrqd', p_sel.astype(dt), v_sel)
        k_win = lax.dynamic_slice_in_dim(kw_pad, i * Q_BLOCK, band, axis=2)
        v_win = lax.dynamic_slice_in_dim(vw_pad, i * Q_BLOCK, band, axis=2)
        wpos = i * Q_BLOCK - WINDOW + jnp.arange(band)
        dist = qpos[:, None] - wpos[None, :]
        wmask = (dist >= 0) & (dist < WINDOW) & (wpos >= 0)[None, :]
        s_win = jnp.einsum('bgrqd,bgkd->bgrqk', qb, k_win) * scale
        p_win = masked_softmax(s_win, wmask)
        o_win = jnp.einsum('bgrqk,bgkd->bgrqd', p_win.astype(dt), v_win)
        return o_sel, o_win

    o_sel, o_win = lax.map(step, (jnp.arange(nq), q_blocks, idx_blocks))
    o_sel = o_sel.transpose(1, 2, 3, 0, 4, 5).reshape(B, N_KV, GROUP_2, S, HEAD_DIM_2)
    o_win = o_win.transpose(1, 2, 3, 0, 4, 5).reshape(B, N_KV, GROUP_2, S, HEAD_DIM_2)

    g = jax.nn.sigmoid(gate_logits).reshape(B, S, N_NSA_BRANCHES, N_KV, GROUP_2).transpose(2, 0, 3, 4, 1)[..., None]
    o = g[0] * o_cmp + g[1] * o_sel + g[2] * o_win
    return o.transpose(0, 3, 1, 2, 4).reshape(B, S, ATTN_WIDTH)

def pool_mixer(u, w_pool, pool_scale):
    B, S, _ = u.shape
    uf = u.astype(jnp.float32)
    csp = jnp.concatenate([jnp.zeros((B, 1, POOL_WIDTH), jnp.float32), jnp.cumsum(uf, axis=1)], axis=1)
    t = jnp.arange(S)
    outs = []
    for gidx, w in enumerate(POOL_WINDOWS):
        lo, hi = gidx * POOL_GROUP, (gidx + 1) * POOL_GROUP
        c = csp[..., lo:hi]
        lower = jnp.concatenate([jnp.zeros((B, w - 1, POOL_GROUP), jnp.float32), c[:, :S - w + 1]], axis=1)
        cnt = jnp.minimum(t + 1, w).astype(jnp.float32)[:, None]
        outs.append((c[:, 1:] - lower) / cnt - uf[..., lo:hi])
    pooled = jnp.stack(outs, axis=2).astype(u.dtype)
    mixed = jnp.einsum('bsgc,gcd->bsgd', pooled, w_pool).reshape(B, S, POOL_WIDTH)
    return mixed * pool_scale

def hybrid_layer(x, norm_mix, w_in, cmp_pe_k, cmp_pe_v, cmp_k_w1, cmp_k_w2, cmp_v_w1, cmp_v_w2,
                 w_branch_attn, pool_w, pool_scale, w_branch_pool, w_out, norm_mlp, w_ff1, w_ff2):
    h = rms_norm_2(x, norm_mix)
    proj = h @ w_in
    q_flat, kv_flat, g_attn, u_pool, g_merge = jnp.split(proj, np.cumsum(IN_SIZES)[:-1].tolist(), axis=-1)
    a = nsa_attention(q_flat, kv_flat, g_attn, cmp_pe_k, cmp_pe_v, cmp_k_w1, cmp_k_w2, cmp_v_w1, cmp_v_w2) @ w_branch_attn
    b = pool_mixer(u_pool, pool_w, pool_scale) @ w_branch_pool
    ga, gb = jnp.split(jax.nn.sigmoid(g_merge), 2, axis=-1)
    x = x + (ga * a + gb * b) @ w_out
    h = rms_norm_2(x, norm_mlp)
    return x + jnp.square(jax.nn.relu(h @ w_ff1)) @ w_ff2

def second_inputs(seed: int = 0) -> dict:
    key = jax.random.key(seed)
    ks = jax.random.split(key, 20)
    f32 = jnp.float32

    def nrm(k, shape, fan_in):
        return jax.random.normal(k, shape, f32) * (fan_in ** -0.5)

    def gain(k, shape):
        return 1.0 + 0.05 * jax.random.normal(k, shape, f32)

    L = DEPTH
    return {
        "x": jax.random.normal(ks[0], (BATCH, SEQ, D_MODEL), f32),
        "norm_mix": gain(ks[1], (L, D_MODEL)),
        "w_in": nrm(ks[2], (L, D_MODEL, IN_WIDTH), D_MODEL),
        "cmp_pe_k": 0.02 * jax.random.normal(ks[3], (L, CMP_BLOCK, HEAD_DIM_2), f32),
        "cmp_pe_v": 0.02 * jax.random.normal(ks[4], (L, CMP_BLOCK, HEAD_DIM_2), f32),
        "cmp_k_w1": nrm(ks[5], (L, CMP_BLOCK * HEAD_DIM_2, CMP_HIDDEN), CMP_BLOCK * HEAD_DIM_2),
        "cmp_k_w2": nrm(ks[6], (L, CMP_HIDDEN, HEAD_DIM_2), CMP_HIDDEN),
        "cmp_v_w1": nrm(ks[7], (L, CMP_BLOCK * HEAD_DIM_2, CMP_HIDDEN), CMP_BLOCK * HEAD_DIM_2),
        "cmp_v_w2": nrm(ks[8], (L, CMP_HIDDEN, HEAD_DIM_2), CMP_HIDDEN),
        "w_branch_attn": nrm(ks[9], (L, ATTN_WIDTH, D_MODEL), ATTN_WIDTH),
        "pool_w": nrm(ks[10], (L, len(POOL_WINDOWS), POOL_GROUP, POOL_GROUP), POOL_GROUP),
        "pool_scale": 1.0 + 0.1 * jax.random.normal(ks[11], (L, POOL_WIDTH), f32),
        "w_branch_pool": nrm(ks[12], (L, POOL_WIDTH, D_MODEL), POOL_WIDTH),
        "w_out": nrm(ks[13], (L, D_MODEL, D_MODEL), D_MODEL),
        "norm_mlp": gain(ks[14], (L, D_MODEL)),
        "w_ff1": nrm(ks[15], (L, D_MODEL, D_FF_2), D_MODEL),
        "w_ff2": nrm(ks[16], (L, D_FF_2, D_MODEL), D_FF_2),
        "norm_final": gain(ks[17], (D_MODEL,)),
    }

def second_block(x, norm_mix, w_in, cmp_pe_k, cmp_pe_v, cmp_k_w1, cmp_k_w2, cmp_v_w1, cmp_v_w2,
              w_branch_attn, pool_w, pool_scale, w_branch_pool, w_out, norm_mlp, w_ff1, w_ff2,
              norm_final):
    for l in range(DEPTH):
        x = hybrid_layer(x, norm_mix[l], w_in[l], cmp_pe_k[l], cmp_pe_v[l], cmp_k_w1[l], cmp_k_w2[l],
                         cmp_v_w1[l], cmp_v_w2[l], w_branch_attn[l], pool_w[l], pool_scale[l],
                         w_branch_pool[l], w_out[l], norm_mlp[l], w_ff1[l], w_ff2[l])
    return rms_norm_2(x, norm_final)


def setup_inputs(seed=0):
    out = dict(first_inputs(seed))
    for name, value in second_inputs(seed + 1).items():
        if name != "x":
            out[name + "_2"] = value
    return out


def reference(
    x, c, ctx, c_ctx, w_mod, b_mod, norm1_g, norm2_g, norm3_g, ffn1_w_in, ffn1_w_out, w_in,
    conv_w, q_norm_g, k_norm_g, w_branch_conv, w_branch_attn, w_out, ffn2_w_in, ffn2_w_out,
    final_g, norm_mix_2, w_in_2, cmp_pe_k_2, cmp_pe_v_2, cmp_k_w1_2, cmp_k_w2_2, cmp_v_w1_2,
    cmp_v_w2_2, w_branch_attn_2, pool_w_2, pool_scale_2, w_branch_pool_2, w_out_2, norm_mlp_2,
    w_ff1_2, w_ff2_2, norm_final_2,
):
    x = first_block(
        x, c, ctx, c_ctx, w_mod, b_mod, norm1_g, norm2_g, norm3_g, ffn1_w_in, ffn1_w_out, w_in,
        conv_w, q_norm_g, k_norm_g, w_branch_conv, w_branch_attn, w_out, ffn2_w_in, ffn2_w_out,
        final_g,
    )
    return second_block(
        x, norm_mix_2, w_in_2, cmp_pe_k_2, cmp_pe_v_2, cmp_k_w1_2, cmp_k_w2_2, cmp_v_w1_2,
        cmp_v_w2_2, w_branch_attn_2, pool_w_2, pool_scale_2, w_branch_pool_2, w_out_2,
        norm_mlp_2, w_ff1_2, w_ff2_2, norm_final_2,
    )


_drawn_inputs = setup_inputs


def setup_inputs(seed=0):
    import zlib

    import numpy as np

    out = dict(_drawn_inputs(seed))
    spreads = {}
    factors = {'ctx': 5.715,
     'norm1_g': 3.085,
     'norm3_g': 3.623,
     'q_norm_g': 8.0,
     'k_norm_g': 8.0,
     'cmp_pe_k_2': 64.0,
     'cmp_pe_v_2': 8.0}
    for name, (base, spread) in spreads.items():
        noise = np.random.default_rng([zlib.crc32(name.encode()), seed]).standard_normal(out[name].shape)
        drawn = base * np.exp(spread * noise) if base else spread * noise
        out[name] = __import__('jax').numpy.asarray(drawn.astype(out[name].dtype))
    for name, factor in factors.items():
        out[name] = (out[name] * factor).astype(out[name].dtype)
    return out
```

```python
from contextlib import ExitStack

import concourse.bass as bass
from concourse import mybir

F32 = mybir.dt.float32
F32R = mybir.dt.float32r
ACT = mybir.ActivationFunctionType
ALU = mybir.AluOpType
AX_X = mybir.AxisListType.X
ds = bass.ds

P = 128
D = 1024
KD = D // P
S = 256
CTX = 256
NB = S + CTX
TT = S // P
EPS = 1e-6

D_FF = 2816
SLABS = (8, 8, 6)
HQ, HKV, HD = 8, 2, 128
GROUP = HQ // HKV
C_BG, C_CG, C_VC = 0, D, 2 * D
C_Q = 3 * D
C_K = C_Q + HQ * HD
C_V = C_K + HKV * HD
C_GATE = C_V + HKV * HD
N_MOD = 9
MOD_TILES = N_MOD * KD
MOD_UNITS = MOD_TILES // 2
MOD_FRONT = 8
MOD_RIDE = 10

H2, G2, R2H, DH = 8, 2, 4, 64
C2_KC = H2 * DH
C2_KS = C2_KC + 2 * G2 * DH
C2_KW = C2_KS + 2 * G2 * DH
C2_GATE = C2_KC + 6 * G2 * DH
C2_POOL = C2_GATE + 3 * H2
C2_MERGE = C2_POOL + 512
CB, CS = 32, 16
NC = (S - CB) // CS + 1
CH = 4 * DH
POOLS = (2, 4, 8, 16)
PAD = max(POOLS)
D_FF2 = 4 * D
SLABS2 = D_FF2 // (8 * P)

K_ID, K_R1, K_R2 = 0, P, 2 * P
K_C1, K_S1, K_C2, K_S2 = (3 * P + i * S for i in range(4))
K_MASK = 3 * P + 4 * S
K_CADD = K_MASK + TT * S
K_CMUL = K_CADD + TT * NC
K_CNT = K_CMUL + TT * NC
K_EPS = K_CNT + len(POOLS) * PAD
K_END = K_EPS + 1

V_N1, V_N2, V_N3, V_F1, V_MIX, V_MLP, V_F2 = (KD * i for i in range(7))
V_CONV = 7 * KD
V_PS = V_CONV + 3 * KD
V_QG = V_PS + 4
V_KG = V_QG + 1
V_END = V_KG + 1
PE_ROWS = 2 * CB
C_ROWS = PE_ROWS + 2 * KD

STAGES = (("ffn1", 34), ("k", 1), ("v", 1), ("q", 4), ("gates", 8), ("conv", 8), ("bg", 4), ("merge", 8),
          ("wout", 4), ("ffn2", 34), ("kcvc", 1), ("ksvs", 1), ("kwvw", 1), ("q2", 2), ("pool", 2),
          ("gates2", 8), ("merge2", 8), ("wout2", 4), ("ff", 32))
FIRST = {}
_n = 0
for _name, _units in STAGES:
    FIRST[_name] = _n
    _n += _units
UNITS = _n
SLOT = KD * 2 * P
HALF = SLOT // 2
LANDED = 48


def program(nc, a, out):
    with ExitStack() as ctx:
        def sb(name, shape, dt=F32):
            return ctx.enter_context(nc.sbuf_tensor(name, shape, dt))

        def sem(name):
            return ctx.enter_context(nc.semaphore(name))

        raw = sb("raw", [P, 2, SLOT])
        w_hi = sb("w_hi", [P, 2, SLOT], F32R)
        w_lo = sb("w_lo", [P, 2, SLOT], F32R)
        mraw = sb("mraw", [P, 2, SLOT])
        x = sb("x", [P, KD, NB])
        x_hi = sb("x_hi", [P, KD, NB], F32R)
        x_lo = sb("x_lo", [P, KD, NB], F32R)
        h_hi = sb("h_hi", [P, KD, NB], F32R)
        h_lo = sb("h_lo", [P, KD, NB], F32R)
        sq = sb("sq", [P, KD, NB])
        s1 = sb("s1", [P, 2, NB])
        t1 = sb("t1", [P, 2, NB])
        scr = sb("scr", [P, 4 * D])
        cst = sb("cst", [P, K_END])
        ones = sb("ones", [P, P])
        vec = sb("vec", [P, V_END])
        pec = sb("pec", [P, C_ROWS])
        bm = sb("bm", [P, MOD_TILES])
        bm_half = sb("bm_half", [P, MOD_TILES])
        sc = sb("sc", [P, KD, 2])
        mods = sb("mods", [P, MOD_TILES, 2])
        am = sb("am", [P, 3, KD, 2])
        gate_half = sb("gate_half", [P, 2, KD, 2])
        root = sb("root", [P, 32])
        rstd = sb("rstd", [P, 32])
        q_scale = sb("q_scale", [P, HQ * TT])
        q_cur = sb("q_cur", [P, 2, S])
        u_pad = sb("u_pad", [P, S + 2])
        top = sb("top", [P, 4])
        neg_top = sb("neg_top", [P, 8])
        total = sb("total", [P, 8])
        inv = sb("inv", [P, 8])
        p_pad = sb("p_pad", [P, PAD + S])
        wg = sb("wg", [P, KD, 3 * H2])
        wg_hi = sb("wg_hi", [P, KD, 3 * H2], F32R)
        wg_lo = sb("wg_lo", [P, KD, 3 * H2], F32R)
        g_tok = sb("g_tok", [P, TT, 3 * H2])
        w_pool = sb("w_pool", [P, 4, P])
        w2c = sb("w2c", [P, 2, 2, DH])
        hid = sb("hid", [P, 2, 2, G2 * NC])
        kc_r = sb("kc_r", [P, 2, NC])
        vc_tok = sb("vc_tok", [P, G2, DH])
        pc = sb("pc", [P, TT, P])
        sc_c = sb("sc_c", [P, TT, NC])

        ps_u = ctx.enter_context(nc.psum_tensor("ps_u", [P, 4, 512], F32))
        ps_a = ctx.enter_context(nc.psum_tensor("ps_a", [P, 4, 512], F32))

        sq_flat = sq[:].rearrange("p k n -> p (k n)")
        vec_rows = s1[0:V_END, 0, 0:P]
        pe_rows = s1[0:C_ROWS, 0, P:2 * P]
        bm_rows = s1[0:MOD_TILES, 0, 2 * P:3 * P]
        xt = scr[:].rearrange("p (t d) -> p t d", t=4)
        probs = scr[:, 0:2 * NB].rearrange("p (t n) -> p t n", t=2)
        probs_t = scr[:, 2 * NB:4 * NB].rearrange("p (k n) -> p k n", k=4)
        q_sq = scr[:, 4 * NB:8 * NB].rearrange("p (h n) -> p h n", h=HQ)
        q_rows = x[:, :, S:NB]
        k_all = sq[:, 0:2, :]
        v_feat = sq[:, 2:4, :]
        v_tok = sq_flat[:, 4 * NB:6 * NB].rearrange("p (k g d) -> p k g d", k=4, g=HKV)
        y_conv = scr[:, 4 * NB:8 * NB].rearrange("p (m n) -> p m n", m=KD)
        g_conv = mraw[:, 0, :].rearrange("p (m n) -> p m n", m=KD)
        g_attn = mraw[:, 1, :].rearrange("p (m n) -> p m n", m=KD)
        mixed = scr[:, 0:2 * NB].rearrange("p (i n) -> p i n", i=4)
        pooled = scr[:, 2 * NB:4 * NB].rearrange("p (i n) -> p i n", i=4)
        kk2 = scr[:, 4 * NB:5 * NB]
        v2_feat = scr[:, 5 * NB:6 * NB].rearrange("p (b n) -> p b n", b=2)
        v2_tok = scr[:, 6 * NB:7 * NB].rearrange("p (b k n) -> p b k n", b=2, k=2)
        cmp_k = scr[:, 7 * NB:7 * NB + CS * G2 * NC].rearrange("p (l g c) -> p l g c", l=CS, g=G2)
        cmp_v = s1[:, 0, 0:CS * G2 * NC].rearrange("p (l g c) -> p l g c", l=CS, g=G2)
        cmp_in = (cmp_k, cmp_v)
        q2 = x[:, 0:4, S:NB]
        gates2 = sq[:].rearrange("p m (a n) -> p m a n", a=2)
        ident = cst[:, K_ID:K_ID + P]
        swap1 = cst[:, K_R1:K_R1 + P]
        swap2 = cst[:, K_R2:K_R2 + P]
        cos1, sin1, cos2, sin2 = (cst[:, k:k + S] for k in (K_C1, K_S1, K_C2, K_S2))
        cadd = cst[:, K_CADD:K_CADD + TT * NC].rearrange("p (t c) -> p t c", t=TT)
        cmul = cst[:, K_CMUL:K_CMUL + TT * NC].rearrange("p (t c) -> p t c", t=TT)
        eps = cst[:, K_EPS:K_EPS + 1]
        mod_ps = ps_a[:, 0, 0:2 * MOD_TILES].rearrange("p (t s) -> p t s", s=2)

        def vcol(v, m):
            return vec[:, v + m:v + m + 1] if isinstance(m, int) else vec[:, ds(m + v, 1)]

        def segs(n):
            return [(0, slice(0, S))] if n == S else [(0, slice(0, S)), (1, slice(S, NB))]

        boot = sem("boot_landed")
        late = sem("late_landed")
        raw_landed = [sem("raw_landed0"), sem("raw_landed1")]
        mod_landed = [sem("mod_landed0"), sem("mod_landed1")]
        h_ready = sem("w_hi_ready")
        l_ready = sem("w_lo_ready")
        unit_done = sem("unit_done")
        drained = sem("unit_drained")
        mod_done = sem("mod_done")
        ones_ready = sem("ones_ready")
        vec_turned = sem("vec_turned")
        vec_ready = sem("vec_ready")
        sc_ready = sem("silu_c_ready")
        x_turned = sem("x_turned")
        x_copied = sem("x_copied")
        sq_ready = sem("squares_ready")
        stat_done = sem("stat_done")
        root_done = sem("root_done")
        recip_done = sem("recip_done")
        diag_done = sem("diag_done")
        rb_done = sem("rstd_spread")
        z_ready = sem("z_ready")
        xh_ready = sem("x_hi_ready")
        xl_ready = sem("x_lo_ready")
        x_normed = sem("x_normed")
        mods_ready = sem("mods_ready")
        gate_ready = sem("gate_ready")
        silu_done = sem("silu_done")
        prod_done = sem("prod_done")
        hh_done = sem("h_hi_done")
        k_squared = sem("k_squared")
        k_gained = sem("k_gained")
        kstat_done = sem("kstat_done")
        kroot_done = sem("kroot_done")
        krecip_done = sem("krecip_done")
        kdiag_done = sem("kdiag_done")
        krb_done = sem("k_rstd_spread")
        k_normed = sem("k_normed")
        k_swapped = sem("k_swapped")
        k_terms = sem("k_rope_terms")
        k_ready = sem("k_ready")
        v_turned = sem("v_turned")
        v_ready = sem("v_ready")
        q_squared = sem("q_squared")
        qstat_done = sem("qstat_done")
        qroot_done = sem("qroot_done")
        qrecip_done = sem("qrecip_done")
        q_scaled = sem("q_scale_ready")
        q_swapped = sem("q_swapped")
        q_terms = sem("q_rope_terms")
        gates_done = sem("gates_done")
        qcur_ready = sem("q_cur_ready")
        qk_done = sem("qk_done")
        top_done = sem("top_done")
        nb_ready = sem("neg_top_ready")
        exp_done = sem("exp_done")
        inv_done = sem("inv_done")
        p_ready = sem("probs_ready")
        t_done = sem("probs_turned")
        pta_ready = sem("probs_t_act_ready")
        ptd_ready = sem("probs_t_dve_ready")
        pv_done = sem("pv_done")
        oh_ready = sem("o_hi_ready")
        cg_copied = sem("cg_copied")
        u_ready = sem("conv_in_ready")
        conv_terms = sem("conv_terms")
        y_done = sem("y_done")
        yh_done = sem("y_hi_done")
        merge_terms = sem("merge_terms")
        zh_done = sem("z_hi_done")
        wg_done = sem("gate_w_hi_done")
        wg_ready = sem("gate_w_ready")
        gt_done = sem("gate_logits_done")
        gt_ready = sem("gate_tok_ready")
        cmp_ready = sem("cmp_in_ready")
        hid_done = sem("cmp_hidden_done")
        gelu_done = sem("cmp_gelu_done")
        cmp_done = sem("cmp_out_done")
        kc_raw = sem("k_cmp_raw")
        kv2_copied = sem("kv2_copied")
        rope2_swapped = sem("rope2_swapped")
        rope2_terms = sem("rope2_terms")
        rope2_done = sem("rope2_done")
        v2_turned = sem("v2_turned")
        pool_steps = sem("pool_steps")
        pooled_ready = sem("pooled_ready")
        mixed_done = sem("pool_mixed")
        ph_done = sem("pool_hi_done")
        pl_done = sem("pool_lo_done")
        g2_copied = sem("gates2_copied")
        g2_done = sem("gates2_done")
        masked = sem("scores_masked")
        cmp_masked = sem("cmp_masked")
        cmp_steps = sem("cmp_softmax_steps")
        coef_steps = sem("coef_steps")
        relu_done = sem("relu_done")
        y_turned = sem("y_turned")
        y_copied = sem("y_copied")
        stored = sem("stored")

        block = ctx.enter_context(nc.Block())


        BOOT = 16 * (1 + 4 + 2 + 2 + 7 + 1 + 1 + 2 + 1)

        @block.sync
        def _(sp):
            def weights(w):
                return w[0].rearrange("(k p) m -> p k m", p=P)

            def slot_free(pr, k):
                sp.wait_ge(l_ready, 4 * pr + (2 * k + 2))

            def wide(pr, k, w, col, kc0=0, kcs=KD):
                slot_free(pr, k)
                dst = raw[:, k % 2, 0:kcs * 2 * P].rearrange("p (k m) -> p k m", k=kcs)
                sp.dma_start(dst, w[:, ds(kc0, kcs), ds(col, 2 * P)]).then_inc(raw_landed[k % 2], LANDED)

            def tile(k, t, kcs):
                return raw[:, k % 2, 0:kcs * 2 * P].rearrange("p (k a c) -> p k a c", k=kcs, a=2)[:, :, t, :]

            def pair(pr, k, w0, col0, w1, col1, kcs=KD):
                slot_free(pr, k)
                sp.dma_start(tile(k, 0, kcs), w0[:, :, ds(col0, P)]).then_inc(raw_landed[k % 2], 16)
                sp.dma_start(tile(k, 1, kcs), w1[:, :, ds(col1, P)]).then_inc(raw_landed[k % 2], LANDED - 16)

            w_mod = weights(a["w_mod"])

            def mod(pr, km, wait=True):
                if wait:
                    sp.wait_ge(mod_done, 2 * pr + (km - 1))
                dst = mraw[:, km % 2, :].rearrange("p (k m) -> p k m", k=KD)
                sp.dma_start(dst, w_mod[:, :, ds(pr * (4 * P) + km * 2 * P, 2 * P)]).then_inc(mod_landed[km % 2], 16)

            mod(0, 0, wait=False)
            mod(0, 1, wait=False)
            with sp.Fori(1, MOD_FRONT // 2) as p:
                for j in range(2):
                    mod(p, j)

            def swiglu(base, w_in, w_out, ride):
                w_in, w_out = weights(w_in), weights(w_out)

                def slab(s, pr, k, chunks):
                    with sp.Fori(0, chunks // 2) as p:
                        for j in range(2):
                            col = s * (8 * P) + p * (2 * P) + j * P
                            pair(pr + p, k + j, w_in, col, w_in, col + D_FF)
                            if ride:
                                mod(s * (MOD_RIDE // 2) + p, MOD_FRONT + j)
                    for i in range(4):
                        wide(pr, k + chunks + i, w_out, i * 2 * P, s * 8, chunks)
                        if ride and i % 2 == 0:
                            mod(s * (MOD_RIDE // 2), MOD_FRONT + chunks + i // 2)

                with sp.Fori(0, 2) as s:
                    slab(s, s * 6, base, SLABS[0])
                slab(2, 0, base + 24, SLABS[2])

            swiglu(FIRST["ffn1"], a["ffn1_w_in"], a["ffn1_w_out"], True)

            w_in = weights(a["w_in"])
            wide(0, FIRST["k"], w_in, C_K)
            wide(0, FIRST["v"], w_in, C_V)
            with sp.Fori(0, 2) as p:
                for j in range(2):
                    wide(p, FIRST["q"] + j, w_in, C_Q + p * (4 * P) + j * 2 * P)
            with sp.Fori(0, 4) as p:
                for j in range(2):
                    col = p * (2 * P) + j * P
                    pair(p, FIRST["gates"] + j, w_in, col + C_GATE, w_in, col + (C_GATE + D))
            with sp.Fori(0, 4) as p:
                for j in range(2):
                    col = p * (2 * P) + j * P
                    pair(p, FIRST["conv"] + j, w_in, col + C_CG, w_in, col + C_VC)
            with sp.Fori(0, 2) as p:
                for j in range(2):
                    wide(p, FIRST["bg"] + j, w_in, C_BG + p * (4 * P) + j * 2 * P)
            w_bc, w_ba = weights(a["w_branch_conv"]), weights(a["w_branch_attn"])
            with sp.Fori(0, 4) as p:
                for j in range(2):
                    col = p * (2 * P) + j * P
                    pair(p, FIRST["merge"] + j, w_bc, col, w_ba, col)
            w_o = weights(a["w_out"])
            with sp.Fori(0, 2) as p:
                for j in range(2):
                    wide(p, FIRST["wout"] + j, w_o, p * (4 * P) + j * 2 * P)
            swiglu(FIRST["ffn2"], a["ffn2_w_in"], a["ffn2_w_out"], False)

            w_in2 = weights(a["w_in_2"])
            wide(0, FIRST["kcvc"], w_in2, C2_KC)
            wide(0, FIRST["ksvs"], w_in2, C2_KS)
            wide(0, FIRST["kwvw"], w_in2, C2_KW)
            for i in range(2):
                wide(0, FIRST["q2"] + i, w_in2, i * 2 * P)
            for i in range(2):
                wide(0, FIRST["pool"] + i, w_in2, C2_POOL + i * 2 * P)
            for i, name in enumerate(("cmp_k_w1_2", "cmp_v_w1_2")):
                w1 = a[name][0].rearrange("(j l d) h -> j d l h", j=2, l=CS)
                for c in range(2):
                    if i:
                        sp.wait_ge(mod_done, MOD_UNITS + c + 1)
                    for j in range(2):
                        dst = mraw[j * DH:(j + 1) * DH, c, :].rearrange("p (l h) -> p l h", l=8)
                        sp.dma_start(dst, w1[j, :, c * 8:(c + 1) * 8, :]).then_inc(mod_landed[c], 16)
            with sp.Fori(0, 4) as p:
                for j in range(2):
                    col = p * (2 * P) + j * P
                    pair(p, FIRST["gates2"] + j, w_in2, col + C2_MERGE, w_in2, col + (C2_MERGE + D))
            w_ba2 = a["w_branch_attn_2"][0].rearrange("(g r d) m -> g d r m", g=G2, d=DH)
            w_bp2 = weights(a["w_branch_pool_2"])
            with sp.Fori(0, 4) as p:
                for j in range(2):
                    k = FIRST["merge2"] + j
                    col = p * (2 * P) + j * P
                    slot_free(p, k)
                    for g in range(G2):
                        sp.dma_start(tile(k, 0, 4)[g * DH:(g + 1) * DH], w_ba2[g, :, :, ds(col, P)])\
                          .then_inc(raw_landed[k % 2], 16)
                    sp.dma_start(tile(k, 1, 4), w_bp2[:, :, ds(col, P)]).then_inc(raw_landed[k % 2], 16)
            w_o2 = weights(a["w_out_2"])
            with sp.Fori(0, 2) as p:
                for j in range(2):
                    wide(p, FIRST["wout2"] + j, w_o2, p * (4 * P) + j * 2 * P)
            w_f1, w_f2 = weights(a["w_ff1_2"]), weights(a["w_ff2_2"])
            with sp.Fori(0, SLABS2) as s:
                with sp.Fori(0, 2) as p:
                    for j in range(2):
                        wide(s * 4 + p, FIRST["ff"] + j, w_f1, s * (8 * P) + p * (4 * P) + j * 2 * P)
                with sp.Fori(0, 2) as p:
                    for j in range(2):
                        wide(s * 4 + p, FIRST["ff"] + 4 + j, w_f2, p * (4 * P) + j * 2 * P, s * 8)

            for t in range(TT):
                sp.wait_ge(y_copied, 2 * (t + 1))
                sp.dma_start(out[0, t * P:(t + 1) * P, :], xt[:, t, :]).then_inc(stored, 16)
            sp.wait_ge(stored, 16 * TT)

        @block.gpsimd
        def _(pool):
            for g in range(HKV):
                with pool.Fori(0, 2) as p:
                    for j in range(2):
                        k = FIRST["conv"] + 4 * g + j
                        if g == 0 and j == 0:
                            pool.wait_ge(drained, FIRST["conv"] + 2)
                        pool.wait_ge(unit_done, 2 * p + k)
                        pool.tensor_copy(q_cur[:, j, :], q_rows[:, 2 * p + (4 * g + j), :]).then_inc(qcur_ready, 1)
            with pool.Fori(0, 4) as r:
                k = FIRST["gates2"]
                pool.wait_ge(rope2_done, 7)
                pool.wait_ge(unit_done, 2 * r + (k + 1))
                pool.tensor_copy(q_cur[:, 0, :], q2[:, r, :]).then_inc(qcur_ready, 1)

        @block.scalar
        def _(act):
            act.dma_start(cst[:], a["consts"]).then_inc(boot, 16)
            for i, name in enumerate(("cmp_pe_k_2", "cmp_pe_v_2")):
                for j in range(2):
                    act.dma_start(pe_rows[i * CB:(i + 1) * CB, j * DH:(j + 1) * DH], a[name][0]).then_inc(boot, 16)
            act.dma_start(pe_rows[PE_ROWS:PE_ROWS + KD, :], a["c"][0].rearrange("(k p) -> k p", p=P)).then_inc(boot, 16)
            act.dma_start(pe_rows[PE_ROWS + KD:C_ROWS, :], a["c_ctx"].rearrange("(k p) -> k p", p=P)).then_inc(boot, 16)
            act.dma_start(xt[:, 0:2, :], a["x"][0].rearrange("(t p) d -> p t d", p=P)).then_inc(boot, 16)
            act.dma_start(xt[:, 2:4, :], a["ctx"][0].rearrange("(t p) d -> p t d", p=P)).then_inc(boot, 16)
            for v, name in ((V_N1, "norm1_g"), (V_N2, "norm2_g"), (V_N3, "norm3_g"), (V_F1, "final_g"),
                            (V_MIX, "norm_mix_2"), (V_MLP, "norm_mlp_2"), (V_F2, "norm_final_2")):
                g = a[name] if name in ("final_g", "norm_final_2") else a[name][0]
                act.dma_start(vec_rows[v:v + KD, :], g.rearrange("(k p) -> k p", p=P)).then_inc(boot, 16)
            act.dma_start(vec_rows[V_CONV:V_PS, :], a["conv_w"][0].rearrange("w (k p) -> (w k) p", p=P)).then_inc(boot, 16)
            act.dma_start(vec_rows[V_PS:V_QG, :], a["pool_scale_2"][0].rearrange("(k p) -> k p", p=P)).then_inc(boot, 16)
            act.dma_start(vec_rows[V_QG:V_KG, :], a["q_norm_g"]).then_inc(boot, 16)
            act.dma_start(vec_rows[V_KG:V_END, :], a["k_norm_g"]).then_inc(boot, 16)
            act.dma_start(bm_rows, a["b_mod"][0].rearrange("(k p) -> k p", p=P)).then_inc(boot, 16)
            act.dma_start(wg[:], a["w_in_2"][0].rearrange("(k p) m -> p k m", p=P)[:, :, C2_GATE:C2_POOL]).then_inc(late, 16)
            act.dma_start(w_pool[:], a["pool_w_2"][0].rearrange("g c d -> c g d")).then_inc(late, 16)
            for i, name in enumerate(("cmp_k_w2_2", "cmp_v_w2_2")):
                act.dma_start(w2c[:, i, :, :], a[name][0].rearrange("(h p) d -> p h d", p=P)).then_inc(late, 16)

            def split(pr, k):
                act.wait_ge(raw_landed[k % 2], pr * LANDED + LANDED * (k // 2 + 1))
                if not (isinstance(pr, int) and pr == 0 and k == 0):
                    act.wait_ge(unit_done, 2 * pr + k)
                for half in range(2):
                    cols = slice(half * HALF, (half + 1) * HALF)
                    act.activation(w_hi[:, k % 2, cols], raw[:, k % 2, cols], ACT.Copy).then_inc(h_ready, 1)

            def done(pr, k):
                act.wait_ge(unit_done, 2 * pr + (k + 2))

            def bank(k, t, n=S):
                return ps_u[:, 2 * (k % 2) + t, 0:n]

            act.wait_ge(vec_turned, 1)
            for i in range(2):
                lo = PE_ROWS + i * KD
                act.activation(sc[:, :, i], ps_a[:, 1, lo:lo + KD], ACT.Silu).then_inc(sc_ready, 1)
            for kc in range(KD):
                act.wait_ge(x_copied, kc + 1)
                act.activation(sq[:, kc, :], x[:, kc, :], ACT.Square).then_inc(sq_ready, 1)

            def roots(n, tiles, width=D):
                act.wait_ge(stat_done, n + 1)
                act.activation(root[:, 0:tiles], ps_a[:, 1, 0:tiles], ACT.Sqrt, bias=eps, scale=1.0 / width)\
                   .then_inc(root_done, 1)

            def norm_hi(i, n, shift):
                for kc in range(KD):
                    act.wait_ge(z_ready, 8 * i + kc + 1)
                    for s, cols in segs(n):
                        if shift is None:
                            ins = act.activation(x_hi[:, kc, cols], sq[:, kc, cols], ACT.Copy)
                        else:
                            ins = act.activation(x_hi[:, kc, cols], sq[:, kc, cols], ACT.Identity,
                                                 bias=mods[:, shift * KD + kc, s:s + 1])
                    ins.then_inc(xh_ready, 1)

            def squares(pr, k, m, n):
                act.wait_ge(drained, 2 * pr + (k + 3))
                for t in range(2):
                    act.activation(sq[:, m + t, 0:n], x[:, m + t, 0:n], ACT.Square).then_inc(sq_ready, 1)

            def swiglu(base, count, n):
                def slab(pr, k, c, chunks, last):
                    with act.Fori(0, chunks // 2) as p:
                        for j in range(2):
                            split(pr + p, k + j + 1)
                            done(pr + p, k + j)
                            act.activation(s1[:, j, 0:n], bank(k + j, 0, n), ACT.Silu).then_inc(silu_done, 1)
                            act.wait_ge(prod_done, c + 2 * p + (j + 1))
                            act.activation(h_hi[:, 2 * p + j, 0:n], t1[:, j, 0:n], ACT.Copy).then_inc(hh_done, 1)
                    for i in range(4):
                        split(pr, k + chunks + i + 1)
                        if last:
                            squares(pr, k + chunks + i, 2 * i, n)

                with act.Fori(0, 2) as s:
                    slab(s * 6, base, s * 8 + count, SLABS[0], False)
                slab(0, base + 24, count + 16, SLABS[2], True)

            roots(0, 4)
            split(0, 0)
            norm_hi(0, NB, 0)
            swiglu(FIRST["ffn1"], 0, NB)
            roots(1, 4)
            norm_hi(1, NB, 3)

            k = FIRST["k"]
            split(0, k + 1)
            done(0, k)
            for t in range(HKV):
                act.activation(s1[:, t, :], bank(k, t, NB), ACT.Square).then_inc(k_squared, 1)
            split(0, k + 2)
            act.wait_ge(kstat_done, 1)
            act.activation(root[:, 0:8], ps_a[:, 1, 8:16], ACT.Sqrt, bias=eps, scale=1.0 / HD).then_inc(kroot_done, 1)
            with act.Fori(0, 2) as p:
                for j in range(2):
                    k = FIRST["q"] + j
                    split(p, k + 1)
                    done(p, k)
                    for t in range(2):
                        act.activation(q_sq[:, 4 * p + (2 * j + t), :], bank(k, t), ACT.Square).then_inc(q_squared, 1)
            act.wait_ge(qstat_done, 1)
            act.activation(root[:, 16:32], ps_a[:, 1, 16:32], ACT.Sqrt, bias=eps, scale=1.0 / HD).then_inc(qroot_done, 1)

            act.wait_ge(mods_ready, 2)
            with act.Fori(0, 4) as p:
                for j in range(2):
                    k = FIRST["gates"] + j
                    split(p, k + 1)
                    done(p, k)
                    act.activation(g_conv[:, 2 * p + j, :], bank(k, 0), ACT.Sigmoid)
                    act.activation(g_attn[:, 2 * p + j, :], bank(k, 1), ACT.Sigmoid).then_inc(gates_done, 1)

            for g in range(HKV):
                with act.Fori(0, 2) as p:
                    for j in range(2):
                        k = FIRST["conv"] + 4 * g + j
                        h = 2 * p + (4 * g + j)
                        split(p, k + 1)
                        for qt in range(TT):
                            act.wait_ge(nb_ready, 2 * h + (qt + 1))
                            act.activation(probs[:, qt, :], ps_a[:, qt, :], ACT.Exp, bias=neg_top[:, qt:qt + 1],
                                           scale=q_scale[:, ds(2 * h + qt, 1)],
                                           accum_out=total[:, qt:qt + 1]).then_inc(exp_done, 1)
                        done(p, k)
                        act.activation(s1[:, j, 0:S], bank(k, 0), ACT.Copy).then_inc(cg_copied, 1)
                        act.wait_ge(t_done, 2 * h + 1)
                        act.activation(probs_t[:, :, 0:P], ps_a[:, 2, :].rearrange("p (k q) -> p k q", k=4), ACT.Copy)\
                           .then_inc(pta_ready, 1)
                        act.wait_ge(pv_done, h + 1)
                        act.activation(h_hi[:, h, S:NB], ps_a[:, 2, 0:S], ACT.Copy).then_inc(oh_ready, 1)
            with act.Fori(0, 2) as p:
                for j in range(2):
                    k = FIRST["bg"] + j
                    split(p, k + 1)
                    for t in range(2):
                        act.wait_ge(y_done, 4 * p + (2 * j + t + 1))
                        act.activation(h_hi[:, 4 * p + (2 * j + t), 0:S], t1[:, t, 0:S], ACT.Copy).then_inc(yh_done, 1)
            with act.Fori(0, 4) as p:
                for j in range(2):
                    k = FIRST["merge"] + j
                    split(p, k + 1)
                    act.wait_ge(merge_terms, 6 * p + (3 * j + 3))
                    act.activation(x_hi[:, 2 * p + j, 0:S], t1[:, j, 0:S], ACT.Copy).then_inc(zh_done, 1)
            for i in range(4):
                k = FIRST["wout"] + i
                split(0, k + 1)
                squares(0, k, 2 * i, S)

            roots(2, 2)
            norm_hi(2, S, 6)
            swiglu(FIRST["ffn2"], 22, S)
            roots(3, 2)
            for kc in range(KD):
                act.wait_ge(x_normed, kc + 1)
                act.activation(sq[:, kc, 0:S], x[:, kc, 0:S], ACT.Square).then_inc(sq_ready, 1)
            roots(4, 2)
            norm_hi(3, S, None)

            act.wait_ge(late, 64)
            act.activation(wg_hi[:], wg[:], ACT.Copy).then_inc(wg_done, 1)
            k = FIRST["kcvc"]
            for i in range(7):
                split(0, k + i + 1)
                if i in (3, 4):
                    done(0, k + i)
                    g = i - 3
                    for t in range(2):
                        for b in range(2):
                            ins = act.activation(q2[g * DH:(g + 1) * DH, 2 * t + b, :],
                                                 ps_u[b * DH:(b + 1) * DH, 2 * ((k + i) % 2) + t, 0:S],
                                                 ACT.Copy, scale=float(DH) ** -0.5)
                    ins.then_inc(kv2_copied, 1)
            act.wait_ge(gt_done, 1)
            act.activation(g_tok[:], ps_a[:, 1, 0:TT * 3 * H2].rearrange("p (t c) -> p t c", t=TT), ACT.Sigmoid)\
               .then_inc(gt_ready, 1)
            for i in range(2):
                act.wait_ge(hid_done, i + 1)
                act.activation(hid[:, i, :, :], ps_a[:, 0, i * 64:i * 64 + 2 * G2 * NC].rearrange("p (h c) -> p h c", h=2),
                               ACT.Gelu_apprx_tanh).then_inc(gelu_done, 1)
            for i in range(4):
                act.wait_ge(mixed_done, i + 1)
                act.activation(mixed[:, i, :], ps_a[:, 3, 0:S], ACT.Identity, scale=vcol(V_PS, i)).then_inc(ph_done, 1)
                act.wait_ge(ph_done, 2 * i + 1)
                act.activation(h_hi[:, i, S:NB], mixed[:, i, :], ACT.Copy).then_inc(ph_done, 1)

            with act.Fori(0, 4) as r:
                for g in range(G2):
                    k = FIRST["gates2"] + g
                    h = 2 * r + g
                    split(r, k + 1)
                    for qt in range(TT):
                        act.wait_ge(masked, 4 * h + (2 * qt + 2))
                        for b in range(2):
                            act.activation(probs[:, qt, b * S:(b + 1) * S], probs[:, qt, b * S:(b + 1) * S], ACT.Exp,
                                           bias=neg_top[:, 2 * qt + b:2 * qt + b + 1],
                                           accum_out=total[:, 2 * qt + b:2 * qt + b + 1]).then_inc(exp_done, 1)
                    act.wait_ge(cmp_masked, 2 * h + 2)
                    for qt in range(TT):
                        ins = act.activation(sc_c[:, qt, :], sc_c[:, qt, :], ACT.Exp, bias=neg_top[:, 4 + qt:5 + qt])
                    ins.then_inc(exp_done, 1)
                    done(r, k)
                    act.activation(gates2[:, 2 * r + g, :, :], ps_u[:, 2 * (k % 2):2 * (k % 2) + 2, 0:S], ACT.Copy)\
                       .then_inc(g2_copied, 1)
                    act.wait_ge(t_done, 2 * HQ + 3 * h + 1)
                    act.activation(probs_t[:, :, 0:P], ps_a[:, 2, :].rearrange("p (k q) -> p k q", k=4), ACT.Copy)\
                       .then_inc(pta_ready, 1)
                    act.wait_ge(pv_done, HQ + h + 1)
                    act.activation(h_hi[g * DH:(g + 1) * DH, r, 0:S], ps_a[g * DH:(g + 1) * DH, 1, 0:S], ACT.Copy)\
                       .then_inc(oh_ready, 1)
            with act.Fori(0, 4) as p:
                for j in range(2):
                    k = FIRST["merge2"] + j
                    split(p, k + 1)
                    act.activation(s1[:, j, :].rearrange("p (a n) -> p a n", a=2), gates2[:, 2 * p + j, :, :], ACT.Sigmoid)\
                       .then_inc(g2_done, 1)
                    act.wait_ge(merge_terms, 6 * p + (24 + 3 * j + 3))
                    act.activation(x_hi[:, 2 * p + j, 0:S], t1[:, j, 0:S], ACT.Copy).then_inc(zh_done, 1)
            for i in range(4):
                k = FIRST["wout2"] + i
                split(0, k + 1)
                squares(0, k, 2 * i, S)
            roots(5, 2)
            norm_hi(4, S, None)

            def relu2(pr, k, c, last):
                with act.Fori(0, 2) as p:
                    for j in range(2):
                        split(pr + p, k + j + 1)
                        done(pr + p, k + j)
                        for t in range(2):
                            act.activation(s1[:, t, 0:S], bank(k + j, t), ACT.Relu).then_inc(relu_done, 1)
                        for t in range(2):
                            act.wait_ge(prod_done, c + 4 * p + (2 * j + t + 1))
                            act.activation(h_hi[:, 4 * p + (2 * j + t), 0:S], t1[:, t, 0:S], ACT.Copy).then_inc(hh_done, 1)
                for i in range(4):
                    if not (last and i == 3):
                        split(pr, k + 4 + i + 1)
                    if last:
                        squares(pr, k + 4 + i, 2 * i, S)

            with act.Fori(0, SLABS2 - 1) as s:
                relu2(s * 4, FIRST["ff"], s * 8 + 44, False)
            relu2(0, FIRST["ff"] + 8 * (SLABS2 - 1), 44 + 8 * (SLABS2 - 1), True)
            roots(6, 2)
            for i in range(4):
                act.wait_ge(y_turned, i + 1)
                act.activation(xt[:, i // 2, (i % 2) * 512:(i % 2 + 1) * 512], ps_u[:, i, :], ACT.Copy).then_inc(y_copied, 1)

        @block.vector
        def _(dve):
            dve.memset(ones[:], 1.0).then_inc(ones_ready, 1)
            dve.memset(u_pad[:], 0.0).then_inc(l_ready, 4)
            dve.memset(p_pad[:], 0.0).then_inc(drained, 2)
            dve.memset(pc[:], 0.0).then_inc(ones_ready, 1)
            dve.memset(vc_tok[:], 0.0).then_inc(ones_ready, 1)
            dve.wait_ge(ones_ready, 3)

            def split(pr, k):
                dve.wait_ge(drained, 2 * pr + (k + 1))
                for half in range(2):
                    cols = slice(half * HALF, (half + 1) * HALF)
                    dve.wait_ge(h_ready, 4 * pr + (2 * k + half + 1))
                    dve.tensor_tensor(w_lo[:, k % 2, cols], raw[:, k % 2, cols], w_hi[:, k % 2, cols].bitcast(F32),
                                      ALU.subtract).then_inc(l_ready, 1)

            def done(pr, k):
                dve.wait_ge(unit_done, 2 * pr + (k + 2))

            def bank(k, t, n=S):
                return ps_u[:, 2 * (k % 2) + t, 0:n]

            dve.wait_ge(sc_ready, 2)
            dve.tensor_copy(pec[:], ps_a[:, 1, 0:C_ROWS]).then_inc(vec_ready, 1)
            dve.wait_ge(vec_turned, 3)
            dve.tensor_copy(vec[:], ps_a[:, 2, 0:V_END]).then_inc(vec_ready, 1)
            dve.tensor_copy(bm[:], ps_a[:, 3, 0:MOD_TILES]).then_inc(vec_ready, 1)
            dve.wait_ge(vec_ready, 3)
            dve.tensor_scalar(bm_half[:], bm[:], 0.5, None, ALU.mult).then_inc(vec_ready, 1)
            for kc in range(KD):
                dve.wait_ge(x_turned, kc + 1)
                dve.tensor_copy(x[:, kc, :], ps_u[:, kc % 4, :]).then_inc(x_copied, 1)

            def modulations(lo, hi, norms, count):
                for s in range(2):
                    ins = dve.tensor_tensor(mods[:, lo:hi, s], mod_ps[:, lo:hi, s], bm[:, lo:hi], ALU.add)
                ins.then_inc(gate_ready, 1)
                dve.wait_ge(gate_ready, count)
                for i, chunk, v in norms:
                    for s in range(2):
                        ins = dve.scalar_tensor_tensor(am[:, i, :, s], mods[:, chunk * KD:(chunk + 1) * KD, s], 1.0,
                                                       vec[:, v:v + KD], ALU.add, ALU.mult)
                ins.then_inc(mods_ready, 1)

            def spread(n, tiles):
                dve.wait_ge(root_done, n + 1)
                dve.reciprocal(rstd[:, 0:tiles], root[:, 0:tiles]).then_inc(recip_done, 1)
                dve.wait_ge(recip_done, n + 1)
                for t in range(tiles):
                    ins = dve.tensor_scalar(t1[:, 0, t * P:(t + 1) * P], ident, rstd[:, t:t + 1], None, ALU.mult)
                ins.then_inc(diag_done, 1)

            def norm_lo(n, i, width, scale, shift):
                dve.wait_ge(rb_done, n + 1)

                def z(kc):
                    for s, cols in segs(width):
                        ins = dve.scalar_tensor_tensor(sq[:, kc, cols], x[:, kc, cols], scale(kc, s), ps_a[:, 2, cols],
                                                       ALU.mult, ALU.mult)
                    ins.then_inc(z_ready, 1)

                def lo(kc):
                    dve.wait_ge(xh_ready, 8 * i + kc + 1)
                    for s, cols in segs(width):
                        hi = x_hi[:, kc, cols].bitcast(F32)
                        if shift is None:
                            ins = dve.tensor_tensor(x_lo[:, kc, cols], sq[:, kc, cols], hi, ALU.subtract)
                        else:
                            ins = dve.scalar_tensor_tensor(x_lo[:, kc, cols], sq[:, kc, cols],
                                                           mods[:, shift * KD + kc, s:s + 1], hi, ALU.add, ALU.subtract)
                    ins.then_inc(xl_ready, 1)

                z(0)
                for kc in range(KD):
                    if kc + 1 < KD:
                        z(kc + 1)
                    lo(kc)

            def modulated(i, scale):
                return lambda kc, s: am[:, i, kc, s:s + 1]

            def plain(v):
                return lambda kc, s: vcol(v, kc)

            def add_out(pr, k, m, n, gate):
                done(pr, k)
                for t in range(2):
                    for s, cols in segs(n):
                        if gate is None:
                            ins = dve.tensor_tensor(x[:, m + t, cols], bank(k, t, n)[:, cols], x[:, m + t, cols], ALU.add)
                        else:
                            ins = dve.scalar_tensor_tensor(x[:, m + t, cols], bank(k, t, n)[:, cols], gate(m + t, s),
                                                           x[:, m + t, cols], ALU.mult, ALU.add)
                ins.then_inc(drained, 1)

            def swiglu(base, count, n, i, first):
                def gate(m, s):
                    return gate_half[:, i, m, s:s + 1]

                def slab(sl, pr, k, c, chunks):
                    with dve.Fori(0, chunks // 2) as p:
                        for j in range(2):
                            split(pr + p, k + j + 1)
                            dve.wait_ge(silu_done, c + 2 * p + (j + 1))
                            dve.tensor_tensor(t1[:, j, 0:n], s1[:, j, 0:n], bank(k + j, 1, n), ALU.mult)\
                               .then_inc(prod_done, 1)
                            dve.wait_ge(hh_done, c + 2 * p + (j + 1))
                            dve.tensor_tensor(h_lo[:, 2 * p + j, 0:n], t1[:, j, 0:n],
                                              h_hi[:, 2 * p + j, 0:n].bitcast(F32), ALU.subtract).then_inc(drained, 1)
                    if first:
                        dve.wait_ge(mod_done, MOD_RIDE * sl + (MOD_FRONT + chunks))
                        for s in range(2):
                            ins = dve.scalar_tensor_tensor(gate_half[:, 0, :, s], mod_ps[:, 2 * KD:3 * KD, s], 0.5,
                                                           bm_half[:, 2 * KD:3 * KD], ALU.mult, ALU.add)
                        ins.then_inc(gate_ready, 1)
                        dve.wait_ge(gate_ready, sl + 2)
                    for o in range(4):
                        split(pr, k + chunks + o + 1)
                        add_out(pr, k + chunks + o, 2 * o, n, gate)

                with dve.Fori(0, 2) as s:
                    slab(s, s * 6, base, s * 8 + count, SLABS[0])
                slab(2, 0, base + 24, count + 16, SLABS[2])

            spread(0, 4)
            dve.wait_ge(mod_done, MOD_FRONT)
            dve.wait_ge(vec_ready, 4)
            dve.wait_ge(x_copied, KD)
            modulations(0, 2 * KD, ((0, 1, V_N1),), 1)
            dve.wait_ge(mods_ready, 1)
            split(0, 0)
            norm_lo(0, 0, NB, modulated(0, 1), 0)
            swiglu(FIRST["ffn1"], 0, NB, 0, True)
            dve.wait_ge(mod_done, MOD_UNITS)
            for s in range(2):
                dve.scalar_tensor_tensor(gate_half[:, 1, :, s], mod_ps[:, 8 * KD:9 * KD, s], 0.5,
                                         bm_half[:, 8 * KD:9 * KD], ALU.mult, ALU.add)
            modulations(3 * KD, 8 * KD, ((1, 4, V_N2), (2, 7, V_N3)), 5)
            dve.wait_ge(mods_ready, 2)
            spread(1, 4)
            norm_lo(1, 1, NB, modulated(1, 4), 3)

            k = FIRST["k"]
            split(0, k + 1)
            for t in range(HKV):
                dve.wait_ge(k_squared, t + 1)
                ins = dve.tensor_scalar(k_all[:, t, :], bank(k, t, NB), vcol(V_KG, 0), None, ALU.mult)
                ins.then_inc(drained if t else k_gained, 1)
            split(0, k + 2)
            done(0, k + 1)
            dve.tensor_copy(v_feat[:, 0, :], bank(k + 1, 0, NB))
            dve.tensor_copy(v_feat[:, 1, :], bank(k + 1, 1, NB)).then_inc(drained, 1)
            dve.wait_ge(kroot_done, 1)
            dve.reciprocal(rstd[:, 0:8], root[:, 0:8]).then_inc(krecip_done, 1)
            dve.wait_ge(krecip_done, 1)
            for t in range(8):
                ins = dve.tensor_scalar(t1[:, t // 4, (t % 4) * P:(t % 4 + 1) * P], ident, rstd[:, t:t + 1], None, ALU.mult)
            ins.then_inc(kdiag_done, 1)

            def q_gain(i):
                kq = FIRST["q"] + i
                split(0, kq + 1)
                for t in range(2):
                    dve.wait_ge(q_squared, 2 * i + t + 1)
                    ins = dve.tensor_scalar(q_rows[:, 2 * i + t, :], bank(kq, t), vcol(V_QG, 0), None, ALU.mult)
                ins.then_inc(drained, 1)

            q_gain(0)
            dve.wait_ge(v_turned, 1)
            dve.tensor_copy(v_tok[:, :, 0, :], ps_a[:, 0, :].rearrange("p (c d) -> p c d", c=4)).then_inc(v_ready, 1)
            q_gain(1)
            for t in range(HKV):
                dve.wait_ge(krb_done, t + 1)
                dve.tensor_tensor(k_all[:, t, :], k_all[:, t, :], ps_a[:, 2 + t, :], ALU.mult).then_inc(k_normed, 1)
            q_gain(2)
            dve.wait_ge(k_normed, 2)
            for t in range(HKV):
                dve.wait_ge(k_swapped, t + 1)
                if t:
                    dve.wait_ge(k_ready, t)
                dve.tensor_tensor(t1[:, 0, 0:S], k_all[:, t, 0:S], cos1, ALU.mult)
                dve.tensor_tensor(t1[:, 1, 0:S], ps_a[:, 2 + t, 0:S], sin1, ALU.mult).then_inc(k_terms, 1)
                dve.wait_ge(k_terms, t + 1)
                dve.tensor_tensor(k_all[:, t, 0:S], t1[:, 0, 0:S], t1[:, 1, 0:S], ALU.add).then_inc(k_ready, 1)
            q_gain(3)
            dve.wait_ge(v_turned, 2)
            dve.tensor_copy(v_tok[:, :, 1, :], ps_a[:, 0, :].rearrange("p (c d) -> p c d", c=4)).then_inc(v_ready, 1)
            dve.wait_ge(qroot_done, 1)
            dve.reciprocal(rstd[:, 16:32], root[:, 16:32]).then_inc(qrecip_done, 1)
            dve.wait_ge(qrecip_done, 1)
            dve.tensor_scalar(q_scale[:], rstd[:, 16:32], float(HD) ** -0.5, None, ALU.mult).then_inc(q_scaled, 1)

            dve.wait_ge(drained, FIRST["gates"] + 2)
            with dve.Fori(0, 4) as p:
                for j in range(2):
                    k = FIRST["gates"] + j
                    h = 2 * p + j
                    split(p, k + 1)
                    dve.wait_ge(q_swapped, h + 1)
                    dve.tensor_tensor(t1[:, j, 0:S], q_rows[:, h, :], cos1, ALU.mult)
                    dve.tensor_tensor(t1[:, j, S:NB], ps_a[:, 2 + j, 0:S], sin1, ALU.mult).then_inc(q_terms, 1)
                    dve.wait_ge(q_terms, h + 1)
                    dve.wait_ge(gates_done, h + 1)
                    dve.tensor_tensor(q_rows[:, h, :], t1[:, j, 0:S], t1[:, j, S:NB], ALU.add).then_inc(drained, 1)

            dve.wait_ge(q_scaled, 1)
            for g in range(HKV):
                with dve.Fori(0, 2) as p:
                    for j in range(2):
                        k = FIRST["conv"] + 4 * g + j
                        h = 2 * p + (4 * g + j)
                        dve.wait_ge(qk_done, h + 1)
                        for qt in range(TT):
                            ins = dve.tensor_reduce(top[:, qt:qt + 1], ps_a[:, qt, :], AX_X, ALU.max)
                        ins.then_inc(top_done, 1)
                        dve.wait_ge(top_done, h + 1)
                        for qt in range(TT):
                            dve.tensor_scalar(neg_top[:, qt:qt + 1], top[:, qt:qt + 1], q_scale[:, ds(2 * h + qt, 1)], -1.0,
                                              ALU.mult, ALU.mult).then_inc(nb_ready, 1)
                        split(p, k + 1)
                        dve.wait_ge(exp_done, 2 * h + 2)
                        dve.reciprocal(inv[:, 0:TT], total[:, 0:TT]).then_inc(inv_done, 1)
                        dve.wait_ge(inv_done, h + 1)
                        for qt in range(TT):
                            dve.tensor_scalar(probs[:, qt, :], probs[:, qt, :], inv[:, qt:qt + 1], None, ALU.mult)\
                               .then_inc(p_ready, 1)
                        dve.wait_ge(cg_copied, h + 1)
                        dve.tensor_tensor(u_pad[:, 1:S + 1], s1[:, j, 0:S], bank(k, 1), ALU.mult).then_inc(u_ready, 1)
                        dve.wait_ge(t_done, 2 * h + 2)
                        dve.tensor_copy(probs_t[:, :, P:2 * P], ps_a[:, 3, :].rearrange("p (k q) -> p k q", k=4))\
                           .then_inc(ptd_ready, 1)
                        dve.wait_ge(u_ready, h + 1)
                        dve.tensor_scalar(t1[:, 0, 0:S], u_pad[:, 0:S], vcol(V_CONV, h), None, ALU.mult)\
                           .then_inc(conv_terms, 1)
                        dve.wait_ge(conv_terms, 2 * h + 1)
                        dve.scalar_tensor_tensor(t1[:, 1, 0:S], u_pad[:, 1:S + 1], vcol(V_CONV + KD, h), t1[:, 0, 0:S],
                                                 ALU.mult, ALU.add).then_inc(conv_terms, 1)
                        dve.wait_ge(conv_terms, 2 * h + 2)
                        dve.scalar_tensor_tensor(y_conv[:, h, :], u_pad[:, 2:S + 2], vcol(V_CONV + 2 * KD, h), t1[:, 1, 0:S],
                                                 ALU.mult, ALU.add)
                        dve.wait_ge(oh_ready, h + 1)
                        dve.tensor_tensor(h_lo[:, h, S:NB], ps_a[:, 2, 0:S], h_hi[:, h, S:NB].bitcast(F32), ALU.subtract)\
                           .then_inc(drained, 1)
            dve.wait_ge(drained, FIRST["bg"] + 2)
            with dve.Fori(0, 2) as p:
                for j in range(2):
                    k = FIRST["bg"] + j
                    split(p, k + 1)
                    done(p, k)
                    for t in range(2):
                        m = 4 * p + (2 * j + t)
                        dve.tensor_tensor(t1[:, t, 0:S], y_conv[:, m, :], bank(k, t), ALU.mult).then_inc(y_done, 1)
                    for t in range(2):
                        m = 4 * p + (2 * j + t)
                        dve.wait_ge(yh_done, m + 1)
                        ins = dve.tensor_tensor(h_lo[:, m, 0:S], t1[:, t, 0:S], h_hi[:, m, 0:S].bitcast(F32), ALU.subtract)
                    ins.then_inc(drained, 1)

            def merge(base, count, gates):
                with dve.Fori(0, 4) as p:
                    for j in range(2):
                        k = base + j
                        m = 2 * p + j
                        split(p, k + 1)
                        done(p, k)
                        ga, gb = gates(m, j)
                        dve.tensor_tensor(t1[:, j, 0:S], ga, bank(k, 0), ALU.mult).then_inc(merge_terms, 1)
                        dve.tensor_tensor(t1[:, j, S:NB], gb, bank(k, 1), ALU.mult).then_inc(merge_terms, 1)
                        dve.wait_ge(merge_terms, 6 * p + (count + 3 * j + 2))
                        dve.tensor_tensor(t1[:, j, 0:S], t1[:, j, 0:S], t1[:, j, S:NB], ALU.add).then_inc(merge_terms, 1)
                        dve.wait_ge(zh_done, m + (count // 3 + 1))
                        dve.tensor_tensor(x_lo[:, m, 0:S], t1[:, j, 0:S], x_hi[:, m, 0:S].bitcast(F32), ALU.subtract)\
                           .then_inc(drained, 1)

            merge(FIRST["merge"], 0, lambda m, j: (g_conv[:, m, :], g_attn[:, m, :]))
            for i in range(4):
                split(0, FIRST["wout"] + i + 1)
                add_out(0, FIRST["wout"] + i, 2 * i, S, lambda m, s: mods[:, 5 * KD + m, s:s + 1])

            spread(2, 2)
            norm_lo(2, 2, S, modulated(2, 7), 6)
            swiglu(FIRST["ffn2"], 22, S, 1, False)

            def normed(n, v):
                dve.wait_ge(rb_done, n + 1)
                for kc in range(KD):
                    dve.scalar_tensor_tensor(x[:, kc, 0:S], x[:, kc, 0:S], vcol(v, kc), ps_a[:, 2, 0:S], ALU.mult, ALU.mult)\
                       .then_inc(x_normed, 1)

            spread(3, 2)
            normed(3, V_F1)
            spread(4, 2)
            dve.wait_ge(x_normed, KD)
            norm_lo(4, 3, S, plain(V_MIX), None)

            dve.wait_ge(wg_done, 1)
            dve.tensor_tensor(wg_lo[:], wg[:], wg_hi[:].bitcast(F32), ALU.subtract).then_inc(wg_ready, 1)
            k = FIRST["kcvc"]
            split(0, k + 1)
            done(0, k)
            for t in range(2):
                for g in range(G2):
                    for j in range(2):
                        rows = slice(j * DH, (j + 1) * DH)
                        src = ps_u[g * DH:(g + 1) * DH, 2 * (k % 2) + t, j * CS:j * CS + NC * CS]
                        pos = pec[rows, t * CB + j * CS:t * CB + (j + 1) * CS]
                        ins = dve.tensor_tensor(cmp_in[t][rows, :, g, :], src.rearrange("p (c l) -> p l c", l=CS),
                                                pos.unsqueeze(2).broadcast_to([DH, CS, NC]), ALU.add)
                ins.then_inc(cmp_ready if t == 0 else drained, 1)
            for b in range(2):
                split(0, k + 2 + b)
                done(0, k + 1 + b)
                dve.tensor_copy(kk2[:, b * S:(b + 1) * S], bank(k + 1 + b, 0))
                dve.tensor_copy(v2_feat[:, b, :], bank(k + 1 + b, 1)).then_inc(drained, 1)
            for i in range(2):
                split(0, k + 4 + i)
                dve.wait_ge(kv2_copied, i + 1)
                dve.drain().then_inc(drained, 1)

            def rope2(n, rows, bank_cols, cos, sin, dst=None):
                dve.wait_ge(rope2_swapped, n + 1)
                if n:
                    dve.wait_ge(rope2_done, n)
                width = rows.shape[-1]
                dve.tensor_tensor(t1[:, 0, 0:width], rows, cos, ALU.mult)
                dve.tensor_tensor(t1[:, 1, 0:width], bank_cols, sin, ALU.mult).then_inc(rope2_terms, 1)
                dve.wait_ge(rope2_terms, n + 1)
                dve.tensor_tensor(rows if dst is None else dst, t1[:, 0, 0:width], t1[:, 1, 0:width], ALU.add)\
                   .then_inc(rope2_done, 1)

            def pool_group(i):
                kp = FIRST["pool"] + i // 2
                w = POOLS[i]
                first = 7 * i
                u = bank(kp, i % 2)
                if i % 2 == 0:
                    split(0, kp + 1)
                    done(0, kp)
                if i:
                    dve.wait_ge(pooled_ready, i)
                dve.tensor_copy(p_pad[:, PAD:PAD + S], u).then_inc(pool_steps, 1)
                dve.wait_ge(pool_steps, first + 1)
                width, step, src, off = 1, 0, p_pad, PAD
                bufs = (t1[:, 0, :], t1[:, 1, :])
                while width < w:
                    dst = bufs[step % 2]
                    if step == 0:
                        ins = dve.tensor_tensor(dst[:, 1:PAD + S], p_pad[:, 1:PAD + S], p_pad[:, 0:PAD + S - 1], ALU.add)
                    else:
                        lo = 2 * width - 1
                        prev = bufs[(step - 1) % 2]
                        ins = dve.tensor_tensor(dst[:, lo:PAD + S], prev[:, lo:PAD + S], prev[:, lo - width:PAD + S - width],
                                                ALU.add)
                    step += 1
                    ins.then_inc(pool_steps, 1)
                    dve.wait_ge(pool_steps, first + 1 + step)
                    width *= 2
                sums = bufs[(step - 1) % 2]
                res = bufs[step % 2]
                cnt = cst[:, K_CNT + i * PAD:K_CNT + (i + 1) * PAD]
                dve.tensor_tensor(res[:, 0:PAD], sums[:, PAD:2 * PAD], cnt, ALU.mult)
                dve.tensor_scalar(res[:, PAD:S], sums[:, 2 * PAD:PAD + S], 1.0 / w, None, ALU.mult).then_inc(pool_steps, 6 - step)
                dve.wait_ge(pool_steps, first + 7)
                ins = dve.tensor_tensor(pooled[:, i, :], res[:, 0:S], p_pad[:, PAD:PAD + S], ALU.subtract)
                ins.then_inc(pooled_ready, 1)

            for i in range(4):
                pool_group(i)
                if i % 2 == 1:
                    dve.drain().then_inc(drained, 1)
            for i in range(4):
                dve.wait_ge(ph_done, 2 * i + 2)
                dve.tensor_tensor(h_lo[:, i, S:NB], mixed[:, i, :], h_hi[:, i, S:NB].bitcast(F32), ALU.subtract)\
                   .then_inc(pl_done, 1)
            for b in range(2):
                rope2(b, kk2[:, b * S:(b + 1) * S], ps_a[:, 2 + b, 0:S], cos2, sin2)
            for r in range(4):
                rope2(2 + r, q2[:, r, :], ps_a[:, 2 + r % 2, 0:S], cos2, sin2)
            dve.wait_ge(cmp_done, 2)
            dve.tensor_copy(kc_r[:, 0, :], ps_a[:, 0, 128:128 + NC]).then_inc(kc_raw, 1)
            dve.tensor_copy(vc_tok[0:NC, :, :], ps_a[0:NC, 0, 256:256 + G2 * DH].rearrange("p (g d) -> p g d", g=G2))\
               .then_inc(kc_raw, 1)
            last = CB - 1
            dve.wait_ge(kc_raw, 1)
            rope2(6, kc_r[:, 0, :], ps_a[:, 2, 0:NC], cos2[:, last:S:CS], sin2[:, last:S:CS], kc_r[:, 1, :])
            dve.wait_ge(v2_turned, 1)
            dve.tensor_copy(v2_tok, ps_a[:, 3, :].rearrange("p (b k n) -> p b k n", b=2, k=2)).then_inc(kc_raw, 1)
            dve.wait_ge(gt_ready, 1)

            with dve.Fori(0, 4) as r:
                for g in range(G2):
                    k = FIRST["gates2"] + g
                    h = 2 * r + g
                    dve.wait_ge(qk_done, HQ + h + 1)
                    for qt in range(TT):
                        mask = cst[:, K_MASK + qt * S:K_MASK + (qt + 1) * S].unsqueeze(1).broadcast_to([P, 2, S])
                        rows = probs[:, qt, :].rearrange("p (b n) -> p b n", b=2)
                        dve.tensor_tensor(rows, ps_a[:, qt, :].rearrange("p (b n) -> p b n", b=2), mask, ALU.add)\
                           .then_inc(masked, 1)
                        dve.wait_ge(masked, 4 * h + (2 * qt + 1))
                        dve.tensor_reduce(neg_top[:, 2 * qt:2 * qt + 2], rows, AX_X, ALU.max, negate=True).then_inc(masked, 1)
                    dve.tensor_tensor(sc_c[:], ps_a[:, 2, 0:2 * 16].rearrange("p (t c) -> p t c", t=TT)[:, :, 0:NC], cadd,
                                      ALU.add).then_inc(cmp_masked, 1)
                    dve.wait_ge(cmp_masked, 2 * h + 1)
                    dve.tensor_reduce(neg_top[:, 4:6], sc_c[:], AX_X, ALU.max, negate=True).then_inc(cmp_masked, 1)
                    split(r, k + 1)
                    dve.wait_ge(exp_done, 2 * HQ + 5 * h + 5)
                    dve.tensor_tensor(sc_c[:], sc_c[:], cmul, ALU.mult).then_inc(cmp_steps, 1)
                    dve.wait_ge(cmp_steps, 2 * h + 1)
                    dve.tensor_reduce(total[:, 4:6], sc_c[:], AX_X, ALU.add).then_inc(cmp_steps, 1)
                    dve.wait_ge(cmp_steps, 2 * h + 2)
                    dve.tensor_scalar(total[:, 0:6], total[:, 0:6], 1e-30, None, ALU.max).then_inc(coef_steps, 1)
                    dve.wait_ge(coef_steps, 3 * h + 1)
                    dve.reciprocal(inv[:, 0:6], total[:, 0:6]).then_inc(coef_steps, 1)
                    dve.wait_ge(coef_steps, 3 * h + 2)
                    head = r + 4 * g
                    for qt in range(TT):
                        for b in range(2):
                            dve.tensor_tensor(inv[:, 2 * qt + b:2 * qt + b + 1], inv[:, 2 * qt + b:2 * qt + b + 1],
                                              g_tok[:, qt, ds(head + (b + 1) * H2, 1)], ALU.mult)
                        ins = dve.tensor_tensor(inv[:, 4 + qt:5 + qt], inv[:, 4 + qt:5 + qt], g_tok[:, qt, ds(head, 1)], ALU.mult)
                    ins.then_inc(coef_steps, 1)
                    dve.wait_ge(coef_steps, 3 * h + 3)
                    for qt in range(TT):
                        for b in range(2):
                            cols = slice(b * S, (b + 1) * S)
                            ins = dve.tensor_scalar(probs[:, qt, cols], probs[:, qt, cols], inv[:, 2 * qt + b:2 * qt + b + 1],
                                                    None, ALU.mult)
                        ins.then_inc(p_ready, 1)
                    for qt in range(TT):
                        ins = dve.tensor_scalar(pc[:, qt, 0:NC], sc_c[:, qt, :], inv[:, 4 + qt:5 + qt], None, ALU.mult)
                    ins.then_inc(p_ready, 1)
                    dve.wait_ge(t_done, 2 * HQ + 3 * h + 2)
                    dve.tensor_copy(probs_t[:, :, P:2 * P], ps_a[:, 3, :].rearrange("p (k q) -> p k q", k=4))\
                       .then_inc(ptd_ready, 1)
                    dve.wait_ge(t_done, 2 * HQ + 3 * h + 3)
                    dve.tensor_copy(q_cur[:, 1, :], ps_a[:, 0, 0:S]).then_inc(ptd_ready, 1)
                    dve.wait_ge(g2_copied, h + 1)
                    dve.wait_ge(oh_ready, HQ + h + 1)
                    rows = slice(g * DH, (g + 1) * DH)
                    dve.tensor_tensor(h_lo[rows, r, 0:S], ps_a[rows, 1, 0:S], h_hi[rows, r, 0:S].bitcast(F32), ALU.subtract)\
                       .then_inc(drained, 1)

            def sigmoids(m, j):
                dve.wait_ge(g2_done, m + 1)
                return s1[:, j, 0:S], s1[:, j, S:NB]

            merge(FIRST["merge2"], 24, sigmoids)
            for i in range(4):
                split(0, FIRST["wout2"] + i + 1)
                add_out(0, FIRST["wout2"] + i, 2 * i, S, None)
            spread(5, 2)
            norm_lo(5, 4, S, plain(V_MLP), None)

            def relu2(pr, k, c, last):
                with dve.Fori(0, 2) as p:
                    for j in range(2):
                        split(pr + p, k + j + 1)
                        for t in range(2):
                            dve.wait_ge(relu_done, c - 44 + 4 * p + (2 * j + t + 1))
                            dve.tensor_tensor(t1[:, t, 0:S], s1[:, t, 0:S], s1[:, t, 0:S], ALU.mult).then_inc(prod_done, 1)
                        for t in range(2):
                            m = 4 * p + (2 * j + t)
                            dve.wait_ge(hh_done, c + m + 1)
                            ins = dve.tensor_tensor(h_lo[:, m, 0:S], t1[:, t, 0:S], h_hi[:, m, 0:S].bitcast(F32), ALU.subtract)
                        ins.then_inc(drained, 1)
                for i in range(4):
                    if not (last and i == 3):
                        split(pr, k + 4 + i + 1)
                    add_out(pr, k + 4 + i, 2 * i, S, None)

            with dve.Fori(0, SLABS2 - 1) as s:
                relu2(s * 4, FIRST["ff"], s * 8 + 44, False)
            relu2(0, FIRST["ff"] + 8 * (SLABS2 - 1), 44 + 8 * (SLABS2 - 1), True)
            spread(6, 2)
            dve.wait_ge(rb_done, 7)
            for kc in range(KD):
                dve.scalar_tensor_tensor(x[:, kc, 0:S], x[:, kc, 0:S], vcol(V_F2, kc), ps_a[:, 2, 0:S], ALU.mult, ALU.mult)\
                   .then_inc(x_normed, 1)

        @block.tensor
        def _(pe):
            def turn(dst, src, n=P):
                return pe.transpose(dst, src, ident[0:n, 0:n])

            pe.wait_ge(boot, BOOT)
            turn(ps_a[:, 1, 0:C_ROWS], pe_rows, C_ROWS).then_inc(vec_turned, 1)
            turn(ps_a[:, 2, 0:V_END], vec_rows, V_END).then_inc(vec_turned, 1)
            turn(ps_a[:, 3, 0:MOD_TILES], bm_rows, MOD_TILES).then_inc(vec_turned, 1)
            for kc in range(KD):
                if kc >= 4:
                    pe.wait_ge(x_copied, kc - 3)
                for t in range(4):
                    ins = turn(ps_u[:, kc % 4, t * P:(t + 1) * P], xt[:, t, kc * P:(kc + 1) * P])
                    if kc == 0 and t == 0:
                        ins.then_inc(unit_done, 1)
                ins.then_inc(x_turned, 1)

            def stat(n, tiles):
                pe.wait_ge(sq_ready, 8 * (n + 1))
                for t in range(tiles):
                    for kc in range(KD):
                        ins = pe.matmul(ps_a[:, 1, t:t + 1], sq[:, kc, t * P:(t + 1) * P], ones[:, 0:1],
                                        start=(kc == 0), stop=(kc == KD - 1))
                ins.then_inc(stat_done, 1)

            def spread(n, tiles):
                pe.wait_ge(diag_done, n + 1)
                pe.matmul(ps_a[:, 2, 0:tiles * P], ones[:], t1[:, 0, 0:tiles * P], start=True, stop=True).then_inc(rb_done, 1)

            def mod(pr, km):
                pe.wait_ge(mod_landed[km % 2], 16 * pr + 16 * (km // 2 + 1))
                for t in range(2):
                    dst = ps_a[:, 0, ds(8 * pr + (4 * km + 2 * t), 2)]
                    for kc in range(KD):
                        lo = kc * 2 * P + t * P
                        ins = pe.matmul(dst, mraw[:, km % 2, lo:lo + P], sc[:, kc, :], start=(kc == 0), stop=(kc == KD - 1))
                ins.then_inc(mod_done, 1)

            def unit(pr, k, operand, n=S, kcs=KD, ready=None):
                pe.wait_ge(drained, 2 * pr + (k + 1))
                for kc in range(kcs):
                    if kc in (0, 4):
                        pe.wait_ge(l_ready, 4 * pr + (2 * k + 5 + kc // 4))
                    if ready is not None:
                        ready(kc)
                    for t in range(2):
                        dst = ps_u[:, 2 * (k % 2) + t, 0:n]
                        lo = kc * 2 * P + t * P
                        wh, wl = w_hi[:, k % 2, lo:lo + P], w_lo[:, k % 2, lo:lo + P]
                        xh, xl = operand(kc, t)
                        pe.matmul(dst, wh, xh, start=(kc == 0), stop=False)
                        pe.matmul(dst, wh, xl, start=False, stop=False)
                        ins = pe.matmul(dst, wl, xh, start=False, stop=(kc == kcs - 1))
                ins.then_inc(unit_done, 1)

            def from_x(n):
                return lambda kc, t: (x_hi[:, kc, 0:n], x_lo[:, kc, 0:n])

            def from_h(n):
                return lambda kc, t: (h_hi[:, kc, 0:n], h_lo[:, kc, 0:n])

            def both_h(kc, t):
                cols = slice(t * S, (t + 1) * S)
                return h_hi[:, kc, cols], h_lo[:, kc, cols]

            def normed(i):
                return lambda kc: pe.wait_ge(xl_ready, 8 * i + kc + 1)

            def drained_at(pr, k, per=1):
                return lambda kc: pe.wait_ge(drained, 2 * pr + (k + kc // per + 3))

            def swiglu(base, i, n, ride):
                def slab(s, pr, k, chunks):
                    with pe.Fori(0, chunks // 2) as p:
                        for j in range(2):
                            unit(pr + p, k + j, from_x(n), n, ready=normed(i))
                            if ride:
                                mod(s * (MOD_RIDE // 2) + p, MOD_FRONT + j)
                    for o in range(4):
                        unit(pr, k + chunks + o, from_h(n), n, chunks, ready=drained_at(pr, k) if o == 0 else None)
                        if ride and o % 2 == 0:
                            if o == 0:
                                pe.wait_ge(gate_ready, s + 2)
                            mod(s * (MOD_RIDE // 2), MOD_FRONT + chunks + o // 2)

                with pe.Fori(0, 2) as s:
                    slab(s, s * 6, base, SLABS[0])
                slab(2, 0, base + 24, SLABS[2])

            pe.wait_ge(ones_ready, 1)
            pe.wait_ge(vec_ready, 3)
            stat(0, 4)
            pe.wait_ge(sc_ready, 2)
            with pe.Fori(0, MOD_FRONT // 2) as p:
                for j in range(2):
                    mod(p, j)
            spread(0, 4)
            swiglu(FIRST["ffn1"], 0, NB, True)
            stat(1, 4)
            spread(1, 4)

            k = FIRST["k"]
            unit(0, k, from_x(NB), NB, ready=normed(1))
            unit(0, k + 1, from_x(NB), NB)
            pe.wait_ge(k_squared, 2)
            for t in range(HKV):
                for c in range(4):
                    at = 8 + 4 * t + c
                    ins = pe.matmul(ps_a[:, 1, at:at + 1], s1[:, t, c * P:(c + 1) * P], ones[:, 0:1], start=True, stop=True)
            ins.then_inc(kstat_done, 1)

            def turn_v(t):
                for c in range(4):
                    ins = turn(ps_a[:, 0, c * P:(c + 1) * P], v_feat[:, t, c * P:(c + 1) * P])
                ins.then_inc(v_turned, 1)

            kq = FIRST["q"]
            unit(0, kq, from_x(S))
            pe.wait_ge(drained, k + 4)
            turn_v(0)
            unit(0, kq + 1, from_x(S))
            pe.wait_ge(kdiag_done, 1)
            for t in range(HKV):
                pe.matmul(ps_a[:, 2 + t, :], ones[:], t1[:, t, :], start=True, stop=True).then_inc(krb_done, 1)
            unit(0, kq + 2, from_x(S))
            for t in range(HKV):
                pe.wait_ge(k_normed, t + 1)
                pe.matmul(ps_a[:, 2 + t, 0:S], swap1, k_all[:, t, 0:S], start=True, stop=True).then_inc(k_swapped, 1)
            pe.wait_ge(v_ready, 1)
            turn_v(1)
            unit(0, kq + 3, from_x(S))
            pe.wait_ge(q_squared, HQ)
            for h in range(HQ):
                for t in range(TT):
                    at = 16 + TT * h + t
                    ins = pe.matmul(ps_a[:, 1, at:at + 1], q_sq[:, h, t * P:(t + 1) * P], ones[:, 0:1], start=True, stop=True)
            ins.then_inc(qstat_done, 1)

            pe.wait_ge(k_ready, 2)
            with pe.Fori(0, 4) as p:
                for j in range(2):
                    kg = FIRST["gates"] + j
                    unit(p, kg, from_x(S))
                    if j == 0:
                        pe.wait_ge(drained, FIRST["gates"] + 2)
                    pe.matmul(ps_a[:, 2 + j, 0:S], swap1, q_rows[:, 2 * p + j, :], start=True, stop=True)\
                      .then_inc(q_swapped, 1)

            pe.wait_ge(q_scaled, 1)
            pe.wait_ge(v_ready, 2)
            for g in range(HKV):
                with pe.Fori(0, 2) as p:
                    for j in range(2):
                        kv = FIRST["conv"] + 4 * g + j
                        h = 2 * p + (4 * g + j)
                        pe.wait_ge(qcur_ready, h + 1)
                        for qt in range(TT):
                            ins = pe.matmul(ps_a[:, qt, :], q_cur[:, j, qt * P:(qt + 1) * P], k_all[:, g, :],
                                            start=True, stop=True)
                        ins.then_inc(qk_done, 1)
                        unit(p, kv, from_x(S))
                        pe.wait_ge(drained, 2 * p + (kv + 2))
                        for qt in range(TT):
                            pe.wait_ge(p_ready, 2 * h + (qt + 1))
                            for c in range(4):
                                ins = turn(ps_a[:, 2 + qt, c * P:(c + 1) * P], probs[:, qt, c * P:(c + 1) * P])
                            ins.then_inc(t_done, 1)
                        pe.wait_ge(pta_ready, h + 1)
                        pe.wait_ge(ptd_ready, h + 1)
                        for c in range(4):
                            ins = pe.matmul(ps_a[:, 2, 0:S], v_tok[:, c, g, :], probs_t[:, c, :], start=(c == 0), stop=(c == 3))
                        ins.then_inc(pv_done, 1)
            with pe.Fori(0, 2) as p:
                for j in range(2):
                    unit(p, FIRST["bg"] + j, from_x(S))
            with pe.Fori(0, 4) as p:
                for j in range(2):
                    unit(p, FIRST["merge"] + j, both_h, ready=drained_at(0, FIRST["bg"], 2))
            with pe.Fori(0, 2) as p:
                for j in range(2):
                    unit(p, FIRST["wout"] + j, from_x(S), ready=drained_at(0, FIRST["merge"]))

            stat(2, 2)
            spread(2, 2)
            swiglu(FIRST["ffn2"], 2, S, False)
            stat(3, 2)
            spread(3, 2)
            stat(4, 2)
            spread(4, 2)

            k = FIRST["kcvc"]
            for i in range(7):
                unit(0, k + i, from_x(S), ready=normed(3) if i == 0 else None)
            pe.wait_ge(wg_ready, 1)
            for t in range(TT):
                dst = ps_a[:, 1, t * 3 * H2:(t + 1) * 3 * H2]
                tok = slice(t * P, (t + 1) * P)
                for kc in range(KD):
                    pe.matmul(dst, x_hi[:, kc, tok], wg_hi[:, kc, :], start=(kc == 0), stop=False)
                    pe.matmul(dst, x_hi[:, kc, tok], wg_lo[:, kc, :], start=False, stop=False)
                    ins = pe.matmul(dst, x_lo[:, kc, tok], wg_hi[:, kc, :], start=False, stop=(kc == KD - 1))
            ins.then_inc(gt_done, 1)
            for i in range(2):
                pe.wait_ge(cmp_ready, 1)
                pe.wait_ge(drained, k + 3)
                if i:
                    pe.wait_ge(gelu_done, 1)
                for c in range(2):
                    pe.wait_ge(mod_landed[c], 16 * (MOD_UNITS // 2) + 32 * (i + 1))
                for half in range(2):
                    dst = ps_a[:, 0, i * 64 + half * G2 * NC:i * 64 + (half + 1) * G2 * NC]
                    for l in range(CS):
                        lo = (l % 8) * CH + half * P
                        ins = pe.matmul(dst, mraw[:, l // 8, lo:lo + P], cmp_in[i][:, l, :, :].rearrange("p g c -> p (g c)"),
                                        start=(l == 0), stop=(l == CS - 1))
                        if half == 1 and l == 7:
                            ins.then_inc(mod_done, 1)
                ins.then_inc(mod_done, 1)
                pe.matmul(ps_a[:, 0, 480:481], ones[:], ones[:, 0:1], start=True, stop=True).then_inc(hid_done, 1)
            pe.wait_ge(late, 64)
            for i in range(4):
                pe.wait_ge(pooled_ready, i + 1)
                if i:
                    pe.wait_ge(ph_done, 2 * i - 1)
                pe.matmul(ps_a[:, 3, 0:S], w_pool[:, i, :], pooled[:, i, :], start=True, stop=True)\
                  .then_inc(mixed_done, 1)
            pe.wait_ge(drained, k + 7)
            pe.wait_ge(ph_done, 7)
            for b in range(2):
                pe.matmul(ps_a[:, 2 + b, 0:S], swap2, kk2[:, b * S:(b + 1) * S], start=True, stop=True)\
                  .then_inc(rope2_swapped, 1)
            pe.wait_ge(kv2_copied, 2)
            for r in range(4):
                pe.wait_ge(rope2_done, r + 1)
                pe.matmul(ps_a[:, 2 + r % 2, 0:S], swap2, q2[:, r, :], start=True, stop=True)\
                  .then_inc(rope2_swapped, 1)
            pe.wait_ge(gelu_done, 2)
            for g in range(G2):
                for half in range(2):
                    ins = pe.matmul(ps_a[g * DH:(g + 1) * DH, 0, 128:128 + NC], w2c[:, 0, half, :],
                                    hid[:, 0, half, g * NC:(g + 1) * NC], start=(half == 0), stop=(half == 1))
            ins.then_inc(cmp_done, 1)
            for g in range(G2):
                for half in range(2):
                    ins = pe.matmul(ps_a[0:NC, 0, 256 + g * DH:256 + (g + 1) * DH], hid[:, 1, half, g * NC:(g + 1) * NC],
                                    w2c[:, 1, half, :], start=(half == 0), stop=(half == 1))
            ins.then_inc(cmp_done, 1)
            pe.wait_ge(kc_raw, 1)
            pe.wait_ge(rope2_done, 6)
            pe.matmul(ps_a[:, 2, 0:NC], swap2, kc_r[:, 0, :], start=True, stop=True).then_inc(rope2_swapped, 1)
            for b in range(2):
                for c in range(2):
                    ins = turn(ps_a[:, 3, (2 * b + c) * P:(2 * b + c + 1) * P], v2_feat[:, b, c * P:(c + 1) * P])
            ins.then_inc(v2_turned, 1)
            pe.wait_ge(kc_raw, 3)
            pe.wait_ge(rope2_done, 7)

            pe.wait_ge(gt_ready, 1)
            with pe.Fori(0, 4) as r:
                pe.wait_ge(qcur_ready, HQ + r + 1)
                for g in range(G2):
                    kg = FIRST["gates2"] + g
                    h = 2 * r + g
                    rows = slice(g * DH, (g + 1) * DH)
                    for qt in range(TT):
                        q = q_cur[rows, 0, qt * P:(qt + 1) * P]
                        pe.matmul(ps_a[:, qt, :], q, kk2[rows, :], start=True, stop=True)
                        ins = pe.matmul(ps_a[:, 2, qt * 16:qt * 16 + NC], q, kc_r[rows, 1, :], start=True, stop=True)
                    ins.then_inc(qk_done, 1)
                    unit(r, kg, from_x(S))
                    for qt in range(TT):
                        pe.wait_ge(p_ready, 2 * HQ + 3 * h + (qt + 1))
                        for c in range(4):
                            ins = turn(ps_a[:, 2 + qt, c * P:(c + 1) * P], probs[:, qt, c * P:(c + 1) * P])
                        ins.then_inc(t_done, 1)
                    pe.wait_ge(p_ready, 2 * HQ + 3 * h + 3)
                    for qt in range(TT):
                        ins = turn(ps_a[:, 0, qt * P:(qt + 1) * P], pc[:, qt, :])
                    ins.then_inc(t_done, 1)
                    pe.wait_ge(pta_ready, HQ + h + 1)
                    pe.wait_ge(ptd_ready, HQ + 2 * h + 2)
                    dst = ps_a[rows, 1, 0:S]
                    for c in range(4):
                        pe.matmul(dst, v2_tok[:, c // 2, c % 2, rows], probs_t[:, c, :], start=(c == 0), stop=False)
                    pe.matmul(dst, vc_tok[:, g, :], q_cur[:, 1, :], start=False, stop=True).then_inc(pv_done, 1)
                    pe.wait_ge(drained, 2 * r + (kg + 3))
            pe.wait_ge(pl_done, 4)

            def rows_done(kc):
                pe.wait_ge(drained, FIRST["gates2"] + 2 * kc + 4)

            with pe.Fori(0, 4) as p:
                for j in range(2):
                    unit(p, FIRST["merge2"] + j, both_h, kcs=4, ready=rows_done)
            with pe.Fori(0, 2) as p:
                for j in range(2):
                    unit(p, FIRST["wout2"] + j, from_x(S), ready=drained_at(0, FIRST["merge2"]))
            stat(5, 2)
            spread(5, 2)
            with pe.Fori(0, SLABS2) as s:
                with pe.Fori(0, 2) as p:
                    for j in range(2):
                        unit(s * 4 + p, FIRST["ff"] + j, from_x(S), ready=normed(4))
                with pe.Fori(0, 2) as p:
                    for j in range(2):
                        unit(s * 4 + p, FIRST["ff"] + 4 + j, from_h(S), ready=drained_at(s * 4, FIRST["ff"], 2))
            stat(6, 2)
            spread(6, 2)
            pe.wait_ge(drained, UNITS + 2)
            for t in range(TT):
                for kc in range(KD):
                    pe.wait_ge(x_normed, KD + kc + 1)
                    at = 2 * t + kc // 4
                    ins = turn(ps_u[:, at, (kc % 4) * P:(kc % 4 + 1) * P], x[:, kc, t * P:(t + 1) * P])
                    if kc % 4 == 3:
                        ins.then_inc(y_turned, 1)


def constants():
    import numpy as np
    f = np.float32
    t = np.zeros((P, K_END), f)
    t[:, K_ID:K_ID + P] = np.eye(P, dtype=f)
    n = HD // 4
    for ax in range(2):
        for i in range(n):
            lo, hi = ax * 2 * n + i, ax * 2 * n + n + i
            t[hi, K_R1 + lo] = -1.0
            t[lo, K_R1 + hi] = 1.0
    inv = (f(10000.0) ** (-np.arange(n, dtype=f) / f(n))).astype(f)
    tok = np.arange(S)
    for ax, pos in enumerate((tok // 64, tok % 64)):
        ang = (pos.astype(f)[:, None] * inv).astype(f).T
        for half in range(2):
            rows = slice(ax * 2 * n + half * n, ax * 2 * n + (half + 1) * n)
            t[rows, K_C1:K_C1 + S] = np.cos(ang)
            t[rows, K_S1:K_S1 + S] = np.sin(ang)
    rot = DH // 4
    inv = (f(500000.0) ** (-np.arange(0, rot, 2, dtype=f) / f(rot))).astype(f)
    ang = (tok.astype(f)[:, None] * inv).astype(f).T
    t[:, K_C2:K_C2 + S] = 1.0
    for g in range(G2):
        for i in range(rot // 2):
            lo, hi = g * DH + i, g * DH + rot // 2 + i
            t[hi, K_R2 + lo] = -1.0
            t[lo, K_R2 + hi] = 1.0
            for row in (lo, hi):
                t[row, K_C2:K_C2 + S] = np.cos(ang[i])
                t[row, K_S2:K_S2 + S] = np.sin(ang[i])
    last = np.arange(NC) * CS + CB - 1
    for qt in range(TT):
        q = qt * P + np.arange(P)
        t[:, K_MASK + qt * S:K_MASK + (qt + 1) * S] = np.where(tok[None, :] <= q[:, None], 0.0, -1e30)
        seen = last[None, :] <= q[:, None]
        t[:, K_CADD + qt * NC:K_CADD + (qt + 1) * NC] = np.where(seen, 0.0, -1e30)
        t[:, K_CMUL + qt * NC:K_CMUL + (qt + 1) * NC] = seen
    for i, w in enumerate(POOLS):
        t[:, K_CNT + i * PAD:K_CNT + (i + 1) * PAD] = f(1.0) / np.minimum(np.arange(PAD) + 1, w).astype(f)
    t[:, K_EPS] = EPS
    return t


_INS = ["x", "c", "ctx", "c_ctx", "w_mod", "b_mod", "norm1_g", "norm2_g", "norm3_g", "ffn1_w_in", "ffn1_w_out", "w_in",
        "conv_w", "q_norm_g", "k_norm_g", "w_branch_conv", "w_branch_attn", "w_out", "ffn2_w_in", "ffn2_w_out",
        "final_g", "norm_mix_2", "w_in_2", "cmp_pe_k_2", "cmp_pe_v_2", "cmp_k_w1_2", "cmp_k_w2_2", "cmp_v_w1_2",
        "cmp_v_w2_2", "w_branch_attn_2", "pool_w_2", "pool_scale_2", "w_branch_pool_2", "w_out_2", "norm_mlp_2",
        "w_ff1_2", "w_ff2_2", "norm_final_2"]


def kernel(**inputs):
    import numpy as np
    import concourse.bacc as bacc
    from concourse.bass_utils import run_bass_kernel_spmd as run

    nc = bacc.Bacc("TRN2", target_bir_lowering=False, num_devices=1)
    arrays, args = {}, {}
    for name in _INS:
        arrays[f"in_{name}"] = np.ascontiguousarray(inputs[name])
    arrays["in_consts"] = constants()
    for name, arr in arrays.items():
        args[name[3:]] = nc.dram_tensor(name, arr.shape, mybir.dt.from_np(arr.dtype), kind="ExternalInput").ap()
    out = nc.dram_tensor("out", (1, S, D), F32, kind="ExternalOutput").ap()
    program(nc, args, out)
    r = run(nc, [arrays], core_ids=[0])
    return r.results[0]["out"]
```

```python
from contextlib import ExitStack

import concourse.bass as bass
from concourse import mybir

F32 = mybir.dt.float32
F32R = mybir.dt.float32r
ACT = mybir.ActivationFunctionType
ALU = mybir.AluOpType
AX_X = mybir.AxisListType.X
ds = bass.ds

P = 128
D = 1024
KD = D // P
S = 256
CTX = 256
NB = S + CTX
TT = S // P
EPS = 1e-6

D_FF = 2816
SLABS = (8, 8, 6)
HQ, HKV, HD = 8, 2, 128
GROUP = HQ // HKV
C_BG, C_CG, C_VC = 0, D, 2 * D
C_Q = 3 * D
C_K = C_Q + HQ * HD
C_V = C_K + HKV * HD
C_GATE = C_V + HKV * HD
N_MOD = 9
MOD_TILES = N_MOD * KD
MOD_UNITS = MOD_TILES // 2
MOD_FRONT = 8
MOD_RIDE = 10
MOD_ROWS = 32

H2, G2, R2H, DH = 8, 2, 4, 64
C2_KC = H2 * DH
C2_KS = C2_KC + 2 * G2 * DH
C2_KW = C2_KS + 2 * G2 * DH
C2_GATE = C2_KC + 6 * G2 * DH
C2_POOL = C2_GATE + 3 * H2
C2_MERGE = C2_POOL + 512
CB, CS = 32, 16
NC = (S - CB) // CS + 1
CH = 4 * DH
POOLS = (2, 4, 8, 16)
PAD = max(POOLS)
D_FF2 = 4 * D
SLABS2 = D_FF2 // (8 * P)

K_ID, K_R1, K_R2 = 0, P, 2 * P
K_C1, K_S1, K_C2, K_S2 = (3 * P + i * S for i in range(4))
K_MASK = 3 * P + 4 * S
K_CADD = K_MASK + TT * S
K_CMUL = K_CADD + TT * NC
K_CNT = K_CMUL + TT * NC
K_EPS = K_CNT + len(POOLS) * PAD
K_END = K_EPS + 1

V_C, V_N1, V_N2, V_N3, V_F1, V_MIX, V_MLP, V_F2 = 0, *(KD * i for i in range(2, 9))
V_CONV = 9 * KD
V_PS = V_CONV + 3 * KD
V_QG = V_PS + 4
V_KG = V_QG + 1
V_BM = V_KG + 1
V_PE = V_BM + MOD_TILES
V_END = V_PE + 2 * CB

L_WG = 0
L_POOL = KD * 3 * H2
L_W2 = L_POOL + len(POOLS) * P
L_END = L_W2 + 2 * 2 * DH

STAGES = (("front", MOD_FRONT), ("ffn1", 62), ("k", 1), ("v", 1), ("q", 4), ("gates", 8), ("conv", 8), ("bg", 4), ("merge", 8),
          ("wout", 4), ("ffn2", 34), ("kcvc", 1), ("ksvs", 1), ("kwvw", 1), ("q2", 2), ("pool", 2),
          ("gates2", 8), ("merge2", 8), ("wout2", 4), ("ff", 32))
FIRST = {}
_n = 0
for _name, _units in STAGES:
    FIRST[_name] = _n
    _n += _units
UNITS = _n
SLOT = KD * 2 * P
HALF = SLOT // 2
LANDED = 16


def program(nc, a, out):
    with ExitStack() as ctx:
        def sb(name, shape, dt=F32):
            return ctx.enter_context(nc.sbuf_tensor(name, shape, dt))

        def sem(name):
            return ctx.enter_context(nc.semaphore(name))

        raw = sb("raw", [P, 2, SLOT])
        w_hi = sb("w_hi", [P, 2, SLOT], F32R)
        w_lo = sb("w_lo", [P, 2, SLOT], F32R)
        wide_scr = sb("wide_scr", [P, 2, SLOT])
        x = sb("x", [P, KD, NB])
        x_hi = sb("x_hi", [P, KD, NB], F32R)
        x_lo = sb("x_lo", [P, KD, NB], F32R)
        h_hi = sb("h_hi", [P, KD, NB], F32R)
        h_lo = sb("h_lo", [P, KD, NB], F32R)
        sq = sb("sq", [P, KD, NB])
        s1 = sb("s1", [P, 2, NB])
        t1 = sb("t1", [P, 2, NB])
        scr = sb("scr", [P, 4 * D])
        cst = sb("cst", [P, K_END])
        ones = sb("ones", [P, P])
        vec = sb("vec", [P, V_END])
        late_w = sb("late_w", [P, L_END])
        gg = sb("gg", [P, KD])
        sc = sb("sc", [P, KD, 2])
        sc_pad = sb("sc_pad", [P, KD, MOD_ROWS], F32R)
        mods = sb("mods", [P, MOD_TILES, 2])
        am = sb("am", [P, 3, KD, 2])
        gate_half = sb("gate_half", [P, 2, KD, 2])
        var = sb("var", [P, 2 * TT])
        root = sb("root", [P, 32])
        rstd = sb("rstd", [P, 32])
        q_scale = sb("q_scale", [P, HQ * TT])
        q_cur = sb("q_cur", [P, 2, S])
        u_pad = sb("u_pad", [P, S + 2])
        top = sb("top", [P, 4])
        neg_top = sb("neg_top", [P, 8])
        total = sb("total", [P, 8])
        inv = sb("inv", [P, 8])
        p_pad = sb("p_pad", [P, PAD + S])
        wg_hi = sb("wg_hi", [P, KD, 3 * H2], F32R)
        wg_lo = sb("wg_lo", [P, KD, 3 * H2], F32R)
        g_tok = sb("g_tok", [P, TT, 3 * H2])
        hid = sb("hid", [P, 2, 2, G2 * NC])
        kc_r = sb("kc_r", [P, 2, NC])
        vc_tok = sb("vc_tok", [P, G2, DH])
        pc = sb("pc", [P, TT, P])
        sc_c = sb("sc_c", [P, TT, NC])

        ps_u = ctx.enter_context(nc.psum_tensor("ps_u", [P, 4, 512], F32))
        ps_a = ctx.enter_context(nc.psum_tensor("ps_a", [P, 4, 512], F32))

        sq_flat = sq[:].rearrange("p k n -> p (k n)")
        bm = vec[:, V_BM:V_BM + MOD_TILES]
        pec = vec[:, V_PE:V_END]
        wg = late_w[:, L_WG:L_POOL].rearrange("p (k m) -> p k m", k=KD)
        w_pool = late_w[:, L_POOL:L_W2].rearrange("p (i n) -> p i n", i=4)
        w2c = late_w[:, L_W2:L_END].rearrange("p (i h d) -> p i h d", i=2, h=2)
        turned = scr[:, 0:4 * MOD_ROWS].rearrange("p (b t c) -> p b t c", b=2, t=2)
        mod_sum = scr[:, P:P + 2 * MOD_TILES].rearrange("p (t s) -> p t s", s=2)
        bm_half = scr[:, 3 * P:3 * P + MOD_TILES]
        probs = scr[:, 0:2 * NB].rearrange("p (t n) -> p t n", t=2)
        probs_t = scr[:, 2 * NB:4 * NB].rearrange("p (k n) -> p k n", k=4)
        q_sq = scr[:, 4 * NB:8 * NB].rearrange("p (h n) -> p h n", h=HQ)
        q_rows = x[:, :, S:NB]
        k_all = sq[:, 0:2, :]
        v_feat = sq[:, 2:4, :]
        v_tok = sq_flat[:, 4 * NB:6 * NB].rearrange("p (k g d) -> p k g d", k=4, g=HKV)
        y_conv = scr[:, 4 * NB:8 * NB].rearrange("p (m n) -> p m n", m=KD)
        g_conv = wide_scr[:, 0, :].rearrange("p (m n) -> p m n", m=KD)
        g_attn = wide_scr[:, 1, :].rearrange("p (m n) -> p m n", m=KD)
        mixed = scr[:, 0:2 * NB].rearrange("p (i n) -> p i n", i=4)
        pooled = scr[:, 2 * NB:4 * NB].rearrange("p (i n) -> p i n", i=4)
        kk2 = scr[:, 4 * NB:5 * NB]
        v2_feat = scr[:, 5 * NB:6 * NB].rearrange("p (b n) -> p b n", b=2)
        v2_tok = scr[:, 6 * NB:7 * NB].rearrange("p (b k n) -> p b k n", b=2, k=2)
        cmp_k = scr[:, 7 * NB:7 * NB + CS * G2 * NC].rearrange("p (l g c) -> p l g c", l=CS, g=G2)
        cmp_v = s1[:, 0, 0:CS * G2 * NC].rearrange("p (l g c) -> p l g c", l=CS, g=G2)
        cmp_in = (cmp_k, cmp_v)
        q2 = x[:, 0:4, S:NB]
        gates2 = sq[:].rearrange("p m (a n) -> p m a n", a=2)
        ident = cst[:, K_ID:K_ID + P]
        swap1 = cst[:, K_R1:K_R1 + P]
        swap2 = cst[:, K_R2:K_R2 + P]
        cos1, sin1, cos2, sin2 = (cst[:, k:k + S] for k in (K_C1, K_S1, K_C2, K_S2))
        cadd = cst[:, K_CADD:K_CADD + TT * NC].rearrange("p (t c) -> p t c", t=TT)
        cmul = cst[:, K_CMUL:K_CMUL + TT * NC].rearrange("p (t c) -> p t c", t=TT)
        eps = cst[:, K_EPS:K_EPS + 1]

        def vcol(v, m):
            return vec[:, v + m:v + m + 1] if isinstance(m, int) else vec[:, ds(m + v, 1)]

        def segs(n):
            return [(0, slice(0, S))] if n == S else [(0, slice(0, S)), (1, slice(S, NB))]

        vec_landed = sem("vectors_landed")
        x_landed = [sem("tokens_landed0"), sem("tokens_landed1")]
        cst_landed = sem("constants_landed")
        late = sem("late_landed")
        raw_landed = [sem("raw_landed0"), sem("raw_landed1")]
        cmp_landed = [sem("cmp_w_landed0"), sem("cmp_w_landed1")]
        h_ready = sem("w_hi_ready")
        l_ready = sem("w_lo_ready")
        halves_done = sem("halves_done")
        drained = sem("unit_drained")
        mod_turned = sem("mod_turned")
        cmp_w_used = sem("cmp_w_used")
        ones_ready = sem("ones_ready")
        vec_ready = sem("vec_ready")
        pad_ready = sem("silu_pad_ready")
        sc_ready = sem("silu_c_ready")
        sq_ready = sem("squares_ready")
        sq_sums = sem("squares_summed")
        var_steps = sem("var_steps")
        stat_done = sem("stat_done")
        root_done = sem("root_done")
        recip_done = sem("recip_done")
        diag_done = sem("diag_done")
        rb_done = sem("rstd_spread")
        z_ready = sem("z_ready")
        xh_ready = sem("x_hi_ready")
        xl_ready = sem("x_lo_ready")
        x_scaled = sem("x_scaled")
        x_normed = sem("x_normed")
        mods_ready = sem("mods_ready")
        gate_ready = sem("gate_ready")
        silu_done = sem("silu_done")
        prod_done = sem("prod_done")
        hh_done = sem("h_hi_done")
        k_squared = sem("k_squared")
        k_gained = sem("k_gained")
        kstat_done = sem("kstat_done")
        kroot_done = sem("kroot_done")
        krecip_done = sem("krecip_done")
        kdiag_done = sem("kdiag_done")
        krb_done = sem("k_rstd_spread")
        k_normed = sem("k_normed")
        k_swapped = sem("k_swapped")
        k_terms = sem("k_rope_terms")
        k_ready = sem("k_ready")
        v_turned = sem("v_turned")
        v_ready = sem("v_ready")
        q_squared = sem("q_squared")
        qstat_done = sem("qstat_done")
        qroot_done = sem("qroot_done")
        qrecip_done = sem("qrecip_done")
        q_scaled = sem("q_scale_ready")
        q_swapped = sem("q_swapped")
        q_terms = sem("q_rope_terms")
        gates_done = sem("gates_done")
        qcur_ready = sem("q_cur_ready")
        qk_done = sem("qk_done")
        top_done = sem("top_done")
        nb_ready = sem("neg_top_ready")
        exp_done = sem("exp_done")
        inv_done = sem("inv_done")
        p_ready = sem("probs_ready")
        t_done = sem("probs_turned")
        pta_ready = sem("probs_t_act_ready")
        ptd_ready = sem("probs_t_dve_ready")
        pv_done = sem("pv_done")
        oh_ready = sem("o_hi_ready")
        cg_copied = sem("cg_copied")
        u_ready = sem("conv_in_ready")
        conv_terms = sem("conv_terms")
        y_done = sem("y_done")
        yh_done = sem("y_hi_done")
        merge_terms = sem("merge_terms")
        zh_done = sem("z_hi_done")
        wg_done = sem("gate_w_hi_done")
        wg_ready = sem("gate_w_ready")
        gt_done = sem("gate_logits_done")
        gt_ready = sem("gate_tok_ready")
        cmp_ready = sem("cmp_in_ready")
        hid_done = sem("cmp_hidden_done")
        gelu_done = sem("cmp_gelu_done")
        cmp_done = sem("cmp_out_done")
        kc_raw = sem("k_cmp_raw")
        kv2_copied = sem("kv2_copied")
        rope2_swapped = sem("rope2_swapped")
        rope2_terms = sem("rope2_terms")
        rope2_done = sem("rope2_done")
        v2_turned = sem("v2_turned")
        pool_steps = sem("pool_steps")
        pooled_ready = sem("pooled_ready")
        mixed_done = sem("pool_mixed")
        ph_done = sem("pool_hi_done")
        pl_done = sem("pool_lo_done")
        g2_copied = sem("gates2_copied")
        g2_done = sem("gates2_done")
        masked = sem("scores_masked")
        cmp_masked = sem("cmp_masked")
        cmp_steps = sem("cmp_softmax_steps")
        coef_steps = sem("coef_steps")
        relu_done = sem("relu_done")
        stored = sem("stored")

        block = ctx.enter_context(nc.Block())


        @block.sync
        def _(sp):
            def load(pr, k, kcs):
                sp.wait_ge(l_ready, 4 * pr + (2 * k + 2))
                cols = slice(0, kcs * 2 * P)
                sp.dma_start(raw[:, k % 2, cols], a["stream"][2 * pr + k, :, cols]).then_inc(raw_landed[k % 2], LANDED)

            def units(first, count, kcs=KD):
                with sp.Fori(0, count // 2) as p:
                    for j in range(2):
                        load(p, first + j, kcs)
                if count % 2:
                    load(0, first + count - 1, kcs)

            def run(first, end):
                units(first, end - first)

            last_out = FIRST["k"] - 6
            run(0, last_out)
            for o in range(6):
                load(0, last_out + o, KD if o in (1, 3) else SLABS[2])
            run(FIRST["k"], FIRST["kcvc"] - 4)
            units(FIRST["kcvc"] - 4, 4, SLABS[2])
            run(FIRST["kcvc"], FIRST["gates2"])
            for i in range(2):
                for c in range(2):
                    if i:
                        sp.wait_ge(cmp_w_used, c + 1)
                    sp.dma_start(wide_scr[:, c, :], a["cmp_w"][2 * i + c]).then_inc(cmp_landed[c], 16)
            run(FIRST["gates2"], FIRST["merge2"])
            units(FIRST["merge2"], 8, 4)
            run(FIRST["wout2"], UNITS)

            for i in range(4):
                chunks = slice(2 * i, 2 * i + 2)
                sp.wait_ge(x_normed, 2 * i + 2)
                sp.dma_start(out[:, chunks, :], x[:, chunks, 0:S]).then_inc(stored, 16)
            sp.wait_ge(stored, 16 * 4)

        @block.gpsimd
        def _(pool):
            def sums(n, width):
                for kc in range(1, KD - 2):
                    pool.wait_ge(sq_ready, KD * n + kc + 1)
                    if kc > 1:
                        pool.wait_ge(sq_sums, 5 * (n - 1) + kc - 1)
                    pool.tensor_tensor(sq[:, 0, 0:width], sq[:, 0, 0:width], sq[:, kc, 0:width], ALU.add).then_inc(sq_sums, 1)

            sums(1, NB)
            for g in range(HKV):
                with pool.Fori(0, 2) as p:
                    for j in range(2):
                        k = FIRST["conv"] + 4 * g + j
                        if g == 0 and j == 0:
                            pool.wait_ge(drained, FIRST["conv"] + 2)
                        pool.wait_ge(halves_done, 4 * p + 2 * k + 2)
                        pool.tensor_copy(q_cur[:, j, :], q_rows[:, 2 * p + (4 * g + j), :]).then_inc(qcur_ready, 1)
            sums(2, S)
            sums(3, NB)
            with pool.Fori(0, 4) as r:
                k = FIRST["gates2"]
                pool.wait_ge(rope2_done, 7)
                pool.wait_ge(halves_done, 4 * r + 2 * k + 4)
                pool.tensor_copy(q_cur[:, 0, :], q2[:, r, :]).then_inc(qcur_ready, 1)
            sums(4, S)
            sums(5, S)

        @block.scalar
        def _(act):
            act.dma_start(vec[:], a["vectors"]).then_inc(vec_landed, 16)
            for i in range(2):
                act.dma_start(x[:, 4 * i:4 * i + 4, :], a["tokens"][:, 4 * i:4 * i + 4, :]).then_inc(x_landed[i], 16)
            act.dma_start(cst[:], a["consts"]).then_inc(cst_landed, 16)
            act.dma_start(late_w[:], a["late"]).then_inc(late, 16)

            def split(pr, k, half):
                if half == 0:
                    act.wait_ge(raw_landed[k % 2], LANDED * pr + LANDED * (k // 2 + 1))
                act.wait_ge(halves_done, 4 * pr + (2 * k + half + 1))
                cols = slice(half * HALF, (half + 1) * HALF)
                act.activation(w_hi[:, k % 2, cols], raw[:, k % 2, cols], ACT.Copy).then_inc(h_ready, 1)

            def splits(pr, k):
                split(pr, k, 0)
                split(pr, k, 1)

            def done(pr, k):
                act.wait_ge(halves_done, 4 * pr + (2 * k + 6))

            def bank(k, t, n=S):
                return ps_u[:, 2 * (k % 2) + t, 0:n]

            act.wait_ge(vec_landed, 16)
            for i in range(2):
                act.activation(sc[:, :, i], vec[:, V_C + i * KD:V_C + (i + 1) * KD], ACT.Silu).then_inc(sc_ready, 1)
            act.wait_ge(sc_ready, 2)
            act.wait_ge(pad_ready, 1)
            act.activation(sc_pad[:, :, 0:2], sc[:], ACT.Copy).then_inc(pad_ready, 1)
            for u in range(2):
                splits(0, u)
            for kc in range(KD):
                act.wait_ge(x_landed[kc // 4], 16)
                act.activation(sq[:, kc, :], x[:, kc, :], ACT.Square).then_inc(sq_ready, 1)

            def roots(n, tiles, width=D):
                act.wait_ge(stat_done, n + 1)
                act.activation(root[:, 0:tiles], ps_a[:, 3, 0:tiles], ACT.Sqrt, bias=eps, scale=1.0 / width)\
                   .then_inc(root_done, 1)

            def norm_hi(i, n, shift):
                for kc in range(KD):
                    act.wait_ge(z_ready, 8 * i + kc + 1)
                    for s, cols in segs(n):
                        if shift is None:
                            ins = act.activation(x_hi[:, kc, cols], sq[:, kc, cols], ACT.Copy)
                        else:
                            ins = act.activation(x_hi[:, kc, cols], sq[:, kc, cols], ACT.Identity,
                                                 bias=mods[:, shift * KD + kc, s:s + 1])
                    ins.then_inc(xh_ready, 1)

            def squares(pr, k, m, n, gain=None):
                act.wait_ge(drained, 2 * pr + (k + 3))
                for t in range(2):
                    if gain is not None:
                        act.activation(sq[:, m + t, S:NB], x[:, m + t, 0:S], ACT.Square, scale=vcol(gain, m + t))
                    act.activation(sq[:, m + t, 0:n], x[:, m + t, 0:n], ACT.Square).then_inc(sq_ready, 1)

            act.wait_ge(cst_landed, 16)
            with act.Fori(0, MOD_FRONT // 4) as p:
                for j in range(4):
                    splits(2 * p, j + 2)
            roots(0, 4)
            norm_hi(0, NB, 0)

            def slab1(s, pr, k, chunks, last):
                with act.Fori(0, chunks // 2) as p:
                    for j in range(2):
                        ki, m = k + 2 * j, 2 * p + j
                        split(pr + 2 * p, ki + 2, 0)
                        done(pr + 2 * p, ki)
                        act.activation(s1[:, j, :], bank(j, 0, NB), ACT.Silu).then_inc(silu_done, 1)
                        act.wait_ge(prod_done, 8 * s + m + 1)
                        act.activation(h_hi[:, m, :], t1[:, j, :], ACT.Copy).then_inc(hh_done, 1)
                        split(pr + 2 * p, ki + 2, 1)
                        splits(pr + 2 * p, ki + 3)
                for i, o in enumerate((0, None, 1, None, 2, 3)):
                    ko = k + 2 * chunks + i
                    split(pr, ko + 2, 0)
                    if last and o is not None:
                        squares(pr, ko, 2 * o, NB)
                    split(pr, ko + 2, 1)

            k = FIRST["ffn1"]
            with act.Fori(0, 2) as s:
                slab1(s, s * 11, k, SLABS[0], False)
            slab1(2, 0, k + 44, SLABS[2], True)
            roots(1, 4)
            norm_hi(1, NB, 3)

            def swiglu(base, count, n, gain):
                def slab(pr, k, c, chunks, last):
                    with act.Fori(0, chunks // 2) as p:
                        for j in range(2):
                            split(pr + p, k + j + 2, 0)
                            done(pr + p, k + j)
                            act.activation(s1[:, j, 0:n], bank(k + j, 0, n), ACT.Silu).then_inc(silu_done, 1)
                            act.wait_ge(prod_done, c + 2 * p + (j + 1))
                            act.activation(h_hi[:, 2 * p + j, 0:n], t1[:, j, 0:n], ACT.Copy).then_inc(hh_done, 1)
                            split(pr + p, k + j + 2, 1)
                    for i in range(4):
                        split(pr, k + chunks + i + 2, 0)
                        if last:
                            squares(pr, k + chunks + i, 2 * i, n, gain)
                        split(pr, k + chunks + i + 2, 1)

                with act.Fori(0, 2) as s:
                    slab(s * 6, base, s * 8 + count, SLABS[0], False)
                slab(0, base + 24, count + 16, SLABS[2], True)

            k = FIRST["k"]
            split(0, k + 2, 0)
            done(0, k)
            for t in range(HKV):
                act.activation(s1[:, t, :], bank(k, t, NB), ACT.Square).then_inc(k_squared, 1)
            split(0, k + 2, 1)
            splits(0, k + 3)
            act.wait_ge(kstat_done, 1)
            act.activation(root[:, 0:8], ps_a[:, 1, 8:16], ACT.Sqrt, bias=eps, scale=1.0 / HD).then_inc(kroot_done, 1)
            with act.Fori(0, 2) as p:
                for j in range(2):
                    k = FIRST["q"] + j
                    split(p, k + 2, 0)
                    done(p, k)
                    for t in range(2):
                        act.activation(q_sq[:, 4 * p + (2 * j + t), :], bank(k, t), ACT.Square).then_inc(q_squared, 1)
                    split(p, k + 2, 1)
            act.wait_ge(qstat_done, 1)
            act.activation(root[:, 16:32], ps_a[:, 1, 16:32], ACT.Sqrt, bias=eps, scale=1.0 / HD).then_inc(qroot_done, 1)

            with act.Fori(0, 4) as p:
                for j in range(2):
                    k = FIRST["gates"] + j
                    split(p, k + 2, 0)
                    done(p, k)
                    act.activation(g_conv[:, 2 * p + j, :], bank(k, 0), ACT.Sigmoid)
                    act.activation(g_attn[:, 2 * p + j, :], bank(k, 1), ACT.Sigmoid).then_inc(gates_done, 1)
                    split(p, k + 2, 1)

            for g in range(HKV):
                with act.Fori(0, 2) as p:
                    for j in range(2):
                        k = FIRST["conv"] + 4 * g + j
                        h = 2 * p + (4 * g + j)
                        for qt in range(TT):
                            act.wait_ge(nb_ready, 2 * h + (qt + 1))
                            act.activation(probs[:, qt, :], ps_a[:, qt, :], ACT.Exp, bias=neg_top[:, qt:qt + 1],
                                           scale=q_scale[:, ds(2 * h + qt, 1)],
                                           accum_out=total[:, qt:qt + 1]).then_inc(exp_done, 1)
                        split(p, k + 2, 0)
                        done(p, k)
                        act.activation(s1[:, j, 0:S], bank(k, 0), ACT.Copy).then_inc(cg_copied, 1)
                        act.wait_ge(t_done, 2 * h + 1)
                        act.activation(probs_t[:, :, 0:P], ps_a[:, 2, :].rearrange("p (k q) -> p k q", k=4), ACT.Copy)\
                           .then_inc(pta_ready, 1)
                        act.wait_ge(pv_done, h + 1)
                        act.activation(h_hi[:, h, S:NB], ps_a[:, 2, 0:S], ACT.Copy).then_inc(oh_ready, 1)
                        split(p, k + 2, 1)
            with act.Fori(0, 2) as p:
                for j in range(2):
                    k = FIRST["bg"] + j
                    split(p, k + 2, 0)
                    for t in range(2):
                        act.wait_ge(y_done, 4 * p + (2 * j + t + 1))
                        act.activation(h_hi[:, 4 * p + (2 * j + t), 0:S], t1[:, t, 0:S], ACT.Copy).then_inc(yh_done, 1)
                    split(p, k + 2, 1)
            with act.Fori(0, 4) as p:
                for j in range(2):
                    k = FIRST["merge"] + j
                    split(p, k + 2, 0)
                    act.wait_ge(merge_terms, 6 * p + (3 * j + 3))
                    act.activation(x_hi[:, 2 * p + j, 0:S], t1[:, j, 0:S], ACT.Copy).then_inc(zh_done, 1)
                    split(p, k + 2, 1)
            for i in range(4):
                k = FIRST["wout"] + i
                split(0, k + 2, 0)
                squares(0, k, 2 * i, S)
                split(0, k + 2, 1)

            roots(2, 2)
            norm_hi(2, S, 6)
            swiglu(FIRST["ffn2"], 22, S, V_F1)
            act.wait_ge(var_steps, 3)
            act.activation(root[:, 0:4], var[:], ACT.Sqrt).then_inc(root_done, 1)
            norm_hi(3, S, None)

            act.wait_ge(late, 16)
            act.activation(wg_hi[:], wg[:], ACT.Copy).then_inc(wg_done, 1)
            k = FIRST["kcvc"]
            for i in range(7):
                split(0, k + i + 2, 0)
                if i in (3, 4):
                    done(0, k + i)
                    g = i - 3
                    for t in range(2):
                        for b in range(2):
                            ins = act.activation(q2[g * DH:(g + 1) * DH, 2 * t + b, :],
                                                 ps_u[b * DH:(b + 1) * DH, 2 * ((k + i) % 2) + t, 0:S],
                                                 ACT.Copy, scale=float(DH) ** -0.5)
                    ins.then_inc(kv2_copied, 1)
                split(0, k + i + 2, 1)
            act.wait_ge(gt_done, 1)
            act.activation(g_tok[:], ps_a[:, 1, 0:TT * 3 * H2].rearrange("p (t c) -> p t c", t=TT), ACT.Sigmoid)\
               .then_inc(gt_ready, 1)
            for i in range(2):
                act.wait_ge(hid_done, i + 1)
                act.activation(hid[:, i, :, :], ps_a[:, 0, i * 64:i * 64 + 2 * G2 * NC].rearrange("p (h c) -> p h c", h=2),
                               ACT.Gelu_apprx_tanh).then_inc(gelu_done, 1)
            for i in range(4):
                act.wait_ge(mixed_done, i + 1)
                act.activation(mixed[:, i, :], ps_a[:, 3, 0:S], ACT.Identity, scale=vcol(V_PS, i)).then_inc(ph_done, 1)
                act.wait_ge(ph_done, 2 * i + 1)
                act.activation(h_hi[:, i, S:NB], mixed[:, i, :], ACT.Copy).then_inc(ph_done, 1)

            with act.Fori(0, 4) as r:
                for g in range(G2):
                    k = FIRST["gates2"] + g
                    h = 2 * r + g
                    for qt in range(TT):
                        act.wait_ge(masked, 4 * h + (2 * qt + 2))
                        for b in range(2):
                            act.activation(probs[:, qt, b * S:(b + 1) * S], probs[:, qt, b * S:(b + 1) * S], ACT.Exp,
                                           bias=neg_top[:, 2 * qt + b:2 * qt + b + 1],
                                           accum_out=total[:, 2 * qt + b:2 * qt + b + 1]).then_inc(exp_done, 1)
                    act.wait_ge(cmp_masked, 2 * h + 2)
                    for qt in range(TT):
                        ins = act.activation(sc_c[:, qt, :], sc_c[:, qt, :], ACT.Exp, bias=neg_top[:, 4 + qt:5 + qt])
                    ins.then_inc(exp_done, 1)
                    split(r, k + 2, 0)
                    done(r, k)
                    act.activation(gates2[:, 2 * r + g, :, :], ps_u[:, 2 * (k % 2):2 * (k % 2) + 2, 0:S], ACT.Copy)\
                       .then_inc(g2_copied, 1)
                    split(r, k + 2, 1)
                    act.wait_ge(t_done, 2 * HQ + 3 * h + 1)
                    act.activation(probs_t[:, :, 0:P], ps_a[:, 2, :].rearrange("p (k q) -> p k q", k=4), ACT.Copy)\
                       .then_inc(pta_ready, 1)
                    act.wait_ge(pv_done, HQ + h + 1)
                    act.activation(h_hi[g * DH:(g + 1) * DH, r, 0:S], ps_a[g * DH:(g + 1) * DH, 1, 0:S], ACT.Copy)\
                       .then_inc(oh_ready, 1)
            with act.Fori(0, 4) as p:
                for j in range(2):
                    k = FIRST["merge2"] + j
                    act.activation(s1[:, j, :].rearrange("p (a n) -> p a n", a=2), gates2[:, 2 * p + j, :, :], ACT.Sigmoid)\
                       .then_inc(g2_done, 1)
                    split(p, k + 2, 0)
                    act.wait_ge(merge_terms, 6 * p + (24 + 3 * j + 3))
                    act.activation(x_hi[:, 2 * p + j, 0:S], t1[:, j, 0:S], ACT.Copy).then_inc(zh_done, 1)
                    split(p, k + 2, 1)
            for i in range(4):
                k = FIRST["wout2"] + i
                split(0, k + 2, 0)
                squares(0, k, 2 * i, S)
                split(0, k + 2, 1)
            roots(4, 2)
            norm_hi(4, S, None)

            def relu2(pr, k, c, last):
                with act.Fori(0, 2) as p:
                    for j in range(2):
                        split(pr + p, k + j + 2, 0)
                        done(pr + p, k + j)
                        for t in range(2):
                            act.activation(s1[:, t, 0:S], bank(k + j, t), ACT.Relu).then_inc(relu_done, 1)
                        for t in range(2):
                            act.wait_ge(prod_done, c + 4 * p + (2 * j + t + 1))
                            act.activation(h_hi[:, 4 * p + (2 * j + t), 0:S], t1[:, t, 0:S], ACT.Copy).then_inc(hh_done, 1)
                        split(pr + p, k + j + 2, 1)
                for i in range(4):
                    more = not (last and i >= 2)
                    if more:
                        split(pr, k + 4 + i + 2, 0)
                    if last:
                        squares(pr, k + 4 + i, 2 * i, S)
                    if more:
                        split(pr, k + 4 + i + 2, 1)

            with act.Fori(0, SLABS2 - 1) as s:
                relu2(s * 4, FIRST["ff"], s * 8 + 44, False)
            relu2(0, FIRST["ff"] + 8 * (SLABS2 - 1), 44 + 8 * (SLABS2 - 1), True)
            roots(5, 2)

        @block.vector
        def _(dve):
            dve.memset(ones[:], 1.0).then_inc(ones_ready, 1)
            dve.memset(u_pad[:], 0.0).then_inc(l_ready, 4)
            dve.memset(p_pad[:], 0.0).then_inc(drained, 2)
            dve.memset(sc_pad[:].bitcast(F32), 0.0).then_inc(pad_ready, 1)
            dve.memset(pc[:], 0.0).then_inc(ones_ready, 1)
            dve.memset(vc_tok[:], 0.0).then_inc(ones_ready, 1)
            dve.wait_ge(ones_ready, 3)

            def split(pr, k, half):
                if half == 0:
                    dve.wait_ge(drained, 2 * pr + k)
                cols = slice(half * HALF, (half + 1) * HALF)
                dve.wait_ge(h_ready, 4 * pr + (2 * k + half + 1))
                dve.tensor_tensor(w_lo[:, k % 2, cols], raw[:, k % 2, cols], w_hi[:, k % 2, cols].bitcast(F32),
                                  ALU.subtract).then_inc(l_ready, 1)

            def splits(pr, k):
                split(pr, k, 0)
                split(pr, k, 1)

            def done(pr, k):
                dve.wait_ge(halves_done, 4 * pr + (2 * k + 6))

            def bank(k, t, n=S):
                return ps_u[:, 2 * (k % 2) + t, 0:n]

            dve.wait_ge(pad_ready, 2)
            dve.tensor_tensor(sc_pad[:, :, 2:4], sc[:], sc_pad[:, :, 0:2].bitcast(F32), ALU.subtract).then_inc(pad_ready, 1)
            dve.tensor_scalar(bm_half[:], bm, 0.5, None, ALU.mult).then_inc(vec_ready, 1)
            dve.tensor_tensor(gg[:], vec[:, V_F1:V_F1 + KD], vec[:, V_MIX:V_MIX + KD], ALU.mult).then_inc(vec_ready, 1)

            def mod(pr, k, m, b):
                done(pr, k)
                for q in range(P // MOD_ROWS):
                    rows = slice(q * MOD_ROWS, (q + 1) * MOD_ROWS)
                    for t in range(2):
                        lo = t * P + q * MOD_ROWS
                        ins = dve.transpose(turned[rows, b, t, :], ps_a[0:MOD_ROWS, b, lo:lo + MOD_ROWS])
                ins.then_inc(mod_turned, 1)
                dve.wait_ge(mod_turned, m + 1)
                dve.tensor_tensor(mod_sum[:, ds(2 * m, 2), :], turned[:, b, :, 0:2], turned[:, b, :, 2:4], ALU.add)\
                   .then_inc(drained, 1)

            def modulations(lo, hi, norms, count):
                for s in range(2):
                    ins = dve.tensor_tensor(mods[:, lo:hi, s], mod_sum[:, lo:hi, s], bm[:, lo:hi], ALU.add)
                ins.then_inc(gate_ready, 1)
                dve.wait_ge(gate_ready, count)
                for i, chunk, v in norms:
                    for s in range(2):
                        ins = dve.scalar_tensor_tensor(am[:, i, :, s], mods[:, chunk * KD:(chunk + 1) * KD, s], 1.0,
                                                       vec[:, v:v + KD], ALU.add, ALU.mult)
                ins.then_inc(mods_ready, 1)

            def gates_of(i, chunk):
                for s in range(2):
                    ins = dve.scalar_tensor_tensor(gate_half[:, i, :, s], mod_sum[:, chunk * KD:(chunk + 1) * KD, s], 0.5,
                                                   bm_half[:, chunk * KD:(chunk + 1) * KD], ALU.mult, ALU.add)
                ins.then_inc(gate_ready, 1)

            def spread(n, tiles):
                dve.wait_ge(root_done, n + 1)
                dve.reciprocal(rstd[:, 0:tiles], root[:, 0:tiles]).then_inc(recip_done, 1)
                dve.wait_ge(recip_done, n + 1)
                for t in range(tiles):
                    ins = dve.tensor_scalar(t1[:, 0, t * P:(t + 1) * P], ident, rstd[:, t:t + 1], None, ALU.mult)
                ins.then_inc(diag_done, 1)

            def norm_lo(n, i, width, scale, shift, at=0):
                dve.wait_ge(rb_done, n + 1)

                def z(kc):
                    for s, cols in segs(width):
                        spread_cols = slice(at + cols.start, at + cols.stop)
                        ins = dve.scalar_tensor_tensor(sq[:, kc, cols], x[:, kc, cols], scale(kc, s), ps_a[:, 2, spread_cols],
                                                       ALU.mult, ALU.mult)
                    ins.then_inc(z_ready, 1)

                def lo(kc):
                    dve.wait_ge(xh_ready, 8 * i + kc + 1)
                    for s, cols in segs(width):
                        hi = x_hi[:, kc, cols].bitcast(F32)
                        if shift is None:
                            ins = dve.tensor_tensor(x_lo[:, kc, cols], sq[:, kc, cols], hi, ALU.subtract)
                        else:
                            ins = dve.scalar_tensor_tensor(x_lo[:, kc, cols], sq[:, kc, cols],
                                                           mods[:, shift * KD + kc, s:s + 1], hi, ALU.add, ALU.subtract)
                    ins.then_inc(xl_ready, 1)

                z(0)
                for kc in range(KD):
                    if kc + 1 < KD:
                        z(kc + 1)
                    lo(kc)

            def modulated(i, scale):
                return lambda kc, s: am[:, i, kc, s:s + 1]

            def plain(v):
                return lambda kc, s: vcol(v, kc)

            def add_out(pr, k, m, n, gate, b=None):
                done(pr, k)
                b = k if b is None else b
                for t in range(2):
                    for s, cols in segs(n):
                        if gate is None:
                            ins = dve.tensor_tensor(x[:, m + t, cols], bank(b, t, n)[:, cols], x[:, m + t, cols], ALU.add)
                        else:
                            ins = dve.scalar_tensor_tensor(x[:, m + t, cols], bank(b, t, n)[:, cols], gate(m + t, s),
                                                           x[:, m + t, cols], ALU.mult, ALU.add)
                ins.then_inc(drained, 1)

            dve.wait_ge(vec_ready, 2)
            for u in range(2):
                splits(0, u)
            with dve.Fori(0, MOD_FRONT // 4) as p:
                for j in range(4):
                    split(2 * p, j + 2, 0)
                    mod(2 * p, j, 4 * p + j, j % 2)
                    split(2 * p, j + 2, 1)
            dve.wait_ge(drained, MOD_FRONT + 2)
            modulations(0, 2 * KD, ((0, 1, V_N1),), 1)
            spread(0, 4)
            dve.wait_ge(mods_ready, 1)
            norm_lo(0, 0, NB, modulated(0, 1), 0)

            def slab1(s, pr, k, chunks, last):
                def ride(m):
                    return MOD_RIDE * s + (MOD_FRONT + m)

                with dve.Fori(0, chunks // 2) as p:
                    for j in range(2):
                        ki, m = k + 2 * j, 2 * p + j
                        split(pr + 2 * p, ki + 2, 0)
                        dve.wait_ge(silu_done, 8 * s + m + 1)
                        dve.tensor_tensor(t1[:, j, :], s1[:, j, :], bank(j, 1, NB), ALU.mult).then_inc(prod_done, 1)
                        dve.wait_ge(hh_done, 8 * s + m + 1)
                        dve.tensor_tensor(h_lo[:, m, :], t1[:, j, :], h_hi[:, m, :].bitcast(F32), ALU.subtract)\
                           .then_inc(drained, 1)
                        split(pr + 2 * p, ki + 2, 1)
                        split(pr + 2 * p, ki + 3, 0)
                        mod(pr + 2 * p, ki + 1, ride(m), j)
                        split(pr + 2 * p, ki + 3, 1)
                ko = k + 2 * chunks
                dve.wait_ge(drained, 2 * pr + (ko + 2))
                gates_of(0, 2)
                dve.wait_ge(gate_ready, s + 2)
                for i, o in enumerate((0, None, 1, None, 2, 3)):
                    split(pr, ko + i + 2, 0)
                    if o is None:
                        mod(pr, ko + i, ride(chunks + i // 2), (i // 2) % 2)
                    else:
                        if last and o == 3:
                            dve.wait_ge(drained, ko + i + 1)
                            gates_of(1, 8)
                            modulations(3 * KD, 8 * KD, ((1, 4, V_N2), (2, 7, V_N3)), 6)
                        add_out(pr, ko + i, 2 * o, NB, lambda m, s: gate_half[:, 0, m, s:s + 1], o)
                    split(pr, ko + i + 2, 1)

            k = FIRST["ffn1"]
            with dve.Fori(0, 2) as s:
                slab1(s, s * 11, k, SLABS[0], False)
            slab1(2, 0, k + 44, SLABS[2], True)
            spread(1, 4)
            dve.wait_ge(mods_ready, 2)
            norm_lo(1, 1, NB, modulated(1, 4), 3)

            def swiglu(base, count, n, i):
                def gate(m, s):
                    return gate_half[:, i, m, s:s + 1]

                def slab(pr, k, c, chunks):
                    with dve.Fori(0, chunks // 2) as p:
                        for j in range(2):
                            split(pr + p, k + j + 2, 0)
                            dve.wait_ge(silu_done, c + 2 * p + (j + 1))
                            dve.tensor_tensor(t1[:, j, 0:n], s1[:, j, 0:n], bank(k + j, 1, n), ALU.mult)\
                               .then_inc(prod_done, 1)
                            dve.wait_ge(hh_done, c + 2 * p + (j + 1))
                            dve.tensor_tensor(h_lo[:, 2 * p + j, 0:n], t1[:, j, 0:n],
                                              h_hi[:, 2 * p + j, 0:n].bitcast(F32), ALU.subtract).then_inc(drained, 1)
                            split(pr + p, k + j + 2, 1)
                    for o in range(4):
                        split(pr, k + chunks + o + 2, 0)
                        add_out(pr, k + chunks + o, 2 * o, n, gate)
                        split(pr, k + chunks + o + 2, 1)

                with dve.Fori(0, 2) as s:
                    slab(s * 6, base, s * 8 + count, SLABS[0])
                slab(0, base + 24, count + 16, SLABS[2])

            k = FIRST["k"]
            split(0, k + 2, 0)
            for t in range(HKV):
                dve.wait_ge(k_squared, t + 1)
                ins = dve.tensor_scalar(k_all[:, t, :], bank(k, t, NB), vcol(V_KG, 0), None, ALU.mult)
                ins.then_inc(drained if t else k_gained, 1)
            split(0, k + 2, 1)
            split(0, k + 3, 0)
            done(0, k + 1)
            dve.tensor_copy(v_feat[:, 0, :], bank(k + 1, 0, NB))
            dve.tensor_copy(v_feat[:, 1, :], bank(k + 1, 1, NB)).then_inc(drained, 1)
            split(0, k + 3, 1)
            dve.wait_ge(kroot_done, 1)
            dve.reciprocal(rstd[:, 0:8], root[:, 0:8]).then_inc(krecip_done, 1)
            dve.wait_ge(krecip_done, 1)
            for t in range(8):
                ins = dve.tensor_scalar(t1[:, t // 4, (t % 4) * P:(t % 4 + 1) * P], ident, rstd[:, t:t + 1], None, ALU.mult)
            ins.then_inc(kdiag_done, 1)

            def q_gain(i):
                kq = FIRST["q"] + i
                split(0, kq + 2, 0)
                for t in range(2):
                    dve.wait_ge(q_squared, 2 * i + t + 1)
                    ins = dve.tensor_scalar(q_rows[:, 2 * i + t, :], bank(kq, t), vcol(V_QG, 0), None, ALU.mult)
                ins.then_inc(drained, 1)
                split(0, kq + 2, 1)

            q_gain(0)
            dve.wait_ge(v_turned, 1)
            dve.tensor_copy(v_tok[:, :, 0, :], ps_a[:, 0, :].rearrange("p (c d) -> p c d", c=4)).then_inc(v_ready, 1)
            q_gain(1)
            for t in range(HKV):
                dve.wait_ge(krb_done, t + 1)
                dve.tensor_tensor(k_all[:, t, :], k_all[:, t, :], ps_a[:, 2 + t, :], ALU.mult).then_inc(k_normed, 1)
            q_gain(2)
            dve.wait_ge(k_normed, 2)
            for t in range(HKV):
                dve.wait_ge(k_swapped, t + 1)
                if t:
                    dve.wait_ge(k_ready, t)
                dve.tensor_tensor(t1[:, 0, 0:S], k_all[:, t, 0:S], cos1, ALU.mult)
                dve.tensor_tensor(t1[:, 1, 0:S], ps_a[:, 2 + t, 0:S], sin1, ALU.mult).then_inc(k_terms, 1)
                dve.wait_ge(k_terms, t + 1)
                dve.tensor_tensor(k_all[:, t, 0:S], t1[:, 0, 0:S], t1[:, 1, 0:S], ALU.add).then_inc(k_ready, 1)
            q_gain(3)
            dve.wait_ge(v_turned, 2)
            dve.tensor_copy(v_tok[:, :, 1, :], ps_a[:, 0, :].rearrange("p (c d) -> p c d", c=4)).then_inc(v_ready, 1)
            dve.wait_ge(qroot_done, 1)
            dve.reciprocal(rstd[:, 16:32], root[:, 16:32]).then_inc(qrecip_done, 1)
            dve.wait_ge(qrecip_done, 1)
            dve.tensor_scalar(q_scale[:], rstd[:, 16:32], float(HD) ** -0.5, None, ALU.mult).then_inc(q_scaled, 1)

            dve.wait_ge(drained, FIRST["gates"] + 2)
            with dve.Fori(0, 4) as p:
                for j in range(2):
                    k = FIRST["gates"] + j
                    h = 2 * p + j
                    split(p, k + 2, 0)
                    dve.wait_ge(q_swapped, h + 1)
                    dve.tensor_tensor(t1[:, j, 0:S], q_rows[:, h, :], cos1, ALU.mult)
                    dve.tensor_tensor(t1[:, j, S:NB], ps_a[:, 2 + j, 0:S], sin1, ALU.mult).then_inc(q_terms, 1)
                    dve.wait_ge(q_terms, h + 1)
                    dve.wait_ge(gates_done, h + 1)
                    dve.tensor_tensor(q_rows[:, h, :], t1[:, j, 0:S], t1[:, j, S:NB], ALU.add).then_inc(drained, 1)
                    split(p, k + 2, 1)

            dve.wait_ge(q_scaled, 1)
            for g in range(HKV):
                with dve.Fori(0, 2) as p:
                    for j in range(2):
                        k = FIRST["conv"] + 4 * g + j
                        h = 2 * p + (4 * g + j)
                        dve.wait_ge(qk_done, h + 1)
                        for qt in range(TT):
                            ins = dve.tensor_reduce(top[:, qt:qt + 1], ps_a[:, qt, :], AX_X, ALU.max)
                        ins.then_inc(top_done, 1)
                        dve.wait_ge(top_done, h + 1)
                        for qt in range(TT):
                            dve.tensor_scalar(neg_top[:, qt:qt + 1], top[:, qt:qt + 1], q_scale[:, ds(2 * h + qt, 1)], -1.0,
                                              ALU.mult, ALU.mult).then_inc(nb_ready, 1)
                        dve.wait_ge(exp_done, 2 * h + 2)
                        dve.reciprocal(inv[:, 0:TT], total[:, 0:TT]).then_inc(inv_done, 1)
                        dve.wait_ge(inv_done, h + 1)
                        for qt in range(TT):
                            dve.tensor_scalar(probs[:, qt, :], probs[:, qt, :], inv[:, qt:qt + 1], None, ALU.mult)\
                               .then_inc(p_ready, 1)
                        split(p, k + 2, 0)
                        dve.wait_ge(cg_copied, h + 1)
                        dve.tensor_tensor(u_pad[:, 1:S + 1], s1[:, j, 0:S], bank(k, 1), ALU.mult).then_inc(u_ready, 1)
                        dve.wait_ge(t_done, 2 * h + 2)
                        dve.tensor_copy(probs_t[:, :, P:2 * P], ps_a[:, 3, :].rearrange("p (k q) -> p k q", k=4))\
                           .then_inc(ptd_ready, 1)
                        dve.wait_ge(u_ready, h + 1)
                        dve.tensor_scalar(t1[:, 0, 0:S], u_pad[:, 0:S], vcol(V_CONV, h), None, ALU.mult)\
                           .then_inc(conv_terms, 1)
                        dve.wait_ge(conv_terms, 2 * h + 1)
                        dve.scalar_tensor_tensor(t1[:, 1, 0:S], u_pad[:, 1:S + 1], vcol(V_CONV + KD, h), t1[:, 0, 0:S],
                                                 ALU.mult, ALU.add).then_inc(conv_terms, 1)
                        dve.wait_ge(conv_terms, 2 * h + 2)
                        dve.scalar_tensor_tensor(y_conv[:, h, :], u_pad[:, 2:S + 2], vcol(V_CONV + 2 * KD, h), t1[:, 1, 0:S],
                                                 ALU.mult, ALU.add)
                        dve.wait_ge(oh_ready, h + 1)
                        dve.tensor_tensor(h_lo[:, h, S:NB], ps_a[:, 2, 0:S], h_hi[:, h, S:NB].bitcast(F32), ALU.subtract)\
                           .then_inc(drained, 1)
                        split(p, k + 2, 1)
            dve.wait_ge(drained, FIRST["bg"] + 2)
            with dve.Fori(0, 2) as p:
                for j in range(2):
                    k = FIRST["bg"] + j
                    split(p, k + 2, 0)
                    done(p, k)
                    for t in range(2):
                        m = 4 * p + (2 * j + t)
                        dve.tensor_tensor(t1[:, t, 0:S], y_conv[:, m, :], bank(k, t), ALU.mult).then_inc(y_done, 1)
                    for t in range(2):
                        m = 4 * p + (2 * j + t)
                        dve.wait_ge(yh_done, m + 1)
                        ins = dve.tensor_tensor(h_lo[:, m, 0:S], t1[:, t, 0:S], h_hi[:, m, 0:S].bitcast(F32), ALU.subtract)
                    ins.then_inc(drained, 1)
                    split(p, k + 2, 1)

            def merge(base, count, gates):
                with dve.Fori(0, 4) as p:
                    for j in range(2):
                        k = base + j
                        m = 2 * p + j
                        split(p, k + 2, 0)
                        done(p, k)
                        ga, gb = gates(m, j)
                        dve.tensor_tensor(t1[:, j, 0:S], ga, bank(k, 0), ALU.mult).then_inc(merge_terms, 1)
                        dve.tensor_tensor(t1[:, j, S:NB], gb, bank(k, 1), ALU.mult).then_inc(merge_terms, 1)
                        dve.wait_ge(merge_terms, 6 * p + (count + 3 * j + 2))
                        dve.tensor_tensor(t1[:, j, 0:S], t1[:, j, 0:S], t1[:, j, S:NB], ALU.add).then_inc(merge_terms, 1)
                        dve.wait_ge(zh_done, m + (count // 3 + 1))
                        dve.tensor_tensor(x_lo[:, m, 0:S], t1[:, j, 0:S], x_hi[:, m, 0:S].bitcast(F32), ALU.subtract)\
                           .then_inc(drained, 1)
                        split(p, k + 2, 1)

            merge(FIRST["merge"], 0, lambda m, j: (g_conv[:, m, :], g_attn[:, m, :]))
            for i in range(4):
                split(0, FIRST["wout"] + i + 2, 0)
                add_out(0, FIRST["wout"] + i, 2 * i, S, lambda m, s: mods[:, 5 * KD + m, s:s + 1])
                split(0, FIRST["wout"] + i + 2, 1)

            spread(2, 2)
            norm_lo(2, 2, S, modulated(2, 7), 6)
            swiglu(FIRST["ffn2"], 22, S, 1)

            dve.wait_ge(stat_done, 4)
            dve.tensor_scalar(var[:], ps_a[:, 3, 0:2 * TT], 1.0 / D, None, ALU.mult).then_inc(var_steps, 1)
            dve.wait_ge(var_steps, 1)
            dve.tensor_scalar(var[:, 0:TT], var[:, 0:TT], EPS, None, ALU.add).then_inc(var_steps, 1)
            dve.wait_ge(var_steps, 2)
            dve.scalar_tensor_tensor(var[:, TT:2 * TT], var[:, 0:TT], EPS, var[:, TT:2 * TT], ALU.mult, ALU.add)\
               .then_inc(var_steps, 1)
            spread(3, 4)
            norm_lo(3, 3, S, lambda kc, s: gg[:, kc:kc + 1], None, S)
            for kc in range(KD):
                ins = dve.scalar_tensor_tensor(x[:, kc, 0:S], x[:, kc, 0:S], vcol(V_F1, kc), ps_a[:, 2, 0:S], ALU.mult, ALU.mult)
            ins.then_inc(x_scaled, 1)

            dve.wait_ge(wg_done, 1)
            dve.tensor_tensor(wg_lo[:], wg[:], wg_hi[:].bitcast(F32), ALU.subtract).then_inc(wg_ready, 1)
            k = FIRST["kcvc"]
            split(0, k + 2, 0)
            done(0, k)
            for t in range(2):
                for g in range(G2):
                    for j in range(2):
                        rows = slice(j * DH, (j + 1) * DH)
                        src = ps_u[g * DH:(g + 1) * DH, 2 * (k % 2) + t, j * CS:j * CS + NC * CS]
                        pos = pec[rows, t * CB + j * CS:t * CB + (j + 1) * CS]
                        ins = dve.tensor_tensor(cmp_in[t][rows, :, g, :], src.rearrange("p (c l) -> p l c", l=CS),
                                                pos.unsqueeze(2).broadcast_to([DH, CS, NC]), ALU.add)
                ins.then_inc(cmp_ready if t == 0 else drained, 1)
            split(0, k + 2, 1)
            for b in range(2):
                split(0, k + 3 + b, 0)
                done(0, k + 1 + b)
                dve.tensor_copy(kk2[:, b * S:(b + 1) * S], bank(k + 1 + b, 0))
                dve.tensor_copy(v2_feat[:, b, :], bank(k + 1 + b, 1)).then_inc(drained, 1)
                split(0, k + 3 + b, 1)
            for i in range(2):
                split(0, k + 5 + i, 0)
                dve.wait_ge(kv2_copied, i + 1)
                dve.drain().then_inc(drained, 1)
                split(0, k + 5 + i, 1)

            def rope2(n, rows, bank_cols, cos, sin, dst=None):
                dve.wait_ge(rope2_swapped, n + 1)
                if n:
                    dve.wait_ge(rope2_done, n)
                width = rows.shape[-1]
                dve.tensor_tensor(t1[:, 0, 0:width], rows, cos, ALU.mult)
                dve.tensor_tensor(t1[:, 1, 0:width], bank_cols, sin, ALU.mult).then_inc(rope2_terms, 1)
                dve.wait_ge(rope2_terms, n + 1)
                dve.tensor_tensor(rows if dst is None else dst, t1[:, 0, 0:width], t1[:, 1, 0:width], ALU.add)\
                   .then_inc(rope2_done, 1)

            def pool_group(i):
                kp = FIRST["pool"] + i // 2
                w = POOLS[i]
                first = 7 * i
                u = bank(kp, i % 2)
                if i % 2 == 0:
                    split(0, kp + 2, 0)
                    done(0, kp)
                if i:
                    dve.wait_ge(pooled_ready, i)
                dve.tensor_copy(p_pad[:, PAD:PAD + S], u).then_inc(pool_steps, 1)
                dve.wait_ge(pool_steps, first + 1)
                width, step, src, off = 1, 0, p_pad, PAD
                bufs = (t1[:, 0, :], t1[:, 1, :])
                while width < w:
                    dst = bufs[step % 2]
                    if step == 0:
                        ins = dve.tensor_tensor(dst[:, 1:PAD + S], p_pad[:, 1:PAD + S], p_pad[:, 0:PAD + S - 1], ALU.add)
                    else:
                        lo = 2 * width - 1
                        prev = bufs[(step - 1) % 2]
                        ins = dve.tensor_tensor(dst[:, lo:PAD + S], prev[:, lo:PAD + S], prev[:, lo - width:PAD + S - width],
                                                ALU.add)
                    step += 1
                    ins.then_inc(pool_steps, 1)
                    dve.wait_ge(pool_steps, first + 1 + step)
                    width *= 2
                sums = bufs[(step - 1) % 2]
                res = bufs[step % 2]
                cnt = cst[:, K_CNT + i * PAD:K_CNT + (i + 1) * PAD]
                dve.tensor_tensor(res[:, 0:PAD], sums[:, PAD:2 * PAD], cnt, ALU.mult)
                dve.tensor_scalar(res[:, PAD:S], sums[:, 2 * PAD:PAD + S], 1.0 / w, None, ALU.mult).then_inc(pool_steps, 6 - step)
                dve.wait_ge(pool_steps, first + 7)
                ins = dve.tensor_tensor(pooled[:, i, :], res[:, 0:S], p_pad[:, PAD:PAD + S], ALU.subtract)
                ins.then_inc(pooled_ready, 1)

            for i in range(4):
                pool_group(i)
                if i % 2 == 1:
                    dve.drain().then_inc(drained, 1)
                    split(0, FIRST["pool"] + i // 2 + 2, 1)
            for i in range(4):
                dve.wait_ge(ph_done, 2 * i + 2)
                dve.tensor_tensor(h_lo[:, i, S:NB], mixed[:, i, :], h_hi[:, i, S:NB].bitcast(F32), ALU.subtract)\
                   .then_inc(pl_done, 1)
            for b in range(2):
                rope2(b, kk2[:, b * S:(b + 1) * S], ps_a[:, 2 + b, 0:S], cos2, sin2)
            for r in range(4):
                rope2(2 + r, q2[:, r, :], ps_a[:, 2 + r % 2, 0:S], cos2, sin2)
            dve.wait_ge(cmp_done, 2)
            dve.tensor_copy(kc_r[:, 0, :], ps_a[:, 0, 128:128 + NC]).then_inc(kc_raw, 1)
            dve.tensor_copy(vc_tok[0:NC, :, :], ps_a[0:NC, 0, 256:256 + G2 * DH].rearrange("p (g d) -> p g d", g=G2))\
               .then_inc(kc_raw, 1)
            last = CB - 1
            dve.wait_ge(kc_raw, 1)
            rope2(6, kc_r[:, 0, :], ps_a[:, 2, 0:NC], cos2[:, last:S:CS], sin2[:, last:S:CS], kc_r[:, 1, :])
            dve.wait_ge(v2_turned, 1)
            dve.tensor_copy(v2_tok, ps_a[:, 3, :].rearrange("p (b k n) -> p b k n", b=2, k=2)).then_inc(kc_raw, 1)
            dve.wait_ge(gt_ready, 1)

            with dve.Fori(0, 4) as r:
                for g in range(G2):
                    k = FIRST["gates2"] + g
                    h = 2 * r + g
                    dve.wait_ge(qk_done, HQ + h + 1)
                    for qt in range(TT):
                        mask = cst[:, K_MASK + qt * S:K_MASK + (qt + 1) * S].unsqueeze(1).broadcast_to([P, 2, S])
                        rows = probs[:, qt, :].rearrange("p (b n) -> p b n", b=2)
                        dve.tensor_tensor(rows, ps_a[:, qt, :].rearrange("p (b n) -> p b n", b=2), mask, ALU.add)\
                           .then_inc(masked, 1)
                        dve.wait_ge(masked, 4 * h + (2 * qt + 1))
                        dve.tensor_reduce(neg_top[:, 2 * qt:2 * qt + 2], rows, AX_X, ALU.max, negate=True).then_inc(masked, 1)
                    dve.tensor_tensor(sc_c[:], ps_a[:, 2, 0:2 * 16].rearrange("p (t c) -> p t c", t=TT)[:, :, 0:NC], cadd,
                                      ALU.add).then_inc(cmp_masked, 1)
                    dve.wait_ge(cmp_masked, 2 * h + 1)
                    dve.tensor_reduce(neg_top[:, 4:6], sc_c[:], AX_X, ALU.max, negate=True).then_inc(cmp_masked, 1)
                    dve.wait_ge(exp_done, 2 * HQ + 5 * h + 5)
                    dve.tensor_tensor(sc_c[:], sc_c[:], cmul, ALU.mult).then_inc(cmp_steps, 1)
                    dve.wait_ge(cmp_steps, 2 * h + 1)
                    dve.tensor_reduce(total[:, 4:6], sc_c[:], AX_X, ALU.add).then_inc(cmp_steps, 1)
                    dve.wait_ge(cmp_steps, 2 * h + 2)
                    dve.tensor_scalar(total[:, 0:6], total[:, 0:6], 1e-30, None, ALU.max).then_inc(coef_steps, 1)
                    dve.wait_ge(coef_steps, 3 * h + 1)
                    dve.reciprocal(inv[:, 0:6], total[:, 0:6]).then_inc(coef_steps, 1)
                    dve.wait_ge(coef_steps, 3 * h + 2)
                    head = r + 4 * g
                    for qt in range(TT):
                        for b in range(2):
                            dve.tensor_tensor(inv[:, 2 * qt + b:2 * qt + b + 1], inv[:, 2 * qt + b:2 * qt + b + 1],
                                              g_tok[:, qt, ds(head + (b + 1) * H2, 1)], ALU.mult)
                        ins = dve.tensor_tensor(inv[:, 4 + qt:5 + qt], inv[:, 4 + qt:5 + qt], g_tok[:, qt, ds(head, 1)], ALU.mult)
                    ins.then_inc(coef_steps, 1)
                    dve.wait_ge(coef_steps, 3 * h + 3)
                    for qt in range(TT):
                        for b in range(2):
                            cols = slice(b * S, (b + 1) * S)
                            ins = dve.tensor_scalar(probs[:, qt, cols], probs[:, qt, cols], inv[:, 2 * qt + b:2 * qt + b + 1],
                                                    None, ALU.mult)
                        ins.then_inc(p_ready, 1)
                    split(r, k + 2, 0)
                    for qt in range(TT):
                        ins = dve.tensor_scalar(pc[:, qt, 0:NC], sc_c[:, qt, :], inv[:, 4 + qt:5 + qt], None, ALU.mult)
                    ins.then_inc(p_ready, 1)
                    dve.wait_ge(t_done, 2 * HQ + 3 * h + 2)
                    dve.tensor_copy(probs_t[:, :, P:2 * P], ps_a[:, 3, :].rearrange("p (k q) -> p k q", k=4))\
                       .then_inc(ptd_ready, 1)
                    dve.wait_ge(t_done, 2 * HQ + 3 * h + 3)
                    dve.tensor_copy(q_cur[:, 1, :], ps_a[:, 0, 0:S]).then_inc(ptd_ready, 1)
                    dve.wait_ge(g2_copied, h + 1)
                    dve.wait_ge(oh_ready, HQ + h + 1)
                    rows = slice(g * DH, (g + 1) * DH)
                    dve.tensor_tensor(h_lo[rows, r, 0:S], ps_a[rows, 1, 0:S], h_hi[rows, r, 0:S].bitcast(F32), ALU.subtract)\
                       .then_inc(drained, 1)
                    split(r, k + 2, 1)

            def sigmoids(m, j):
                dve.wait_ge(g2_done, m + 1)
                return s1[:, j, 0:S], s1[:, j, S:NB]

            merge(FIRST["merge2"], 24, sigmoids)
            dve.wait_ge(x_scaled, 1)
            for i in range(4):
                split(0, FIRST["wout2"] + i + 2, 0)
                add_out(0, FIRST["wout2"] + i, 2 * i, S, None)
                split(0, FIRST["wout2"] + i + 2, 1)
            spread(4, 2)
            norm_lo(4, 4, S, plain(V_MLP), None)

            def relu2(pr, k, c, last):
                with dve.Fori(0, 2) as p:
                    for j in range(2):
                        split(pr + p, k + j + 2, 0)
                        for t in range(2):
                            dve.wait_ge(relu_done, c - 44 + 4 * p + (2 * j + t + 1))
                            dve.tensor_tensor(t1[:, t, 0:S], s1[:, t, 0:S], s1[:, t, 0:S], ALU.mult).then_inc(prod_done, 1)
                        for t in range(2):
                            m = 4 * p + (2 * j + t)
                            dve.wait_ge(hh_done, c + m + 1)
                            ins = dve.tensor_tensor(h_lo[:, m, 0:S], t1[:, t, 0:S], h_hi[:, m, 0:S].bitcast(F32), ALU.subtract)
                        ins.then_inc(drained, 1)
                        split(pr + p, k + j + 2, 1)
                for i in range(4):
                    more = not (last and i >= 2)
                    if more:
                        split(pr, k + 4 + i + 2, 0)
                    add_out(pr, k + 4 + i, 2 * i, S, None)
                    if more:
                        split(pr, k + 4 + i + 2, 1)

            with dve.Fori(0, SLABS2 - 1) as s:
                relu2(s * 4, FIRST["ff"], s * 8 + 44, False)
            relu2(0, FIRST["ff"] + 8 * (SLABS2 - 1), 44 + 8 * (SLABS2 - 1), True)
            spread(5, 2)
            dve.wait_ge(rb_done, 6)
            for kc in range(KD):
                dve.scalar_tensor_tensor(x[:, kc, 0:S], x[:, kc, 0:S], vcol(V_F2, kc), ps_a[:, 2, 0:S], ALU.mult, ALU.mult)\
                   .then_inc(x_normed, 1)

        @block.tensor
        def _(pe):
            def turn(dst, src, n=P):
                return pe.transpose(dst, src, ident[0:n, 0:n])

            def stat(n, tiles):
                pe.wait_ge(sq_ready, KD * (n + 1))
                if n:
                    pe.wait_ge(sq_sums, 5 * n)
                parts = (0, KD - 2, KD - 1) if n else range(KD)
                for t in range(tiles):
                    for kc in parts:
                        ins = pe.matmul(ps_a[:, 3, t:t + 1], sq[:, kc, t * P:(t + 1) * P], ones[:, 0:1],
                                        start=(kc == 0), stop=(kc == KD - 1))
                ins.then_inc(stat_done, 1)

            def spread(n, tiles):
                pe.wait_ge(diag_done, n + 1)
                pe.matmul(ps_a[:, 2, 0:tiles * P], ones[:], t1[:, 0, 0:tiles * P], start=True, stop=True).then_inc(rb_done, 1)

            def mod(pr, k, b, lag):
                pe.wait_ge(drained, 2 * pr + (k + 3 - lag))
                dst = ps_a[0:MOD_ROWS, b, 0:2 * P]
                for kc in range(KD):
                    if kc in (0, 4):
                        pe.wait_ge(l_ready, 4 * pr + (2 * k + 5 + kc // 4))
                    cols = slice(kc * 2 * P, (kc + 1) * 2 * P)
                    pe.matmul(dst, sc_pad[:, kc, :], w_hi[:, k % 2, cols], start=(kc == 0), stop=False)
                    ins = pe.matmul(dst, sc_pad[:, kc, :], w_lo[:, k % 2, cols], start=False, stop=(kc == KD - 1))
                    if kc in (3, KD - 1):
                        ins.then_inc(halves_done, 1)

            def unit(pr, k, operand, n=S, kcs=KD, ready=None, b=None, lag=2):
                pe.wait_ge(drained, 2 * pr + (k + 3 - lag))
                b = k % 2 if b is None else b
                for kc in range(kcs):
                    if kc in (0, 4):
                        pe.wait_ge(l_ready, 4 * pr + (2 * k + 5 + kc // 4))
                    if ready is not None:
                        ready(kc)
                    for t in range(2):
                        dst = ps_u[:, 2 * b + t, 0:n]
                        lo = kc * 2 * P + t * P
                        wh, wl = w_hi[:, k % 2, lo:lo + P], w_lo[:, k % 2, lo:lo + P]
                        xh, xl = operand(kc, t)
                        pe.matmul(dst, wh, xh, start=(kc == 0), stop=False)
                        pe.matmul(dst, wh, xl, start=False, stop=False)
                        ins = pe.matmul(dst, wl, xh, start=False, stop=(kc == kcs - 1))
                    if kc in (3, kcs - 1):
                        ins.then_inc(halves_done, 2 if kcs == 4 else 1)

            def from_x(n):
                return lambda kc, t: (x_hi[:, kc, 0:n], x_lo[:, kc, 0:n])

            def from_h(n):
                return lambda kc, t: (h_hi[:, kc, 0:n], h_lo[:, kc, 0:n])

            def both_h(kc, t):
                cols = slice(t * S, (t + 1) * S)
                return h_hi[:, kc, cols], h_lo[:, kc, cols]

            def normed(i):
                return lambda kc: pe.wait_ge(xl_ready, 8 * i + kc + 1)

            def drained_at(pr, k, per=1, step=1):
                return lambda kc: pe.wait_ge(drained, 2 * pr + (k + step * (kc // per) + 3))

            def swiglu(base, i, n):
                def slab(s, pr, k, chunks):
                    with pe.Fori(0, chunks // 2) as p:
                        for j in range(2):
                            unit(pr + p, k + j, from_x(n), n, ready=normed(i))
                    for o in range(4):
                        unit(pr, k + chunks + o, from_h(n), n, chunks, ready=drained_at(pr, k) if o == 0 else None)

                with pe.Fori(0, 2) as s:
                    slab(s, s * 6, base, SLABS[0])
                slab(2, 0, base + 24, SLABS[2])

            pe.drain().then_inc(halves_done, 4)
            pe.wait_ge(ones_ready, 1)
            pe.wait_ge(pad_ready, 3)
            with pe.Fori(0, MOD_FRONT // 4) as p:
                for j in range(4):
                    mod(2 * p, j, j % 2, 2)
            stat(0, 4)
            spread(0, 4)

            def slab1(pr, k, chunks):
                with pe.Fori(0, chunks // 2) as p:
                    for j in range(2):
                        unit(pr + 2 * p, k + 2 * j, from_x(NB), NB, ready=normed(0), b=j, lag=4 - j)
                        mod(pr + 2 * p, k + 2 * j + 1, j, 3)
                ko = k + 2 * chunks

                def before_taken(kc):
                    if kc == chunks - 1:
                        pe.wait_ge(drained, 2 * pr + (ko + 7))

                for i, o in enumerate((0, None, 1, None, 2, 3)):
                    if o is None:
                        mod(pr, ko + i, (i // 2) % 2, 3)
                    else:
                        unit(pr, ko + i, from_h(NB), NB, chunks, b=o % 2, lag=3 if o == 3 else 4,
                             ready={0: drained_at(pr, k, 1, 2), 3: before_taken}.get(o))

            k = FIRST["ffn1"]
            with pe.Fori(0, 2) as s:
                slab1(s * 11, k, SLABS[0])
            slab1(0, k + 44, SLABS[2])
            stat(1, 4)
            spread(1, 4)

            k = FIRST["k"]
            unit(0, k, from_x(NB), NB, ready=normed(1))
            unit(0, k + 1, from_x(NB), NB)
            pe.wait_ge(k_squared, 2)
            for t in range(HKV):
                for c in range(4):
                    at = 8 + 4 * t + c
                    ins = pe.matmul(ps_a[:, 1, at:at + 1], s1[:, t, c * P:(c + 1) * P], ones[:, 0:1], start=True, stop=True)
            ins.then_inc(kstat_done, 1)

            def turn_v(t):
                for c in range(4):
                    ins = turn(ps_a[:, 0, c * P:(c + 1) * P], v_feat[:, t, c * P:(c + 1) * P])
                ins.then_inc(v_turned, 1)

            kq = FIRST["q"]
            unit(0, kq, from_x(S))
            pe.wait_ge(drained, k + 4)
            turn_v(0)
            unit(0, kq + 1, from_x(S))
            pe.wait_ge(kdiag_done, 1)
            for t in range(HKV):
                pe.matmul(ps_a[:, 2 + t, :], ones[:], t1[:, t, :], start=True, stop=True).then_inc(krb_done, 1)
            unit(0, kq + 2, from_x(S))
            for t in range(HKV):
                pe.wait_ge(k_normed, t + 1)
                pe.matmul(ps_a[:, 2 + t, 0:S], swap1, k_all[:, t, 0:S], start=True, stop=True).then_inc(k_swapped, 1)
            pe.wait_ge(v_ready, 1)
            turn_v(1)
            unit(0, kq + 3, from_x(S))
            pe.wait_ge(q_squared, HQ)
            for h in range(HQ):
                for t in range(TT):
                    at = 16 + TT * h + t
                    ins = pe.matmul(ps_a[:, 1, at:at + 1], q_sq[:, h, t * P:(t + 1) * P], ones[:, 0:1], start=True, stop=True)
            ins.then_inc(qstat_done, 1)

            pe.wait_ge(k_ready, 2)
            with pe.Fori(0, 4) as p:
                for j in range(2):
                    kg = FIRST["gates"] + j
                    unit(p, kg, from_x(S))
                    if j == 0:
                        pe.wait_ge(drained, FIRST["gates"] + 2)
                    pe.matmul(ps_a[:, 2 + j, 0:S], swap1, q_rows[:, 2 * p + j, :], start=True, stop=True)\
                      .then_inc(q_swapped, 1)

            pe.wait_ge(q_scaled, 1)
            pe.wait_ge(v_ready, 2)
            for g in range(HKV):
                with pe.Fori(0, 2) as p:
                    for j in range(2):
                        kv = FIRST["conv"] + 4 * g + j
                        h = 2 * p + (4 * g + j)
                        pe.wait_ge(qcur_ready, h + 1)
                        for qt in range(TT):
                            ins = pe.matmul(ps_a[:, qt, :], q_cur[:, j, qt * P:(qt + 1) * P], k_all[:, g, :],
                                            start=True, stop=True)
                        ins.then_inc(qk_done, 1)
                        unit(p, kv, from_x(S))
                        pe.wait_ge(drained, 2 * p + (kv + 2))
                        for qt in range(TT):
                            pe.wait_ge(p_ready, 2 * h + (qt + 1))
                            for c in range(4):
                                ins = turn(ps_a[:, 2 + qt, c * P:(c + 1) * P], probs[:, qt, c * P:(c + 1) * P])
                            ins.then_inc(t_done, 1)
                        pe.wait_ge(pta_ready, h + 1)
                        pe.wait_ge(ptd_ready, h + 1)
                        for c in range(4):
                            ins = pe.matmul(ps_a[:, 2, 0:S], v_tok[:, c, g, :], probs_t[:, c, :], start=(c == 0), stop=(c == 3))
                        ins.then_inc(pv_done, 1)
            with pe.Fori(0, 2) as p:
                for j in range(2):
                    unit(p, FIRST["bg"] + j, from_x(S))
            with pe.Fori(0, 4) as p:
                for j in range(2):
                    unit(p, FIRST["merge"] + j, both_h, ready=drained_at(0, FIRST["bg"], 2))
            with pe.Fori(0, 2) as p:
                for j in range(2):
                    unit(p, FIRST["wout"] + j, from_x(S), ready=drained_at(0, FIRST["merge"]))

            stat(2, 2)
            spread(2, 2)
            swiglu(FIRST["ffn2"], 2, S)
            stat(3, 4)
            spread(3, 4)

            k = FIRST["kcvc"]
            for i in range(7):
                unit(0, k + i, from_x(S), ready=normed(3) if i == 0 else None)
            pe.wait_ge(wg_ready, 1)
            for t in range(TT):
                dst = ps_a[:, 1, t * 3 * H2:(t + 1) * 3 * H2]
                tok = slice(t * P, (t + 1) * P)
                for kc in range(KD):
                    pe.matmul(dst, x_hi[:, kc, tok], wg_hi[:, kc, :], start=(kc == 0), stop=False)
                    pe.matmul(dst, x_hi[:, kc, tok], wg_lo[:, kc, :], start=False, stop=False)
                    ins = pe.matmul(dst, x_lo[:, kc, tok], wg_hi[:, kc, :], start=False, stop=(kc == KD - 1))
            ins.then_inc(gt_done, 1)
            for i in range(2):
                pe.wait_ge(cmp_ready, 1)
                pe.wait_ge(drained, k + 3)
                if i:
                    pe.wait_ge(gelu_done, 1)
                for c in range(2):
                    pe.wait_ge(cmp_landed[c], 16 * (i + 1))
                for half in range(2):
                    dst = ps_a[:, 0, i * 64 + half * G2 * NC:i * 64 + (half + 1) * G2 * NC]
                    for l in range(CS):
                        lo = (l % 8) * CH + half * P
                        ins = pe.matmul(dst, wide_scr[:, l // 8, lo:lo + P], cmp_in[i][:, l, :, :].rearrange("p g c -> p (g c)"),
                                        start=(l == 0), stop=(l == CS - 1))
                        if half == 1 and l == 7:
                            ins.then_inc(cmp_w_used, 1)
                ins.then_inc(cmp_w_used, 1)
                pe.matmul(ps_a[:, 0, 480:481], ones[:], ones[:, 0:1], start=True, stop=True).then_inc(hid_done, 1)
            pe.wait_ge(late, 16)
            for i in range(4):
                pe.wait_ge(pooled_ready, i + 1)
                if i:
                    pe.wait_ge(ph_done, 2 * i - 1)
                pe.matmul(ps_a[:, 3, 0:S], w_pool[:, i, :], pooled[:, i, :], start=True, stop=True)\
                  .then_inc(mixed_done, 1)
            pe.wait_ge(drained, k + 7)
            pe.wait_ge(ph_done, 7)
            for b in range(2):
                pe.matmul(ps_a[:, 2 + b, 0:S], swap2, kk2[:, b * S:(b + 1) * S], start=True, stop=True)\
                  .then_inc(rope2_swapped, 1)
            pe.wait_ge(kv2_copied, 2)
            for r in range(4):
                pe.wait_ge(rope2_done, r + 1)
                pe.matmul(ps_a[:, 2 + r % 2, 0:S], swap2, q2[:, r, :], start=True, stop=True)\
                  .then_inc(rope2_swapped, 1)
            pe.wait_ge(gelu_done, 2)
            for g in range(G2):
                for half in range(2):
                    ins = pe.matmul(ps_a[g * DH:(g + 1) * DH, 0, 128:128 + NC], w2c[:, 0, half, :],
                                    hid[:, 0, half, g * NC:(g + 1) * NC], start=(half == 0), stop=(half == 1))
            ins.then_inc(cmp_done, 1)
            for g in range(G2):
                for half in range(2):
                    ins = pe.matmul(ps_a[0:NC, 0, 256 + g * DH:256 + (g + 1) * DH], hid[:, 1, half, g * NC:(g + 1) * NC],
                                    w2c[:, 1, half, :], start=(half == 0), stop=(half == 1))
            ins.then_inc(cmp_done, 1)
            pe.wait_ge(kc_raw, 1)
            pe.wait_ge(rope2_done, 6)
            pe.matmul(ps_a[:, 2, 0:NC], swap2, kc_r[:, 0, :], start=True, stop=True).then_inc(rope2_swapped, 1)
            for b in range(2):
                for c in range(2):
                    ins = turn(ps_a[:, 3, (2 * b + c) * P:(2 * b + c + 1) * P], v2_feat[:, b, c * P:(c + 1) * P])
            ins.then_inc(v2_turned, 1)
            pe.wait_ge(kc_raw, 3)
            pe.wait_ge(rope2_done, 7)

            pe.wait_ge(gt_ready, 1)
            with pe.Fori(0, 4) as r:
                pe.wait_ge(qcur_ready, HQ + r + 1)
                for g in range(G2):
                    kg = FIRST["gates2"] + g
                    h = 2 * r + g
                    rows = slice(g * DH, (g + 1) * DH)
                    for qt in range(TT):
                        q = q_cur[rows, 0, qt * P:(qt + 1) * P]
                        pe.matmul(ps_a[:, qt, :], q, kk2[rows, :], start=True, stop=True)
                        ins = pe.matmul(ps_a[:, 2, qt * 16:qt * 16 + NC], q, kc_r[rows, 1, :], start=True, stop=True)
                    ins.then_inc(qk_done, 1)
                    unit(r, kg, from_x(S))
                    for qt in range(TT):
                        pe.wait_ge(p_ready, 2 * HQ + 3 * h + (qt + 1))
                        for c in range(4):
                            ins = turn(ps_a[:, 2 + qt, c * P:(c + 1) * P], probs[:, qt, c * P:(c + 1) * P])
                        ins.then_inc(t_done, 1)
                    pe.wait_ge(p_ready, 2 * HQ + 3 * h + 3)
                    for qt in range(TT):
                        ins = turn(ps_a[:, 0, qt * P:(qt + 1) * P], pc[:, qt, :])
                    ins.then_inc(t_done, 1)
                    pe.wait_ge(pta_ready, HQ + h + 1)
                    pe.wait_ge(ptd_ready, HQ + 2 * h + 2)
                    dst = ps_a[rows, 1, 0:S]
                    for c in range(4):
                        pe.matmul(dst, v2_tok[:, c // 2, c % 2, rows], probs_t[:, c, :], start=(c == 0), stop=False)
                    pe.matmul(dst, vc_tok[:, g, :], q_cur[:, 1, :], start=False, stop=True).then_inc(pv_done, 1)
                    pe.wait_ge(drained, 2 * r + (kg + 3))
            pe.wait_ge(pl_done, 4)

            def rows_done(kc):
                pe.wait_ge(drained, FIRST["gates2"] + 2 * kc + 4)

            with pe.Fori(0, 4) as p:
                for j in range(2):
                    unit(p, FIRST["merge2"] + j, both_h, kcs=4, ready=rows_done)
            with pe.Fori(0, 2) as p:
                for j in range(2):
                    unit(p, FIRST["wout2"] + j, from_x(S), ready=drained_at(0, FIRST["merge2"]))
            stat(4, 2)
            spread(4, 2)
            with pe.Fori(0, SLABS2) as s:
                with pe.Fori(0, 2) as p:
                    for j in range(2):
                        unit(s * 4 + p, FIRST["ff"] + j, from_x(S), ready=normed(4))
                with pe.Fori(0, 2) as p:
                    for j in range(2):
                        unit(s * 4 + p, FIRST["ff"] + 4 + j, from_h(S), ready=drained_at(s * 4, FIRST["ff"], 2))
            stat(5, 2)
            spread(5, 2)


def constants():
    import numpy as np
    f = np.float32
    t = np.zeros((P, K_END), f)
    t[:, K_ID:K_ID + P] = np.eye(P, dtype=f)
    n = HD // 4
    for ax in range(2):
        for i in range(n):
            lo, hi = ax * 2 * n + i, ax * 2 * n + n + i
            t[hi, K_R1 + lo] = -1.0
            t[lo, K_R1 + hi] = 1.0
    inv = (f(10000.0) ** (-np.arange(n, dtype=f) / f(n))).astype(f)
    tok = np.arange(S)
    for ax, pos in enumerate((tok // 64, tok % 64)):
        ang = (pos.astype(f)[:, None] * inv).astype(f).T
        for half in range(2):
            rows = slice(ax * 2 * n + half * n, ax * 2 * n + (half + 1) * n)
            t[rows, K_C1:K_C1 + S] = np.cos(ang)
            t[rows, K_S1:K_S1 + S] = np.sin(ang)
    rot = DH // 4
    inv = (f(500000.0) ** (-np.arange(0, rot, 2, dtype=f) / f(rot))).astype(f)
    ang = (tok.astype(f)[:, None] * inv).astype(f).T
    t[:, K_C2:K_C2 + S] = 1.0
    for g in range(G2):
        for i in range(rot // 2):
            lo, hi = g * DH + i, g * DH + rot // 2 + i
            t[hi, K_R2 + lo] = -1.0
            t[lo, K_R2 + hi] = 1.0
            for row in (lo, hi):
                t[row, K_C2:K_C2 + S] = np.cos(ang[i])
                t[row, K_S2:K_S2 + S] = np.sin(ang[i])
    last = np.arange(NC) * CS + CB - 1
    for qt in range(TT):
        q = qt * P + np.arange(P)
        t[:, K_MASK + qt * S:K_MASK + (qt + 1) * S] = np.where(tok[None, :] <= q[:, None], 0.0, -1e30)
        seen = last[None, :] <= q[:, None]
        t[:, K_CADD + qt * NC:K_CADD + (qt + 1) * NC] = np.where(seen, 0.0, -1e30)
        t[:, K_CMUL + qt * NC:K_CMUL + (qt + 1) * NC] = seen
    for i, w in enumerate(POOLS):
        t[:, K_CNT + i * PAD:K_CNT + (i + 1) * PAD] = f(1.0) / np.minimum(np.arange(PAD) + 1, w).astype(f)
    t[:, K_EPS] = EPS
    return t


def lay_out(i):
    import numpy as np
    f = np.float32

    def rows(w, kc0=0, kcs=KD):
        return np.asarray(w)[kc0 * P:(kc0 + kcs) * P].reshape(kcs, P, -1).transpose(1, 0, 2)

    def feature_major(v):
        return np.asarray(v, f).reshape(-1, P).T

    stream = np.zeros((UNITS, P, SLOT), f)
    unit = iter(range(UNITS))

    def put(tile0, tile1):
        u = np.concatenate([tile0, tile1], axis=2)
        stream[next(unit), :, :u.shape[1] * 2 * P] = u.reshape(P, -1)

    def wide(w, col, kc0=0, kcs=KD):
        tiles = rows(w, kc0, kcs)[:, :, col:col + 2 * P]
        put(tiles[:, :, :P], tiles[:, :, P:])

    def pair(w0, col0, w1, col1):
        put(rows(w0)[:, :, col0:col0 + P], rows(w1)[:, :, col1:col1 + P])

    def swiglu(w_in, w_out, ride):
        m = MOD_FRONT
        for s, chunks in enumerate(SLABS):
            for c in range(chunks):
                col = (8 * s + c) * P
                pair(w_in, col, w_in, col + D_FF)
                if ride:
                    wide(w_mod, m * 2 * P)
                    m += 1
            for o in range(4):
                wide(w_out, o * 2 * P, 8 * s, chunks)
                if ride and o < 2:
                    wide(w_mod, m * 2 * P)
                    m += 1

    w_mod, w_in, w_in2 = i["w_mod"][0], i["w_in"][0], i["w_in_2"][0]
    for m in range(MOD_FRONT):
        wide(w_mod, m * 2 * P)
    swiglu(i["ffn1_w_in"][0], i["ffn1_w_out"][0], True)
    for col in (C_K, C_V, *range(C_Q, C_K, 2 * P)):
        wide(w_in, col)
    for m in range(KD):
        pair(w_in, C_GATE + m * P, w_in, C_GATE + D + m * P)
    for m in range(KD):
        pair(w_in, C_CG + m * P, w_in, C_VC + m * P)
    for col in range(C_BG, C_CG, 2 * P):
        wide(w_in, col)
    for m in range(KD):
        pair(i["w_branch_conv"][0], m * P, i["w_branch_attn"][0], m * P)
    for col in range(0, D, 2 * P):
        wide(i["w_out"][0], col)
    swiglu(i["ffn2_w_in"][0], i["ffn2_w_out"][0], False)
    for col in (C2_KC, C2_KS, C2_KW, 0, 2 * P, C2_POOL, C2_POOL + 2 * P):
        wide(w_in2, col)
    for m in range(KD):
        pair(w_in2, C2_MERGE + m * P, w_in2, C2_MERGE + D + m * P)
    w_ba2 = np.asarray(i["w_branch_attn_2"][0]).reshape(G2, R2H, DH, D).transpose(0, 2, 1, 3).reshape(P, R2H, D)
    w_bp2 = rows(i["w_branch_pool_2"][0], 0, 4)
    for m in range(KD):
        put(w_ba2[:, :, m * P:(m + 1) * P], w_bp2[:, :, m * P:(m + 1) * P])
    for col in range(0, D, 2 * P):
        wide(i["w_out_2"][0], col)
    for s in range(SLABS2):
        for o in range(4):
            wide(i["w_ff1_2"][0], s * 8 * P + o * 2 * P)
        for o in range(4):
            wide(i["w_ff2_2"][0], o * 2 * P, 8 * s)

    cmp_w = np.concatenate([np.asarray(i[name][0]).reshape(2, 2, CS // 2, DH, CH).transpose(1, 0, 3, 2, 4).reshape(2, P, SLOT)
                            for name in ("cmp_k_w1_2", "cmp_v_w1_2")])
    pe = np.concatenate([np.tile(np.asarray(i[name][0]).T, (2, 1)) for name in ("cmp_pe_k_2", "cmp_pe_v_2")], axis=1)
    vectors = np.concatenate([feature_major(i[name]) for name in (
        "c", "c_ctx", "norm1_g", "norm2_g", "norm3_g", "final_g", "norm_mix_2", "norm_mlp_2", "norm_final_2", "conv_w",
        "pool_scale_2", "q_norm_g", "k_norm_g", "b_mod")] + [pe], axis=1)
    late = np.concatenate(
        [rows(w_in2)[:, :, C2_GATE:C2_POOL].reshape(P, -1),
         np.asarray(i["pool_w_2"][0]).transpose(1, 0, 2).reshape(P, -1)]
        + [np.asarray(i[name][0]).reshape(2, P, DH).transpose(1, 0, 2).reshape(P, -1) for name in ("cmp_k_w2_2", "cmp_v_w2_2")],
        axis=1)
    tokens = np.concatenate([np.asarray(i["x"][0]), np.asarray(i["ctx"][0])]).T.reshape(KD, P, NB).transpose(1, 0, 2)
    return {"stream": stream, "cmp_w": cmp_w, "vectors": vectors, "late": late, "tokens": tokens, "consts": constants()}


def kernel(**inputs):
    import numpy as np
    import concourse.bacc as bacc
    from concourse.bass_utils import run_bass_kernel_spmd as run

    nc = bacc.Bacc("TRN2", target_bir_lowering=False, num_devices=1)
    arrays = {f"in_{name}": np.ascontiguousarray(arr) for name, arr in lay_out(inputs).items()}
    args = {name[3:]: nc.dram_tensor(name, arr.shape, mybir.dt.from_np(arr.dtype), kind="ExternalInput").ap()
            for name, arr in arrays.items()}
    out = nc.dram_tensor("out", (P, KD, S), F32, kind="ExternalOutput").ap()
    program(nc, args, out)
    r = run(nc, [arrays], core_ids=[0])
    return r.results[0]["out"].transpose(2, 1, 0).reshape(1, S, D)
```

```python
from contextlib import ExitStack

import concourse.bass as bass
from concourse import mybir

F32 = mybir.dt.float32
F32R = mybir.dt.float32r
ACT = mybir.ActivationFunctionType
ALU = mybir.AluOpType
AX_X = mybir.AxisListType.X
ds = bass.ds

P = 128
D = 1024
KD = D // P
S = 256
CTX = 256
NB = S + CTX
TT = S // P
EPS = 1e-6

D_FF = 2816
SLABS = (8, 8, 6)
HQ, HKV, HD = 8, 2, 128
GROUP = HQ // HKV
C_BG, C_CG, C_VC = 0, D, 2 * D
C_Q = 3 * D
C_K = C_Q + HQ * HD
C_V = C_K + HKV * HD
C_GATE = C_V + HKV * HD
N_MOD = 9
MOD_TILES = N_MOD * KD
MOD_UNITS = MOD_TILES // 2
MOD_FRONT = 8
MOD_RIDE = 10
MOD_ROWS = 32

H2, G2, R2H, DH = 8, 2, 4, 64
C2_KC = H2 * DH
C2_KS = C2_KC + 2 * G2 * DH
C2_KW = C2_KS + 2 * G2 * DH
C2_GATE = C2_KC + 6 * G2 * DH
C2_POOL = C2_GATE + 3 * H2
C2_MERGE = C2_POOL + 512
CB, CS = 32, 16
NC = (S - CB) // CS + 1
CH = 4 * DH
POOLS = (2, 4, 8, 16)
PAD = max(POOLS)
D_FF2 = 4 * D
SLABS2 = D_FF2 // (8 * P)

K_ID, K_EPS, K_R1, K_R2 = 0, P, P + 1, 2 * P + 1
K_C1, K_S1, K_C2, K_S2 = (3 * P + 1 + i * S for i in range(4))
K_MASK = 3 * P + 1 + 4 * S
K_CADD = K_MASK + P
K_CMUL = K_CADD + TT * NC
K_CNT = K_CMUL + TT * NC
K_END = K_CNT + len(POOLS) * PAD

V_C, V_N1, V_N2, V_N3, V_F1, V_MIX, V_MLP, V_F2 = 0, *(KD * i for i in range(2, 9))
V_CONV = 9 * KD
V_PS = V_CONV + 3 * KD
V_QG = V_PS + 4
V_KG = V_QG + 1
V_BM = V_KG + 1
V_PE = V_BM + MOD_TILES
V_END = V_PE + 2 * CB

L_WG = 0
L_POOL = KD * 3 * H2
L_W2 = L_POOL + len(POOLS) * P
L_END = L_W2 + 2 * 2 * DH

STAGES = (("front", MOD_FRONT), ("ffn1", 62), ("k", 1), ("v", 1), ("q", 4), ("gates", 8), ("conv", 8), ("bg", 4), ("merge", 8),
          ("wout", 4), ("ffn2", 34), ("kcvc", 1), ("ksvs", 1), ("kwvw", 1), ("q2", 2), ("pool", 2),
          ("gates2", 8), ("merge2", 4), ("wout2", 4), ("ff", 32))
FIRST = {}
_n = 0
for _name, _units in STAGES:
    FIRST[_name] = _n
    _n += _units
UNITS = _n
SLOT = KD * 2 * P
HALF = SLOT // 2
LANDED = 16


def program(nc, a, out):
    with ExitStack() as ctx:
        def sb(name, shape, dt=F32):
            return ctx.enter_context(nc.sbuf_tensor(name, shape, dt))

        def sem(name):
            return ctx.enter_context(nc.semaphore(name))

        raw = sb("raw", [P, 2, SLOT])
        w_hi = sb("w_hi", [P, 2, SLOT], F32R)
        w_lo = sb("w_lo", [P, 2, SLOT], F32R)
        wide_scr = sb("wide_scr", [P, 2, SLOT])
        x = sb("x", [P, KD, NB])
        x_hi = sb("x_hi", [P, KD, NB], F32R)
        x_lo = sb("x_lo", [P, KD, NB], F32R)
        h_hi = sb("h_hi", [P, KD, NB], F32R)
        h_lo = sb("h_lo", [P, KD, NB], F32R)
        sq = sb("sq", [P, KD, NB])
        s1 = sb("s1", [P, 2, NB])
        t1 = sb("t1", [P, 2, NB])
        scr = sb("scr", [P, 4 * D])
        cst = sb("cst", [P, K_END])
        ones = sb("ones", [P, P])
        vec = sb("vec", [P, V_END])
        late_w = sb("late_w", [P, L_END])
        gg = sb("gg", [P, KD])
        sc = sb("sc", [P, KD, 2])
        sc_pad = sb("sc_pad", [P, KD, MOD_ROWS], F32R)
        mods = sb("mods", [P, MOD_TILES, 2])
        am = sb("am", [P, 3, KD, 2])
        gate_half = sb("gate_half", [P, 2, KD, 2])
        var = sb("var", [P, 2 * TT])
        root = sb("root", [P, 32])
        rstd = sb("rstd", [P, 32])
        q_scale = sb("q_scale", [P, HQ * TT])
        q_cur = sb("q_cur", [P, 2, S])
        u_pad = sb("u_pad", [P, S + 2])
        top = sb("top", [P, 4])
        neg_top = sb("neg_top", [P, TT])
        total = sb("total", [P, TT])
        inv = sb("inv", [P, TT])
        neg_top2 = sb("neg_top2", [P, TT, 3])
        total2 = sb("total2", [P, TT, 3])
        inv2 = sb("inv2", [P, TT, 3])
        p_pad = sb("p_pad", [P, PAD + S])
        wg_hi = sb("wg_hi", [P, KD, 3 * H2], F32R)
        wg_lo = sb("wg_lo", [P, KD, 3 * H2], F32R)
        g_tok = sb("g_tok", [P, TT, 3 * H2])
        hid = sb("hid", [P, 2, 2, G2 * NC])
        kc_r = sb("kc_r", [P, 2, NC])
        vc_tok = sb("vc_tok", [P, G2, DH])
        pc = sb("pc", [P, TT, P])
        sc_c = sb("sc_c", [P, TT, NC])
        tick = sb("tick", [P, 1])
        table = sb("table", [P, 1])

        ps_u = ctx.enter_context(nc.psum_tensor("ps_u", [P, 4, 512], F32))
        ps_a = ctx.enter_context(nc.psum_tensor("ps_a", [P, 4, 512], F32))

        sq_flat = sq[:].rearrange("p k n -> p (k n)")
        bm = vec[:, V_BM:V_BM + MOD_TILES]
        pec = vec[:, V_PE:V_END]
        wg = late_w[:, L_WG:L_POOL].rearrange("p (k m) -> p k m", k=KD)
        w_pool = late_w[:, L_POOL:L_W2].rearrange("p (i n) -> p i n", i=4)
        w2c = late_w[:, L_W2:L_END].rearrange("p (i h d) -> p i h d", i=2, h=2)
        turned = scr[:, 0:4 * MOD_ROWS].rearrange("p (b t c) -> p b t c", b=2, t=2)
        mod_sum = scr[:, P:P + 2 * MOD_TILES].rearrange("p (t s) -> p t s", s=2)
        bm_half = scr[:, 3 * P:3 * P + MOD_TILES]
        probs = scr[:, 0:2 * NB].rearrange("p (t n) -> p t n", t=2)
        probs_t = scr[:, 2 * NB:4 * NB].rearrange("p (k n) -> p k n", k=4)
        q_sq = scr[:, 4 * NB:8 * NB].rearrange("p (h n) -> p h n", h=HQ)
        q_rows = x[:, :, S:NB]
        k_all = sq[:, 0:2, :]
        v_feat = sq[:, 2:4, :]
        v_tok = sq_flat[:, 4 * NB:6 * NB].rearrange("p (k g d) -> p k g d", k=4, g=HKV)
        y_conv = scr[:, 4 * NB:8 * NB].rearrange("p (m n) -> p m n", m=KD)
        g_conv = wide_scr[:, 0, :].rearrange("p (m n) -> p m n", m=KD)
        g_attn = wide_scr[:, 1, :].rearrange("p (m n) -> p m n", m=KD)
        mixed = scr[:, 0:2 * NB].rearrange("p (i n) -> p i n", i=4)
        pooled = x[:, 4:8, S:NB]
        probs_lo = scr[:, 0:2 * P].rearrange("p (b n) -> p b n", b=2)
        probs_hi = scr[:, 2 * P:6 * P].rearrange("p (b n) -> p b n", b=2)
        kk2 = scr[:, 4 * NB:5 * NB]
        v2_feat = scr[:, 5 * NB:6 * NB].rearrange("p (b n) -> p b n", b=2)
        v2_tok = scr[:, 6 * NB:7 * NB].rearrange("p (b k n) -> p b k n", b=2, k=2)
        cmp_k = scr[:, 7 * NB:7 * NB + CS * G2 * NC].rearrange("p (l g c) -> p l g c", l=CS, g=G2)
        cmp_v = s1[:, 0, 0:CS * G2 * NC].rearrange("p (l g c) -> p l g c", l=CS, g=G2)
        cmp_in = (cmp_k, cmp_v)
        g_feat = s1[0:3 * H2, 1, 0:S]
        hid_rows = q_cur[0:G2 * NC, :, :]
        cmp_w = (wide_scr[:], sq[:].rearrange("p (c k) n -> p c (k n)", c=2))
        q2 = x[:, 0:4, S:NB]
        gates2 = sq[:].rearrange("p m (a n) -> p m a n", a=2)
        ident = cst[:, K_ID:K_ID + P]
        swap1 = cst[:, K_R1:K_R1 + P]
        swap2 = cst[:, K_R2:K_R2 + P]
        cos1, sin1, cos2, sin2 = (cst[:, k:k + S] for k in (K_C1, K_S1, K_C2, K_S2))
        cadd = cst[:, K_CADD:K_CADD + TT * NC].rearrange("p (t c) -> p t c", t=TT)
        cmul = cst[:, K_CMUL:K_CMUL + TT * NC].rearrange("p (t c) -> p t c", t=TT)
        eps = cst[:, K_EPS:K_EPS + 1]

        def vcol(v, m):
            return vec[:, v + m:v + m + 1] if isinstance(m, int) else vec[:, ds(m + v, 1)]

        def segs(n):
            return [(0, slice(0, S))] if n == S else [(0, slice(0, S)), (1, slice(S, NB))]

        vec_landed = sem("vectors_landed")
        x_landed = [sem("tokens_landed0"), sem("tokens_landed1")]
        ident_landed = sem("identity_landed")
        cst_landed = sem("constants_landed")
        late = sem("late_landed")
        raw_landed = [sem("raw_landed0"), sem("raw_landed1")]
        front_landed = [sem("front_landed0"), sem("front_landed1")]
        cmp_landed = [sem("cmp_k_w_landed"), sem("cmp_v_w_landed")]
        h_ready = sem("w_hi_ready")
        l_ready = sem("w_lo_ready")
        halves_done = sem("halves_done")
        drained = sem("unit_drained")
        mod_turned = sem("mod_turned")
        ones_ready = sem("ones_ready")
        vec_ready = sem("vec_ready")
        pad_ready = sem("silu_pad_ready")
        sc_ready = sem("silu_c_ready")
        sq_ready = sem("squares_ready")
        sq_sums = sem("squares_summed")
        var_steps = sem("var_steps")
        stat_done = sem("stat_done")
        root_done = sem("root_done")
        recip_done = sem("recip_done")
        diag_done = sem("diag_done")
        rb_done = sem("rstd_spread")
        z_ready = sem("z_ready")
        xh_ready = sem("x_hi_ready")
        xl_ready = sem("x_lo_ready")
        x_scaled = sem("x_scaled")
        x_normed = sem("x_normed")
        mods_ready = sem("mods_ready")
        gate_ready = sem("gate_ready")
        silu_done = sem("silu_done")
        prod_done = sem("prod_done")
        hh_done = sem("h_hi_done")
        k_squared = sem("k_squared")
        k_gained = sem("k_gained")
        kstat_done = sem("kstat_done")
        kroot_done = sem("kroot_done")
        krecip_done = sem("krecip_done")
        kdiag_done = sem("kdiag_done")
        krb_done = sem("k_rstd_spread")
        k_normed = sem("k_normed")
        k_swapped = sem("k_swapped")
        k_terms = sem("k_rope_terms")
        k_ready = sem("k_ready")
        v_turned = sem("v_turned")
        v_ready = sem("v_ready")
        q_squared = sem("q_squared")
        qstat_done = sem("qstat_done")
        qroot_done = sem("qroot_done")
        qrecip_done = sem("qrecip_done")
        q_scaled = sem("q_scale_ready")
        q_swapped = sem("q_swapped")
        q_terms = sem("q_rope_terms")
        gates_done = sem("gates_done")
        qcur_ready = sem("q_cur_ready")
        qk_done = sem("qk_done")
        top_done = sem("top_done")
        nb_ready = sem("neg_top_ready")
        exp_done = sem("exp_done")
        inv_done = sem("inv_done")
        p_ready = sem("probs_ready")
        t_done = sem("probs_turned")
        pta_ready = sem("probs_t_act_ready")
        ptd_ready = sem("probs_t_dve_ready")
        pv_done = sem("pv_done")
        oh_ready = sem("o_hi_ready")
        o1_done = sem("o1_done")
        cg_copied = sem("cg_copied")
        u_ready = sem("conv_in_ready")
        conv_terms = sem("conv_terms")
        y_done = sem("y_done")
        yh_done = sem("y_hi_done")
        merge_terms = sem("merge_terms")
        zh_done = sem("z_hi_done")
        wg_done = sem("gate_w_hi_done")
        wg_ready = sem("gate_w_ready")
        gt_done = sem("gate_logits_done")
        gt_sig = sem("gate_sigmoid_done")
        gt_turned = sem("gate_tok_turned")
        gt_ready = sem("gate_tok_ready")
        hid_turned = sem("cmp_hidden_turned")
        hid_copied = sem("cmp_hidden_copied")
        cmp_ready = sem("cmp_in_ready")
        hid_done = sem("cmp_hidden_done")
        gelu_done = sem("cmp_gelu_done")
        cmp_done = sem("cmp_out_done")
        kc_raw = sem("k_cmp_raw")
        kv2_copied = sem("kv2_copied")
        rope2_swapped = sem("rope2_swapped")
        rope2_terms = sem("rope2_terms")
        rope2_done = sem("rope2_done")
        v2_turned = sem("v2_turned")
        v2_ready = sem("v2_ready")
        pool_copied = sem("pool_copied")
        o2_done = sem("o2_done")
        pool_steps = sem("pool_steps")
        pooled_ready = sem("pooled_ready")
        mixed_done = sem("pool_mixed")
        ph_done = sem("pool_hi_done")
        pl_done = sem("pool_lo_done")
        g2_copied = sem("gates2_copied")
        g2_done = sem("gates2_done")
        masked = sem("scores_masked")
        cmp_masked = sem("cmp_masked")
        cmp_steps = sem("cmp_softmax_steps")
        coef_steps = sem("coef_steps")
        relu_done = sem("relu_done")
        stored = sem("stored")

        def landed_in(k):
            return wide_scr if k < MOD_FRONT and k // 2 % 2 else raw

        block = ctx.enter_context(nc.Block())


        @block.sync
        def _(sp):
            def load(pr, k, kcs):
                sp.wait_ge(l_ready, 4 * pr + (2 * k + 2))
                cols = slice(0, kcs * 2 * P)
                sp.dma_start(raw[:, k % 2, cols], a["stream"][2 * pr + k, :, cols]).then_inc(raw_landed[k % 2], LANDED)

            def units(first, count, kcs=KD):
                with sp.Fori(0, count // 2) as p:
                    for j in range(2):
                        load(p, first + j, kcs)
                if count % 2:
                    load(0, first + count - 1, kcs)

            def run(first, end):
                units(first, end - first)

            for u in range(MOD_FRONT):
                if u >= 4:
                    sp.wait_ge(l_ready, 2 * u - 2)
                dst, landed = ((raw, raw_landed), (wide_scr, front_landed))[u // 2 % 2]
                sp.dma_start(dst[:, u % 2, :], a["stream"][u]).then_inc(landed[u % 2], LANDED)

            last_out = FIRST["k"] - 6
            run(MOD_FRONT, last_out)
            for o in range(6):
                load(0, last_out + o, KD if o in (1, 3) else SLABS[2])
            run(FIRST["k"], FIRST["ffn2"])

            def cmp_weights(i):
                for c in range(2):
                    ins = sp.dma_start(cmp_w[i][:, c, :], a["cmp_w"][2 * i + c])
                    ins.then_inc(cmp_landed[i], 16)

            run(FIRST["ffn2"], FIRST["ffn2"] + 4)
            sp.wait_ge(drained, FIRST["wout"] + 2)
            cmp_weights(0)
            run(FIRST["ffn2"] + 4, FIRST["kcvc"] - 4)
            units(FIRST["kcvc"] - 4, 4, SLABS[2])
            run(FIRST["kcvc"], FIRST["kcvc"] + 4)
            sp.wait_ge(xl_ready, 4 * KD)
            cmp_weights(1)
            run(FIRST["kcvc"] + 4, UNITS)

            for i in range(4):
                chunks = slice(2 * i, 2 * i + 2)
                sp.wait_ge(x_normed, 2 * i + 2)
                sp.dma_start(out[:, chunks, :], x[:, chunks, 0:S]).then_inc(stored, 16)
            sp.wait_ge(stored, 16 * 4)

        @block.gpsimd
        def _(pool):
            def sums(n, width):
                for kc in range(1, KD - 2):
                    pool.wait_ge(sq_ready, KD * n + kc + 1)
                    if kc > 1:
                        pool.wait_ge(sq_sums, 5 * n + kc - 1)
                    pool.tensor_tensor(sq[:, 0, 0:width], sq[:, 0, 0:width], sq[:, kc, 0:width], ALU.add).then_inc(sq_sums, 1)

            sums(0, NB)
            sums(1, NB)
            for g in range(HKV):
                with pool.Fori(0, 2) as p:
                    for j in range(2):
                        k = FIRST["conv"] + 4 * g + j
                        if g == 0 and j == 0:
                            pool.wait_ge(drained, FIRST["conv"] + 2)
                        pool.wait_ge(halves_done, 4 * p + 2 * k + 2)
                        pool.tensor_copy(q_cur[:, j, :], q_rows[:, 2 * p + (4 * g + j), :]).then_inc(qcur_ready, 1)
            sums(2, S)
            sums(3, NB)
            def pool_group(i):
                w = POOLS[i]
                first = 7 * i
                pool.wait_ge(pool_copied, i // 2 + 1)
                if i:
                    pool.wait_ge(pooled_ready, i)
                pool.tensor_copy(p_pad[:, PAD:PAD + S], pooled[:, i, :]).then_inc(pool_steps, 1)
                pool.wait_ge(pool_steps, first + 1)
                width, step = 1, 0
                bufs = (s1[:, 0, :], s1[:, 1, :])
                while width < w:
                    dst, lo = bufs[step % 2], 2 * width - 1
                    prev = p_pad if step == 0 else bufs[(step - 1) % 2]
                    ins = pool.tensor_tensor(dst[:, lo:PAD + S], prev[:, lo:PAD + S], prev[:, lo - width:PAD + S - width], ALU.add)
                    step += 1
                    ins.then_inc(pool_steps, 1)
                    pool.wait_ge(pool_steps, first + 1 + step)
                    width *= 2
                sums_w, res = bufs[(step - 1) % 2], bufs[step % 2]
                cnt = cst[:, K_CNT + i * PAD:K_CNT + (i + 1) * PAD]
                pool.tensor_tensor(res[:, 0:PAD], sums_w[:, PAD:2 * PAD], cnt, ALU.mult)
                pool.tensor_scalar(res[:, PAD:S], sums_w[:, 2 * PAD:PAD + S], 1.0 / w, None, ALU.mult)\
                    .then_inc(pool_steps, 6 - step)
                pool.wait_ge(pool_steps, first + 7)
                pool.tensor_tensor(pooled[:, i, :], res[:, 0:S], pooled[:, i, :], ALU.subtract).then_inc(pooled_ready, 1)

            for r in range(4):
                pool.wait_ge(rope2_done, 3 + r if r < 2 else 4 + r)
                if r:
                    pool.wait_ge(qk_done, HQ + 2 * r)
                else:
                    pool.wait_ge(hid_turned, 1)
                    pool.wait_ge(gt_ready, 1)
                pool.tensor_copy(q_cur[:, 0, :], q2[:, r, :]).then_inc(qcur_ready, 1)
                pool_group(r)
            sums(4, S)
            sums(5, S)

        @block.scalar
        def _(act):
            act.dma_start(vec[:], a["vectors"]).then_inc(vec_landed, 16)
            for i in range(2):
                act.dma_start(x[:, 4 * i:4 * i + 4, :], a["tokens"][:, 4 * i:4 * i + 4, :]).then_inc(x_landed[i], 16)
            act.dma_start(cst[:, 0:K_R1], a["consts"][:, 0:K_R1]).then_inc(ident_landed, 16)

            def split(pr, k, half):
                src = landed_in(k)
                if half == 0:
                    if src is raw:
                        act.wait_ge(raw_landed[k % 2], LANDED * pr + LANDED * (k // 2 + 1 - min(k, MOD_FRONT) // 4))
                    else:
                        act.wait_ge(front_landed[k % 2], LANDED * (k // 4 + 1))
                act.wait_ge(halves_done, 4 * pr + (2 * k + half + 1))
                cols = slice(half * HALF, (half + 1) * HALF)
                act.activation(w_hi[:, k % 2, cols], src[:, k % 2, cols], ACT.Copy).then_inc(h_ready, 1)

            def splits(pr, k):
                split(pr, k, 0)
                split(pr, k, 1)

            def done(pr, k):
                act.wait_ge(halves_done, 4 * pr + (2 * k + 6))

            def bank(k, t, n=S):
                return ps_u[:, 2 * (k % 2) + t, 0:n]

            act.wait_ge(vec_landed, 16)
            for i in range(2):
                act.activation(sc[:, :, i], vec[:, V_C + i * KD:V_C + (i + 1) * KD], ACT.Silu).then_inc(sc_ready, 1)
            act.wait_ge(sc_ready, 2)
            act.wait_ge(pad_ready, 1)
            act.activation(sc_pad[:, :, 0:2], sc[:], ACT.Copy).then_inc(pad_ready, 1)
            for u in range(2):
                splits(0, u)
            for kc in range(KD):
                act.wait_ge(x_landed[kc // 4], 16)
                act.activation(sq[:, kc, :], x[:, kc, :], ACT.Square).then_inc(sq_ready, 1)

            def prepare_root():
                act.activation(table[:], eps, ACT.Sqrt)

            def roots(n, tiles, width=D):
                act.wait_ge(stat_done, n + 1)
                act.activation(root[:, 0:tiles], ps_a[:, 3, 0:tiles], ACT.Sqrt, bias=eps, scale=1.0 / width)\
                   .then_inc(root_done, 1)

            def norm_hi(i, n, shift):
                for kc in range(KD):
                    act.wait_ge(z_ready, 8 * i + kc + 1)
                    for s, cols in segs(n):
                        if shift is None:
                            ins = act.activation(x_hi[:, kc, cols], sq[:, kc, cols], ACT.Copy)
                        else:
                            ins = act.activation(x_hi[:, kc, cols], sq[:, kc, cols], ACT.Identity,
                                                 bias=mods[:, shift * KD + kc, s:s + 1])
                    ins.then_inc(xh_ready, 1)

            def squares(pr, k, m, n, gain=None):
                act.wait_ge(drained, 2 * pr + (k + 3))
                for t in range(2):
                    if gain is not None:
                        act.activation(sq[:, m + t, S:NB], x[:, m + t, 0:S], ACT.Square, scale=vcol(gain, m + t))
                    act.activation(sq[:, m + t, 0:n], x[:, m + t, 0:n], ACT.Square).then_inc(sq_ready, 1)

            def out_step(pr, k0, i, n, gain=None, last=True, more=True):
                if last and i == 3:
                    prepare_root()
                    squares(pr, k0 + 2, 4, n, gain)
                    squares(pr, k0 + 3, 6, n, gain)
                if more:
                    splits(pr, k0 + i + 2)
                if last and i in (1, 2):
                    squares(pr, k0 + i - 1, 2 * i - 2, n, gain)

            act.wait_ge(ident_landed, 16)
            prepare_root()
            for u in range(MOD_FRONT):
                splits(0, u + 2)
                if u == 3:
                    roots(0, 4)
            act.dma_start(cst[:, K_R1:K_END], a["consts"][:, K_R1:K_END]).then_inc(cst_landed, 16)
            act.dma_start(late_w[:], a["late"]).then_inc(late, 16)
            norm_hi(0, NB, 0)
            act.wait_ge(cst_landed, 16)
            act.wait_ge(late, 16)
            act.activation(wg_hi[:], wg, ACT.Copy).then_inc(wg_done, 1)

            def slab1(s, pr, k, chunks, last):
                with act.Fori(0, chunks // 2) as p:
                    for j in range(2):
                        ki, m = k + 2 * j, 2 * p + j
                        split(pr + 2 * p, ki + 2, 0)
                        done(pr + 2 * p, ki)
                        act.activation(s1[:, j, :], bank(j, 0, NB), ACT.Silu).then_inc(silu_done, 1)
                        act.wait_ge(prod_done, 8 * s + m + 1)
                        act.activation(h_hi[:, m, :], t1[:, j, :], ACT.Copy).then_inc(hh_done, 1)
                        split(pr + 2 * p, ki + 2, 1)
                        splits(pr + 2 * p, ki + 3)
                for i, o in enumerate((0, None, 1, None, 2, 3)):
                    ko = k + 2 * chunks + i
                    if last and o == 3:
                        prepare_root()
                        squares(pr, ko - 1, 2 * o - 2, NB)
                        squares(pr, ko, 2 * o, NB)
                    splits(pr, ko + 2)
                    if last and o is None:
                        squares(pr, ko - 1, i - 1, NB)

            k = FIRST["ffn1"]
            with act.Fori(0, 2) as s:
                slab1(s, s * 11, k, SLABS[0], False)
            slab1(2, 0, k + 44, SLABS[2], True)
            roots(1, 4)
            norm_hi(1, NB, 3)

            def swiglu(base, count, n, gain):
                def slab(pr, k, c, chunks, last):
                    with act.Fori(0, chunks // 2) as p:
                        for j in range(2):
                            split(pr + p, k + j + 2, 0)
                            done(pr + p, k + j)
                            act.activation(s1[:, j, 0:n], bank(k + j, 0, n), ACT.Silu).then_inc(silu_done, 1)
                            act.wait_ge(prod_done, c + 2 * p + (j + 1))
                            act.activation(h_hi[:, 2 * p + j, 0:n], t1[:, j, 0:n], ACT.Copy).then_inc(hh_done, 1)
                            split(pr + p, k + j + 2, 1)
                    for i in range(4):
                        out_step(pr, k + chunks, i, n, gain if last else None, last)

                with act.Fori(0, 2) as s:
                    slab(s * 6, base, s * 8 + count, SLABS[0], False)
                slab(0, base + 24, count + 16, SLABS[2], True)

            k = FIRST["k"]
            split(0, k + 2, 0)
            done(0, k)
            for t in range(HKV):
                act.activation(s1[:, t, :], bank(k, t, NB), ACT.Square).then_inc(k_squared, 1)
            split(0, k + 2, 1)
            splits(0, k + 3)
            act.wait_ge(kstat_done, 1)
            act.activation(root[:, 0:8], ps_a[:, 1, 8:16], ACT.Sqrt, bias=eps, scale=1.0 / HD).then_inc(kroot_done, 1)
            with act.Fori(0, 2) as p:
                for j in range(2):
                    k = FIRST["q"] + j
                    split(p, k + 2, 0)
                    done(p, k)
                    for t in range(2):
                        act.activation(q_sq[:, 4 * p + (2 * j + t), :], bank(k, t), ACT.Square).then_inc(q_squared, 1)
                    split(p, k + 2, 1)
            act.wait_ge(qstat_done, 1)
            act.activation(root[:, 16:32], ps_a[:, 1, 16:32], ACT.Sqrt, bias=eps, scale=1.0 / HD).then_inc(qroot_done, 1)

            with act.Fori(0, 4) as p:
                for j in range(2):
                    k = FIRST["gates"] + j
                    split(p, k + 2, 0)
                    done(p, k)
                    act.activation(g_conv[:, 2 * p + j, :], bank(k, 0), ACT.Sigmoid)
                    act.activation(g_attn[:, 2 * p + j, :], bank(k, 1), ACT.Sigmoid).then_inc(gates_done, 1)
                    split(p, k + 2, 1)

            def turned1(h):
                act.wait_ge(t_done, 2 * h + 2)
                act.activation(probs_t[:, :, 0:P], ps_a[:, 2, :].rearrange("p (k q) -> p k q", k=4), ACT.Copy)\
                   .then_inc(pta_ready, 1)

            def head1_hi(h):
                act.wait_ge(pv_done, h + 1)
                act.activation(h_hi[:, h, S:NB], ps_a[:, 2, 0:S], ACT.Copy).then_inc(oh_ready, 1)

            def head1(pr, i, first=False):
                k, h = FIRST["conv"] + i, 2 * pr + i
                if not first:
                    turned1(h - 1)
                for qt in range(TT):
                    act.wait_ge(nb_ready, 2 * h + (qt + 1))
                    act.activation(probs[:, qt, :], ps_a[:, qt, :], ACT.Exp, bias=neg_top[:, qt:qt + 1],
                                   scale=q_scale[:, ds(2 * h + qt, 1)], accum_out=total[:, qt:qt + 1]).then_inc(exp_done, 1)
                split(pr, k + 2, 0)
                done(pr, k)
                act.activation(s1[:, i % 2, 0:S], bank(k, 0), ACT.Copy).then_inc(cg_copied, 1)
                split(pr, k + 2, 1)
                if not first:
                    head1_hi(h - 1)

            head1(0, 0, first=True)
            with act.Fori(0, 2) as p:
                head1(p, 1)
                head1(p, 2)
            for h in range(5, HQ):
                head1(0, h)
            turned1(HQ - 1)
            with act.Fori(0, 2) as p:
                for j in range(2):
                    k = FIRST["bg"] + j
                    split(p, k + 2, 0)
                    for t in range(2):
                        act.wait_ge(y_done, 4 * p + (2 * j + t + 1))
                        act.activation(h_hi[:, 4 * p + (2 * j + t), 0:S], t1[:, t, 0:S], ACT.Copy).then_inc(yh_done, 1)
                    split(p, k + 2, 1)
            head1_hi(HQ - 1)
            with act.Fori(0, 4) as p:
                for j in range(2):
                    k = FIRST["merge"] + j
                    split(p, k + 2, 0)
                    act.wait_ge(merge_terms, 6 * p + (3 * j + 3))
                    act.activation(x_hi[:, 2 * p + j, 0:S], t1[:, j, 0:S], ACT.Copy).then_inc(zh_done, 1)
                    split(p, k + 2, 1)
            for i in range(4):
                out_step(0, FIRST["wout"], i, S)

            roots(2, 2)
            norm_hi(2, S, 6)
            swiglu(FIRST["ffn2"], 22, S, V_F1)
            act.wait_ge(var_steps, 3)
            act.activation(root[:, 0:4], var[:], ACT.Sqrt).then_inc(root_done, 1)
            norm_hi(3, S, None)

            k = FIRST["kcvc"]

            def queries(g):
                done(0, k + 3 + g)
                for t in range(2):
                    for b in range(2):
                        ins = act.activation(q2[g * DH:(g + 1) * DH, 2 * t + b, :],
                                             ps_u[b * DH:(b + 1) * DH, 2 * ((k + 3 + g) % 2) + t, 0:S],
                                             ACT.Copy, scale=float(DH) ** -0.5)
                ins.then_inc(kv2_copied, 1)

            def gelu(i):
                act.wait_ge(hid_done, i + 1)
                act.activation(hid_rows[:, i, :], ps_a[0:G2 * NC, 0, i * CH:(i + 1) * CH], ACT.Gelu_apprx_tanh).then_inc(gelu_done, 1)

            splits(0, k + 2)
            act.wait_ge(gt_done, 1)
            act.activation(g_feat, ps_a[0:3 * H2, 1, 0:S], ACT.Sigmoid).then_inc(gt_sig, 1)
            splits(0, k + 3)
            act.wait_ge(gt_turned, 1)
            act.activation(g_tok[:], ps_a[:, 1, 0:TT * 3 * H2].rearrange("p (t c) -> p t c", t=TT), ACT.Copy).then_inc(gt_ready, 1)
            gelu(0)
            splits(0, k + 4)
            gelu(1)
            for g in range(G2):
                split(0, k + 5 + g, 0)
                queries(g)
                split(0, k + 5 + g, 1)
            splits(0, k + 7)
            splits(0, k + 8)

            def turned_probs(h):
                act.wait_ge(t_done, 2 * HQ + h + 1)
                act.activation(probs_t[:, :, P:2 * P], ps_a[:, 2, :].rearrange("p (k q) -> p k q", k=4), ACT.Copy)\
                   .then_inc(pta_ready, 1)

            def exps(h):
                act.wait_ge(masked, 3 * h + 3)
                for qt, rows in ((0, probs_lo), (1, probs_hi)):
                    for b in range(2):
                        n = (qt + 1) * P
                        act.activation(rows[:, b, :], ps_a[:, 1 - qt, b * n:(b + 1) * n], ACT.Exp,
                                       bias=neg_top2[:, qt, b + 1:b + 2], accum_out=total2[:, qt, b + 1:b + 2])
                for qt in range(TT):
                    ins = act.activation(sc_c[:, qt, :], sc_c[:, qt, :], ACT.Exp, bias=neg_top2[:, qt, 0:1])
                ins.then_inc(exp_done, 1)

            def gates_out(r, g):
                kg = FIRST["gates2"] + g
                done(r, kg)
                act.activation(gates2[:, 2 * r + g, :, :], ps_u[:, 2 * (kg % 2):2 * (kg % 2) + 2, 0:S], ACT.Copy)\
                   .then_inc(g2_copied, 1)

            def head_hi(h, r, g):
                act.wait_ge(pv_done, HQ + h + 1)
                act.activation(h_hi[g * DH:(g + 1) * DH, r, 0:S], ps_a[g * DH:(g + 1) * DH, 2, 0:S], ACT.Copy)\
                   .then_inc(oh_ready, 1)

            def head(h, r, g, before, first=False):
                kg = FIRST["gates2"] + g
                if not first:
                    turned_probs(h - 1)
                exps(h)
                split(r, kg + 2, 0)
                gates_out(r, g)
                split(r, kg + 2, 1)
                if not first:
                    head_hi(h - 1, *before)

            head(0, 0, 0, None, first=True)
            with act.Fori(0, 2) as p:
                head(2 * p + 1, p, 1, (p, 0))
                head(2 * p + 2, p + 1, 0, (p, 1))
            head(5, 2, 1, (2, 0))
            head(6, 3, 0, (2, 1))
            head(7, 3, 1, (3, 0))
            turned_probs(7)
            for i in range(4):
                act.wait_ge(mixed_done, i + 1)
                act.activation(mixed[:, i, :], ps_a[:, i % 2, 0:S], ACT.Identity, scale=vcol(V_PS, i)).then_inc(ph_done, 1)
                act.wait_ge(ph_done, 2 * i + 1)
                act.activation(h_hi[:, i, S:NB], mixed[:, i, :], ACT.Copy).then_inc(ph_done, 1)
            head_hi(7, 3, 1)

            with act.Fori(0, 2) as p:
                for j in range(2):
                    k, m = FIRST["merge2"] + j, 4 * p + 2 * j
                    act.activation(gates2[:, ds(m, 2), :, :], gates2[:, ds(m, 2), :, :], ACT.Sigmoid).then_inc(g2_done, 1)
                    split(p, k + 2, 0)
                    act.wait_ge(merge_terms, 6 * p + (24 + 3 * j + 3))
                    act.activation(x_hi[:, ds(m, 2), 0:S], t1[:, 0, :].rearrange("p (m n) -> p m n", m=2), ACT.Copy)\
                       .then_inc(zh_done, 1)
                    split(p, k + 2, 1)
            for i in range(4):
                out_step(0, FIRST["wout2"], i, S)
            roots(4, 2)
            norm_hi(4, S, None)

            def relu2(pr, k, c, last):
                with act.Fori(0, 2) as p:
                    for j in range(2):
                        split(pr + p, k + j + 2, 0)
                        done(pr + p, k + j)
                        for t in range(2):
                            act.activation(s1[:, t, 0:S], bank(k + j, t), ACT.Relu).then_inc(relu_done, 1)
                        for t in range(2):
                            act.wait_ge(prod_done, c + 4 * p + (2 * j + t + 1))
                            act.activation(h_hi[:, 4 * p + (2 * j + t), 0:S], t1[:, t, 0:S], ACT.Copy).then_inc(hh_done, 1)
                        split(pr + p, k + j + 2, 1)
                for i in range(4):
                    out_step(pr, k + 4, i, S, None, last, not (last and i >= 2))

            with act.Fori(0, SLABS2 - 1) as s:
                relu2(s * 4, FIRST["ff"], s * 8 + 44, False)
            relu2(0, FIRST["ff"] + 8 * (SLABS2 - 1), 44 + 8 * (SLABS2 - 1), True)
            roots(5, 2)

        @block.vector
        def _(dve):
            dve.memset(ones[:], 1.0).then_inc(ones_ready, 1)
            dve.memset(u_pad[:], 0.0).then_inc(l_ready, 4)
            dve.memset(p_pad[:], 0.0).then_inc(drained, 2)
            dve.memset(sc_pad[:].bitcast(F32), 0.0).then_inc(pad_ready, 1)
            dve.memset(pc[:], 0.0).then_inc(ones_ready, 1)
            dve.memset(tick[:], 0.0).then_inc(o1_done, 1)
            dve.memset(vc_tok[:], 0.0).then_inc(ones_ready, 1)
            dve.wait_ge(ones_ready, 3)

            def split(pr, k, half):
                if half == 0:
                    dve.wait_ge(drained, 2 * pr + k)
                cols = slice(half * HALF, (half + 1) * HALF)
                dve.wait_ge(h_ready, 4 * pr + (2 * k + half + 1))
                dve.tensor_tensor(w_lo[:, k % 2, cols], landed_in(k)[:, k % 2, cols], w_hi[:, k % 2, cols].bitcast(F32),
                                  ALU.subtract).then_inc(l_ready, 1)

            def splits(pr, k):
                split(pr, k, 0)
                split(pr, k, 1)

            def done(pr, k):
                dve.wait_ge(halves_done, 4 * pr + (2 * k + 6))

            def bank(k, t, n=S):
                return ps_u[:, 2 * (k % 2) + t, 0:n]

            dve.wait_ge(pad_ready, 2)
            dve.tensor_tensor(sc_pad[:, :, 2:4], sc[:], sc_pad[:, :, 0:2].bitcast(F32), ALU.subtract).then_inc(pad_ready, 1)
            dve.tensor_scalar(bm_half[:], bm, 0.5, None, ALU.mult).then_inc(vec_ready, 1)
            dve.tensor_tensor(gg[:], vec[:, V_F1:V_F1 + KD], vec[:, V_MIX:V_MIX + KD], ALU.mult).then_inc(vec_ready, 1)

            def mod(pr, k, m, b):
                done(pr, k)
                for q in range(P // MOD_ROWS):
                    rows = slice(q * MOD_ROWS, (q + 1) * MOD_ROWS)
                    for t in range(2):
                        lo = t * P + q * MOD_ROWS
                        ins = dve.transpose(turned[rows, b, t, :], ps_a[0:MOD_ROWS, b, lo:lo + MOD_ROWS])
                ins.then_inc(mod_turned, 1)
                dve.wait_ge(mod_turned, m + 1)
                dve.tensor_tensor(mod_sum[:, ds(2 * m, 2), :], turned[:, b, :, 0:2], turned[:, b, :, 2:4], ALU.add)\
                   .then_inc(drained, 1)

            def modulations(lo, hi, norms, count):
                for s in range(2):
                    ins = dve.tensor_tensor(mods[:, lo:hi, s], mod_sum[:, lo:hi, s], bm[:, lo:hi], ALU.add)
                ins.then_inc(gate_ready, 1)
                dve.wait_ge(gate_ready, count)
                for i, chunk, v in norms:
                    for s in range(2):
                        ins = dve.scalar_tensor_tensor(am[:, i, :, s], mods[:, chunk * KD:(chunk + 1) * KD, s], 1.0,
                                                       vec[:, v:v + KD], ALU.add, ALU.mult)
                ins.then_inc(mods_ready, 1)

            def gates_of(i, chunk):
                for s in range(2):
                    ins = dve.scalar_tensor_tensor(gate_half[:, i, :, s], mod_sum[:, chunk * KD:(chunk + 1) * KD, s], 0.5,
                                                   bm_half[:, chunk * KD:(chunk + 1) * KD], ALU.mult, ALU.add)
                ins.then_inc(gate_ready, 1)

            def spread(n, tiles):
                dve.wait_ge(root_done, n + 1)
                dve.reciprocal(rstd[:, 0:tiles], root[:, 0:tiles]).then_inc(recip_done, 1)
                dve.wait_ge(recip_done, n + 1)
                for t in range(tiles):
                    ins = dve.tensor_scalar(t1[:, 0, t * P:(t + 1) * P], ident, rstd[:, t:t + 1], None, ALU.mult)
                ins.then_inc(diag_done, 1)

            def norm_lo(n, i, width, scale, shift, at=0):
                dve.wait_ge(rb_done, n + 1)

                def z(kc):
                    for s, cols in segs(width):
                        spread_cols = slice(at + cols.start, at + cols.stop)
                        ins = dve.scalar_tensor_tensor(sq[:, kc, cols], x[:, kc, cols], scale(kc, s), ps_a[:, 2, spread_cols],
                                                       ALU.mult, ALU.mult)
                    ins.then_inc(z_ready, 1)

                def lo(kc):
                    dve.wait_ge(xh_ready, 8 * i + kc + 1)
                    for s, cols in segs(width):
                        hi = x_hi[:, kc, cols].bitcast(F32)
                        if shift is None:
                            ins = dve.tensor_tensor(x_lo[:, kc, cols], sq[:, kc, cols], hi, ALU.subtract)
                        else:
                            ins = dve.scalar_tensor_tensor(x_lo[:, kc, cols], sq[:, kc, cols],
                                                           mods[:, shift * KD + kc, s:s + 1], hi, ALU.add, ALU.subtract)
                    ins.then_inc(xl_ready, 1)

                z(0)
                for kc in range(KD):
                    if kc + 1 < KD:
                        z(kc + 1)
                    lo(kc)

            def modulated(i, scale):
                return lambda kc, s: am[:, i, kc, s:s + 1]

            def plain(v):
                return lambda kc, s: vcol(v, kc)

            def add_out(pr, k, m, n, gate, b=None):
                done(pr, k)
                b = k if b is None else b
                for t in range(2):
                    for s, cols in segs(n):
                        if gate is None:
                            ins = dve.tensor_tensor(x[:, m + t, cols], bank(b, t, n)[:, cols], x[:, m + t, cols], ALU.add)
                        else:
                            ins = dve.scalar_tensor_tensor(x[:, m + t, cols], bank(b, t, n)[:, cols], gate(m + t, s),
                                                           x[:, m + t, cols], ALU.mult, ALU.add)
                ins.then_inc(drained, 1)

            def out_step(pr, k0, i, n, gate, last=True, more=True):
                hurry = last and i == 3
                if more and not hurry:
                    split(pr, k0 + i + 2, 0)
                add_out(pr, k0 + i, 2 * i, n, gate)
                if more and hurry:
                    split(pr, k0 + i + 2, 0)
                if more:
                    split(pr, k0 + i + 2, 1)

            dve.wait_ge(vec_ready, 2)
            for u in range(2):
                splits(0, u)
            for u in range(MOD_FRONT):
                split(0, u + 2, 0)
                mod(0, u, u, u % 2)
                split(0, u + 2, 1)
                if u == 4:
                    spread(0, 4)
            dve.wait_ge(drained, MOD_FRONT + 2)
            modulations(0, 2 * KD, ((0, 1, V_N1),), 1)
            dve.wait_ge(mods_ready, 1)
            norm_lo(0, 0, NB, modulated(0, 1), 0)
            dve.wait_ge(wg_done, 1)
            dve.tensor_tensor(wg_lo[:], wg, wg_hi[:].bitcast(F32), ALU.subtract).then_inc(wg_ready, 1)

            def slab1(s, pr, k, chunks, last):
                def ride(m):
                    return MOD_RIDE * s + (MOD_FRONT + m)

                with dve.Fori(0, chunks // 2) as p:
                    for j in range(2):
                        ki, m = k + 2 * j, 2 * p + j
                        split(pr + 2 * p, ki + 2, 0)
                        dve.wait_ge(silu_done, 8 * s + m + 1)
                        dve.tensor_tensor(t1[:, j, :], s1[:, j, :], bank(j, 1, NB), ALU.mult).then_inc(prod_done, 1)
                        dve.wait_ge(hh_done, 8 * s + m + 1)
                        dve.tensor_tensor(h_lo[:, m, :], t1[:, j, :], h_hi[:, m, :].bitcast(F32), ALU.subtract)\
                           .then_inc(drained, 1)
                        split(pr + 2 * p, ki + 2, 1)
                        split(pr + 2 * p, ki + 3, 0)
                        mod(pr + 2 * p, ki + 1, ride(m), j)
                        split(pr + 2 * p, ki + 3, 1)
                ko = k + 2 * chunks
                dve.wait_ge(drained, 2 * pr + (ko + 2))
                gates_of(0, 2)
                dve.wait_ge(gate_ready, s + 2)
                for i, o in enumerate((0, None, 1, None, 2, 3)):
                    if not (last and o == 3):
                        split(pr, ko + i + 2, 0)
                    if o is None:
                        mod(pr, ko + i, ride(chunks + i // 2), (i // 2) % 2)
                    else:
                        if last and o == 3:
                            dve.wait_ge(drained, ko + i + 1)
                            gates_of(1, 8)
                            modulations(3 * KD, 8 * KD, ((1, 4, V_N2), (2, 7, V_N3)), 6)
                        add_out(pr, ko + i, 2 * o, NB, lambda m, s: gate_half[:, 0, m, s:s + 1], o)
                    if last and o == 3:
                        split(pr, ko + i + 2, 0)
                    split(pr, ko + i + 2, 1)

            k = FIRST["ffn1"]
            with dve.Fori(0, 2) as s:
                slab1(s, s * 11, k, SLABS[0], False)
            slab1(2, 0, k + 44, SLABS[2], True)
            spread(1, 4)
            dve.wait_ge(mods_ready, 2)
            norm_lo(1, 1, NB, modulated(1, 4), 3)

            def swiglu(base, count, n, i):
                def gate(m, s):
                    return gate_half[:, i, m, s:s + 1]

                def slab(pr, k, c, chunks, last):
                    with dve.Fori(0, chunks // 2) as p:
                        for j in range(2):
                            split(pr + p, k + j + 2, 0)
                            dve.wait_ge(silu_done, c + 2 * p + (j + 1))
                            dve.tensor_tensor(t1[:, j, 0:n], s1[:, j, 0:n], bank(k + j, 1, n), ALU.mult)\
                               .then_inc(prod_done, 1)
                            dve.wait_ge(hh_done, c + 2 * p + (j + 1))
                            dve.tensor_tensor(h_lo[:, 2 * p + j, 0:n], t1[:, j, 0:n],
                                              h_hi[:, 2 * p + j, 0:n].bitcast(F32), ALU.subtract).then_inc(drained, 1)
                            split(pr + p, k + j + 2, 1)
                    for o in range(4):
                        out_step(pr, k + chunks, o, n, gate, last)

                with dve.Fori(0, 2) as s:
                    slab(s * 6, base, s * 8 + count, SLABS[0], False)
                slab(0, base + 24, count + 16, SLABS[2], True)

            k = FIRST["k"]
            split(0, k + 2, 0)
            for t in range(HKV):
                dve.wait_ge(k_squared, t + 1)
                ins = dve.tensor_scalar(k_all[:, t, :], bank(k, t, NB), vcol(V_KG, 0), None, ALU.mult)
                ins.then_inc(drained if t else k_gained, 1)
            split(0, k + 2, 1)
            split(0, k + 3, 0)
            done(0, k + 1)
            dve.tensor_copy(v_feat[:, 0, :], bank(k + 1, 0, NB))
            dve.tensor_copy(v_feat[:, 1, :], bank(k + 1, 1, NB)).then_inc(drained, 1)
            split(0, k + 3, 1)
            dve.wait_ge(kroot_done, 1)
            dve.reciprocal(rstd[:, 0:8], root[:, 0:8]).then_inc(krecip_done, 1)
            dve.wait_ge(krecip_done, 1)
            for t in range(8):
                ins = dve.tensor_scalar(t1[:, t // 4, (t % 4) * P:(t % 4 + 1) * P], ident, rstd[:, t:t + 1], None, ALU.mult)
            ins.then_inc(kdiag_done, 1)

            def q_gain(i):
                kq = FIRST["q"] + i
                split(0, kq + 2, 0)
                for t in range(2):
                    dve.wait_ge(q_squared, 2 * i + t + 1)
                    ins = dve.tensor_scalar(q_rows[:, 2 * i + t, :], bank(kq, t), vcol(V_QG, 0), None, ALU.mult)
                ins.then_inc(drained, 1)
                split(0, kq + 2, 1)

            q_gain(0)
            dve.wait_ge(v_turned, 1)
            dve.tensor_copy(v_tok[:, :, 0, :], ps_a[:, 0, :].rearrange("p (c d) -> p c d", c=4)).then_inc(v_ready, 1)
            q_gain(1)
            for t in range(HKV):
                dve.wait_ge(krb_done, t + 1)
                dve.tensor_tensor(k_all[:, t, :], k_all[:, t, :], ps_a[:, 2 + t, :], ALU.mult).then_inc(k_normed, 1)
            q_gain(2)
            dve.wait_ge(k_normed, 2)
            for t in range(HKV):
                dve.wait_ge(k_swapped, t + 1)
                if t:
                    dve.wait_ge(k_ready, t)
                dve.tensor_tensor(t1[:, 0, 0:S], k_all[:, t, 0:S], cos1, ALU.mult)
                dve.tensor_tensor(t1[:, 1, 0:S], ps_a[:, 2 + t, 0:S], sin1, ALU.mult).then_inc(k_terms, 1)
                dve.wait_ge(k_terms, t + 1)
                dve.tensor_tensor(k_all[:, t, 0:S], t1[:, 0, 0:S], t1[:, 1, 0:S], ALU.add).then_inc(k_ready, 1)
            q_gain(3)
            dve.wait_ge(v_turned, 2)
            dve.tensor_copy(v_tok[:, :, 1, :], ps_a[:, 0, :].rearrange("p (c d) -> p c d", c=4)).then_inc(v_ready, 1)
            dve.wait_ge(qroot_done, 1)
            dve.reciprocal(rstd[:, 16:32], root[:, 16:32]).then_inc(qrecip_done, 1)
            dve.wait_ge(qrecip_done, 1)
            dve.tensor_scalar(q_scale[:], rstd[:, 16:32], float(HD) ** -0.5, None, ALU.mult).then_inc(q_scaled, 1)

            dve.wait_ge(drained, FIRST["gates"] + 2)
            with dve.Fori(0, 4) as p:
                for j in range(2):
                    k = FIRST["gates"] + j
                    h = 2 * p + j
                    split(p, k + 2, 0)
                    dve.wait_ge(q_swapped, h + 1)
                    dve.tensor_tensor(t1[:, j, 0:S], q_rows[:, h, :], cos1, ALU.mult)
                    dve.tensor_tensor(t1[:, j, S:NB], ps_a[:, 2 + j, 0:S], sin1, ALU.mult).then_inc(q_terms, 1)
                    dve.wait_ge(q_terms, h + 1)
                    dve.wait_ge(gates_done, h + 1)
                    dve.tensor_tensor(q_rows[:, h, :], t1[:, j, 0:S], t1[:, j, S:NB], ALU.add).then_inc(drained, 1)
                    split(p, k + 2, 1)

            dve.wait_ge(q_scaled, 1)

            def turned1(h):
                dve.wait_ge(t_done, 2 * h + 2)
                dve.tensor_copy(probs_t[:, :, P:2 * P], ps_a[:, 3, :].rearrange("p (k q) -> p k q", k=4)).then_inc(ptd_ready, 1)

            def head1_lo(h):
                dve.wait_ge(oh_ready, h + 1)
                dve.tensor_tensor(h_lo[:, h, S:NB], ps_a[:, 2, 0:S], h_hi[:, h, S:NB].bitcast(F32), ALU.subtract)\
                   .then_inc(o1_done, 1)

            def head1(pr, i, first=False):
                k, h = FIRST["conv"] + i, 2 * pr + i
                dve.wait_ge(qk_done, h + 1)
                for qt in range(TT):
                    ins = dve.tensor_reduce(top[:, qt:qt + 1], ps_a[:, qt, :], AX_X, ALU.max)
                ins.then_inc(top_done, 1)
                dve.wait_ge(top_done, h + 1)
                for qt in range(TT):
                    dve.tensor_scalar(neg_top[:, qt:qt + 1], top[:, qt:qt + 1], q_scale[:, ds(2 * h + qt, 1)], -1.0,
                                      ALU.mult, ALU.mult).then_inc(nb_ready, 1)
                if not first:
                    turned1(h - 1)
                dve.wait_ge(exp_done, 2 * h + 2)
                dve.reciprocal(inv[:], total[:]).then_inc(inv_done, 1)
                dve.wait_ge(inv_done, h + 1)
                for qt in range(TT):
                    dve.tensor_scalar(probs[:, qt, :], probs[:, qt, :], inv[:, qt:qt + 1], None, ALU.mult).then_inc(p_ready, 1)
                split(pr, k + 2, 0)
                dve.wait_ge(cg_copied, h + 1)
                dve.tensor_tensor(u_pad[:, 1:S + 1], s1[:, i % 2, 0:S], bank(k, 1), ALU.mult).then_inc(u_ready, 1)
                dve.wait_ge(u_ready, h + 1)
                dve.tensor_scalar(t1[:, 0, 0:S], u_pad[:, 0:S], vcol(V_CONV, h), None, ALU.mult).then_inc(conv_terms, 1)
                dve.wait_ge(conv_terms, 2 * h + 1)
                dve.scalar_tensor_tensor(t1[:, 1, 0:S], u_pad[:, 1:S + 1], vcol(V_CONV + KD, h), t1[:, 0, 0:S],
                                         ALU.mult, ALU.add).then_inc(conv_terms, 1)
                dve.wait_ge(conv_terms, 2 * h + 2)
                dve.scalar_tensor_tensor(y_conv[:, h, :], u_pad[:, 2:S + 2], vcol(V_CONV + 2 * KD, h), t1[:, 1, 0:S],
                                         ALU.mult, ALU.add).then_inc(drained, 1)
                split(pr, k + 2, 1)
                if not first:
                    head1_lo(h - 1)

            head1(0, 0, first=True)
            with dve.Fori(0, 2) as p:
                head1(p, 1)
                head1(p, 2)
            for h in range(5, HQ):
                head1(0, h)
            turned1(HQ - 1)
            dve.wait_ge(drained, FIRST["bg"] + 2)
            with dve.Fori(0, 2) as p:
                for j in range(2):
                    k = FIRST["bg"] + j
                    split(p, k + 2, 0)
                    done(p, k)
                    for t in range(2):
                        m = 4 * p + (2 * j + t)
                        dve.tensor_tensor(t1[:, t, 0:S], y_conv[:, m, :], bank(k, t), ALU.mult).then_inc(y_done, 1)
                    for t in range(2):
                        m = 4 * p + (2 * j + t)
                        dve.wait_ge(yh_done, m + 1)
                        ins = dve.tensor_tensor(h_lo[:, m, 0:S], t1[:, t, 0:S], h_hi[:, m, 0:S].bitcast(F32), ALU.subtract)
                    ins.then_inc(drained, 1)
                    split(p, k + 2, 1)
            head1_lo(HQ - 1)

            with dve.Fori(0, 4) as p:
                for j in range(2):
                    k = FIRST["merge"] + j
                    m = 2 * p + j
                    split(p, k + 2, 0)
                    done(p, k)
                    dve.tensor_tensor(t1[:, j, 0:S], g_conv[:, m, :], bank(k, 0), ALU.mult).then_inc(merge_terms, 1)
                    dve.tensor_tensor(t1[:, j, S:NB], g_attn[:, m, :], bank(k, 1), ALU.mult).then_inc(merge_terms, 1)
                    dve.wait_ge(merge_terms, 6 * p + (3 * j + 2))
                    dve.tensor_tensor(t1[:, j, 0:S], t1[:, j, 0:S], t1[:, j, S:NB], ALU.add).then_inc(merge_terms, 1)
                    dve.wait_ge(zh_done, m + 1)
                    dve.tensor_tensor(x_lo[:, m, 0:S], t1[:, j, 0:S], x_hi[:, m, 0:S].bitcast(F32), ALU.subtract)\
                       .then_inc(drained, 1)
                    split(p, k + 2, 1)
            for i in range(4):
                out_step(0, FIRST["wout"], i, S, lambda m, s: mods[:, 5 * KD + m, s:s + 1])

            spread(2, 2)
            norm_lo(2, 2, S, modulated(2, 7), 6)
            swiglu(FIRST["ffn2"], 22, S, 1)

            dve.wait_ge(stat_done, 4)
            dve.tensor_scalar(var[:], ps_a[:, 3, 0:2 * TT], 1.0 / D, None, ALU.mult).then_inc(var_steps, 1)
            dve.wait_ge(var_steps, 1)
            dve.tensor_scalar(var[:, 0:TT], var[:, 0:TT], EPS, None, ALU.add).then_inc(var_steps, 1)
            dve.wait_ge(var_steps, 2)
            dve.scalar_tensor_tensor(var[:, TT:2 * TT], var[:, 0:TT], EPS, var[:, TT:2 * TT], ALU.mult, ALU.add)\
               .then_inc(var_steps, 1)
            spread(3, 4)
            norm_lo(3, 3, S, lambda kc, s: gg[:, kc:kc + 1], None, S)
            k = FIRST["kcvc"]
            split(0, k + 2, 0)
            done(0, k)
            for t in range(2):
                for g in range(G2):
                    for j in range(2):
                        rows = slice(j * DH, (j + 1) * DH)
                        src = ps_u[g * DH:(g + 1) * DH, 2 * (k % 2) + t, j * CS:j * CS + NC * CS]
                        pos = pec[rows, t * CB + j * CS:t * CB + (j + 1) * CS]
                        ins = dve.tensor_tensor(cmp_in[t][rows, :, g, :], src.rearrange("p (c l) -> p l c", l=CS),
                                                pos.unsqueeze(2).broadcast_to([DH, CS, NC]), ALU.add)
                ins.then_inc(cmp_ready if t == 0 else drained, 1)
            split(0, k + 2, 1)
            for kc in range(KD):
                ins = dve.scalar_tensor_tensor(x[:, kc, 0:S], x[:, kc, 0:S], vcol(V_F1, kc), ps_a[:, 2, 0:S], ALU.mult, ALU.mult)
            ins.then_inc(x_scaled, 1)
            for b in range(2):
                split(0, k + 3 + b, 0)
                done(0, k + 1 + b)
                dve.tensor_copy(kk2[:, b * S:(b + 1) * S], bank(k + 1 + b, 0))
                dve.tensor_copy(v2_feat[:, b, :], bank(k + 1 + b, 1)).then_inc(drained, 1)
                split(0, k + 3 + b, 1)

            def rope2(n, rows, bank_cols, cos, sin, dst=None):
                dve.wait_ge(rope2_swapped, n + 1)
                if n:
                    dve.wait_ge(rope2_done, n)
                width = rows.shape[-1]
                dve.tensor_tensor(t1[:, 0, 0:width], rows, cos, ALU.mult)
                dve.tensor_tensor(t1[:, 1, 0:width], bank_cols, sin, ALU.mult).then_inc(rope2_terms, 1)
                dve.wait_ge(rope2_terms, n + 1)
                dve.tensor_tensor(rows if dst is None else dst, t1[:, 0, 0:width], t1[:, 1, 0:width], ALU.add)\
                   .then_inc(rope2_done, 1)

            def queries(g):
                split(0, k + 5 + g, 0)
                dve.wait_ge(kv2_copied, g + 1)
                dve.drain().then_inc(drained, 1)
                split(0, k + 5 + g, 1)

            def pool_in(i):
                split(0, k + 7 + i, 0)
                done(0, k + 5 + i)
                b = (k + 5 + i) % 2
                dve.tensor_copy(pooled[:, 2 * i:2 * i + 2, :], ps_u[:, 2 * b:2 * b + 2, 0:S]).then_inc(pool_copied, 1)
                dve.drain().then_inc(drained, 1)
                split(0, k + 7 + i, 1)

            queries(0)
            for b in range(2):
                rope2(b, kk2[:, b * S:(b + 1) * S], ps_a[:, 2 + b, 0:S], cos2, sin2)
            dve.wait_ge(v2_turned, 1)
            dve.tensor_copy(v2_tok, ps_a[:, 1, :].rearrange("p (b k n) -> p b k n", b=2, k=2)).then_inc(v2_ready, 1)
            dve.wait_ge(hid_turned, 1)
            dve.tensor_copy(hid[:], ps_a[:, 0, 0:4 * G2 * NC].rearrange("p (i h c) -> p i h c", i=2, h=2)).then_inc(hid_copied, 1)
            queries(1)
            dve.wait_ge(cmp_done, 2)
            dve.tensor_copy(kc_r[:, 0, :], ps_a[:, 0, 128:128 + NC]).then_inc(kc_raw, 1)
            dve.tensor_copy(vc_tok[0:NC, :, :], ps_a[0:NC, 0, 256:256 + G2 * DH].rearrange("p (g d) -> p g d", g=G2))\
               .then_inc(kc_raw, 1)
            pool_in(0)
            for r in range(2):
                rope2(2 + r, q2[:, r, :], ps_a[:, 2 + r % 2, 0:S], cos2, sin2)
            last = CB - 1
            dve.wait_ge(kc_raw, 2)
            rope2(4, kc_r[:, 0, :], ps_a[:, 1, 0:NC], cos2[:, last:S:CS], sin2[:, last:S:CS], kc_r[:, 1, :])
            pool_in(1)
            for r in range(2, 4):
                rope2(3 + r, q2[:, r, :], ps_a[:, 2 + r % 2, 0:S], cos2, sin2)
            dve.wait_ge(gt_ready, 1)
            g_head = g_tok[:].rearrange("p t (b h) -> p t b h", b=3)
            diag = cst[:, K_MASK:K_MASK + P].unsqueeze(1).broadcast_to([P, 2, P])

            def maxima(h, first):
                dve.wait_ge(qk_done, HQ + h + 1)
                if not first:
                    dve.wait_ge(p_ready, 2 * HQ + h)
                lo = ps_a[:, 1, 0:2 * P].rearrange("p (b n) -> p b n", b=2)
                hi = ps_a[:, 0, :].rearrange("p (b n) -> p b n", b=2)
                dve.tensor_tensor(lo, lo, diag, ALU.add).then_inc(cmp_masked, 1)
                dve.tensor_tensor(hi[:, :, P:2 * P], hi[:, :, P:2 * P], diag, ALU.add).then_inc(cmp_masked, 1)
                dve.tensor_tensor(sc_c[:], ps_a[:, 1, 2 * P:2 * P + TT * 16].rearrange("p (t c) -> p t c", t=TT)[:, :, 0:NC],
                                  cadd, ALU.add).then_inc(cmp_masked, 1)
                dve.wait_ge(cmp_masked, 3 * h + 3)
                dve.tensor_reduce(neg_top2[:, 0, 1:3], lo, AX_X, ALU.max, negate=True).then_inc(masked, 1)
                dve.tensor_reduce(neg_top2[:, 1, 1:3], hi, AX_X, ALU.max, negate=True).then_inc(masked, 1)
                dve.tensor_reduce(neg_top2[:, :, 0], sc_c[:], AX_X, ALU.max, negate=True).then_inc(masked, 1)

            def turned_probs(h):
                dve.wait_ge(t_done, 2 * HQ + h + 1)
                dve.tensor_copy(probs_t[:, 0:4:2, 0:P], ps_a[:, 3, 0:2 * P].rearrange("p (k q) -> p k q", k=2))
                dve.tensor_copy(q_cur[:, 1, :], ps_a[:, 3, 2 * P:4 * P]).then_inc(ptd_ready, 1)

            def scaled(h, r, g):
                dve.wait_ge(exp_done, 2 * HQ + h + 1)
                dve.tensor_tensor(sc_c[:], sc_c[:], cmul, ALU.mult).then_inc(cmp_steps, 1)
                dve.wait_ge(cmp_steps, 2 * h + 1)
                dve.tensor_reduce(total2[:, :, 0], sc_c[:], AX_X, ALU.add).then_inc(cmp_steps, 1)
                dve.wait_ge(cmp_steps, 2 * h + 2)
                dve.tensor_scalar(total2[:], total2[:], 1e-30, None, ALU.max).then_inc(coef_steps, 1)
                dve.wait_ge(coef_steps, 3 * h + 1)
                dve.reciprocal(inv2[:], total2[:]).then_inc(coef_steps, 1)
                dve.wait_ge(coef_steps, 3 * h + 2)
                dve.tensor_tensor(inv2[:], inv2[:], g_head[:, :, :, r + 4 * g], ALU.mult).then_inc(coef_steps, 1)
                dve.wait_ge(coef_steps, 3 * h + 3)
                for qt, rows in ((0, probs_lo), (1, probs_hi)):
                    for b in range(2):
                        dve.tensor_scalar(rows[:, b, :], rows[:, b, :], inv2[:, qt, b + 1:b + 2], None, ALU.mult)
                for qt in range(TT):
                    ins = dve.tensor_scalar(pc[:, qt, 0:NC], sc_c[:, qt, :], inv2[:, qt, 0:1], None, ALU.mult)
                ins.then_inc(p_ready, 1)

            def head_lo(h, r, g):
                dve.wait_ge(oh_ready, HQ + h + 1)
                rows = slice(g * DH, (g + 1) * DH)
                dve.tensor_tensor(h_lo[rows, r, 0:S], ps_a[rows, 2, 0:S], h_hi[rows, r, 0:S].bitcast(F32), ALU.subtract)\
                   .then_inc(o2_done, 1)

            def head(h, r, g, before, first=False):
                kg = FIRST["gates2"] + g
                maxima(h, first)
                if not first:
                    turned_probs(h - 1)
                scaled(h, r, g)
                split(r, kg + 2, 0)
                dve.wait_ge(g2_copied, h + 1)
                dve.tensor_copy(tick[:], eps).then_inc(drained, 1)
                split(r, kg + 2, 1)
                if not first:
                    head_lo(h - 1, *before)

            head(0, 0, 0, None, first=True)
            with dve.Fori(0, 2) as p:
                head(2 * p + 1, p, 1, (p, 0))
                head(2 * p + 2, p + 1, 0, (p, 1))
            head(5, 2, 1, (2, 0))
            head(6, 3, 0, (2, 1))
            head(7, 3, 1, (3, 0))
            turned_probs(7)
            for i in range(4):
                dve.wait_ge(ph_done, 2 * i + 2)
                dve.tensor_tensor(h_lo[:, i, S:NB], mixed[:, i, :], h_hi[:, i, S:NB].bitcast(F32), ALU.subtract)\
                   .then_inc(pl_done, 1)
            head_lo(7, 3, 1)

            with dve.Fori(0, 2) as p:
                for j in range(2):
                    k, m = FIRST["merge2"] + j, 4 * p + 2 * j
                    split(p, k + 2, 0)
                    dve.wait_ge(g2_done, 2 * p + (j + 1))
                    done(p, k)
                    for t in range(2):
                        dve.tensor_tensor(t1[:, t, :].rearrange("p (m n) -> p m n", m=2), gates2[:, ds(m, 2), t, :],
                                          bank(k, t, NB).rearrange("p (m n) -> p m n", m=2), ALU.mult).then_inc(merge_terms, 1)
                    dve.wait_ge(merge_terms, 6 * p + (24 + 3 * j + 2))
                    dve.tensor_tensor(t1[:, 0, :], t1[:, 0, :], t1[:, 1, :], ALU.add).then_inc(merge_terms, 1)
                    dve.wait_ge(zh_done, 2 * p + (j + KD + 1))
                    dve.tensor_tensor(x_lo[:, ds(m, 2), 0:S], t1[:, 0, :].rearrange("p (m n) -> p m n", m=2),
                                      x_hi[:, ds(m, 2), 0:S].bitcast(F32), ALU.subtract).then_inc(drained, 1)
                    split(p, k + 2, 1)

            dve.wait_ge(x_scaled, 1)
            for i in range(4):
                out_step(0, FIRST["wout2"], i, S, None)
            spread(4, 2)
            norm_lo(4, 4, S, plain(V_MLP), None)

            def relu2(pr, k, c, last):
                with dve.Fori(0, 2) as p:
                    for j in range(2):
                        split(pr + p, k + j + 2, 0)
                        for t in range(2):
                            dve.wait_ge(relu_done, c - 44 + 4 * p + (2 * j + t + 1))
                            dve.tensor_tensor(t1[:, t, 0:S], s1[:, t, 0:S], s1[:, t, 0:S], ALU.mult).then_inc(prod_done, 1)
                        for t in range(2):
                            m = 4 * p + (2 * j + t)
                            dve.wait_ge(hh_done, c + m + 1)
                            ins = dve.tensor_tensor(h_lo[:, m, 0:S], t1[:, t, 0:S], h_hi[:, m, 0:S].bitcast(F32), ALU.subtract)
                        ins.then_inc(drained, 1)
                        split(pr + p, k + j + 2, 1)
                for i in range(4):
                    out_step(pr, k + 4, i, S, None, last, not (last and i >= 2))

            with dve.Fori(0, SLABS2 - 1) as s:
                relu2(s * 4, FIRST["ff"], s * 8 + 44, False)
            relu2(0, FIRST["ff"] + 8 * (SLABS2 - 1), 44 + 8 * (SLABS2 - 1), True)
            spread(5, 2)
            dve.wait_ge(rb_done, 6)
            for kc in range(KD):
                dve.scalar_tensor_tensor(x[:, kc, 0:S], x[:, kc, 0:S], vcol(V_F2, kc), ps_a[:, 2, 0:S], ALU.mult, ALU.mult)\
                   .then_inc(x_normed, 1)

        @block.tensor
        def _(pe):
            def turn(dst, src, n=P):
                return pe.transpose(dst, src, ident[0:n, 0:n])

            def stat(n, tiles):
                for kc in (0, KD - 2, KD - 1):
                    pe.wait_ge(sq_ready, KD * n + kc + 1)
                    if kc == 0:
                        pe.wait_ge(sq_sums, 5 * (n + 1))
                    for t in range(tiles):
                        ins = pe.matmul(ps_a[:, 3, t:t + 1], sq[:, kc, t * P:(t + 1) * P], ones[:, 0:1],
                                        start=(kc == 0 and t == 0), stop=(kc == KD - 1 and t == tiles - 1))
                ins.then_inc(stat_done, 1)

            def spread(n, tiles):
                pe.wait_ge(diag_done, n + 1)
                pe.matmul(ps_a[:, 2, 0:tiles * P], ones[:], t1[:, 0, 0:tiles * P], start=True, stop=True).then_inc(rb_done, 1)

            def mod(pr, k, b, lag):
                pe.wait_ge(drained, 2 * pr + (k + 3 - lag))
                dst = ps_a[0:MOD_ROWS, b, 0:2 * P]
                for kc in range(KD):
                    if kc in (0, 4):
                        pe.wait_ge(l_ready, 4 * pr + (2 * k + 5 + kc // 4))
                    cols = slice(kc * 2 * P, (kc + 1) * 2 * P)
                    pe.matmul(dst, sc_pad[:, kc, :], w_hi[:, k % 2, cols], start=(kc == 0), stop=False)
                    ins = pe.matmul(dst, sc_pad[:, kc, :], w_lo[:, k % 2, cols], start=False, stop=(kc == KD - 1))
                    if kc in (3, KD - 1):
                        ins.then_inc(halves_done, 1)

            def unit(pr, k, operand, n=S, kcs=KD, ready=None, b=None, lag=2, parts=1):
                pe.wait_ge(drained, 2 * pr + (k + 3 - lag))
                b = k % 2 if b is None else b
                span = kcs // parts
                for i in range(kcs):
                    if i in (0, 4):
                        pe.wait_ge(l_ready, 4 * pr + (2 * k + 5 + i // 4))
                    part, kc = divmod(i, span)
                    if ready is not None and part == 0:
                        ready(kc)
                    for t in range(2):
                        dst = ps_u[:, 2 * b + t, part * n:(part + 1) * n]
                        lo = i * 2 * P + t * P
                        wh, wl = w_hi[:, k % 2, lo:lo + P], w_lo[:, k % 2, lo:lo + P]
                        xh, xl = operand(kc, t)
                        pe.matmul(dst, wh, xh, start=(kc == 0), stop=False)
                        pe.matmul(dst, wh, xl, start=False, stop=False)
                        ins = pe.matmul(dst, wl, xh, start=False, stop=(kc == span - 1))
                    if i in (3, kcs - 1):
                        ins.then_inc(halves_done, 1)

            def from_x(n):
                return lambda kc, t: (x_hi[:, kc, 0:n], x_lo[:, kc, 0:n])

            def from_h(n):
                return lambda kc, t: (h_hi[:, kc, 0:n], h_lo[:, kc, 0:n])

            def both_h(kc, t):
                cols = slice(t * S, (t + 1) * S)
                return h_hi[:, kc, cols], h_lo[:, kc, cols]

            def normed(i):
                return lambda kc: pe.wait_ge(xl_ready, 8 * i + kc + 1)

            def drained_at(pr, k, per=1, step=1):
                return lambda kc: pe.wait_ge(drained, 2 * pr + (k + step * (kc // per) + 3))

            def swiglu(base, i, n):
                def slab(s, pr, k, chunks):
                    with pe.Fori(0, chunks // 2) as p:
                        for j in range(2):
                            unit(pr + p, k + j, from_x(n), n, ready=normed(i))
                    for o in range(4):
                        unit(pr, k + chunks + o, from_h(n), n, chunks, ready=drained_at(pr, k) if o == 0 else None)

                with pe.Fori(0, 2) as s:
                    slab(s, s * 6, base, SLABS[0])
                slab(2, 0, base + 24, SLABS[2])

            pe.drain().then_inc(halves_done, 4)
            pe.wait_ge(ones_ready, 1)
            pe.wait_ge(pad_ready, 3)
            for u in range(MOD_FRONT):
                mod(0, u, u % 2, 2)
                if u == 3:
                    stat(0, 4)
                if u == 5:
                    spread(0, 4)

            def slab1(pr, k, chunks):
                with pe.Fori(0, chunks // 2) as p:
                    for j in range(2):
                        unit(pr + 2 * p, k + 2 * j, from_x(NB), NB, ready=normed(0), b=j, lag=4 - j)
                        mod(pr + 2 * p, k + 2 * j + 1, j, 3)
                ko = k + 2 * chunks

                def before_taken(kc):
                    if kc == chunks - 1:
                        pe.wait_ge(drained, 2 * pr + (ko + 7))

                for i, o in enumerate((0, None, 1, None, 2, 3)):
                    if o is None:
                        mod(pr, ko + i, (i // 2) % 2, 3)
                    else:
                        unit(pr, ko + i, from_h(NB), NB, chunks, b=o % 2, lag=3 if o == 3 else 4,
                             ready={0: drained_at(pr, k, 1, 2), 3: before_taken}.get(o))

            k = FIRST["ffn1"]
            with pe.Fori(0, 2) as s:
                slab1(s * 11, k, SLABS[0])
            slab1(0, k + 44, SLABS[2])
            stat(1, 4)
            spread(1, 4)

            k = FIRST["k"]
            unit(0, k, from_x(NB), NB, ready=normed(1))
            unit(0, k + 1, from_x(NB), NB)
            pe.wait_ge(k_squared, 2)
            for t in range(HKV):
                for c in range(4):
                    at = 8 + 4 * t + c
                    ins = pe.matmul(ps_a[:, 1, at:at + 1], s1[:, t, c * P:(c + 1) * P], ones[:, 0:1], start=True, stop=True)
            ins.then_inc(kstat_done, 1)

            def turn_v(t):
                for c in range(4):
                    ins = turn(ps_a[:, 0, c * P:(c + 1) * P], v_feat[:, t, c * P:(c + 1) * P])
                ins.then_inc(v_turned, 1)

            kq = FIRST["q"]
            unit(0, kq, from_x(S))
            pe.wait_ge(drained, k + 4)
            turn_v(0)
            unit(0, kq + 1, from_x(S))
            pe.wait_ge(kdiag_done, 1)
            for t in range(HKV):
                pe.matmul(ps_a[:, 2 + t, :], ones[:], t1[:, t, :], start=True, stop=True).then_inc(krb_done, 1)
            unit(0, kq + 2, from_x(S))
            for t in range(HKV):
                pe.wait_ge(k_normed, t + 1)
                pe.matmul(ps_a[:, 2 + t, 0:S], swap1, k_all[:, t, 0:S], start=True, stop=True).then_inc(k_swapped, 1)
            pe.wait_ge(v_ready, 1)
            turn_v(1)
            unit(0, kq + 3, from_x(S))
            pe.wait_ge(q_squared, HQ)
            for h in range(HQ):
                for t in range(TT):
                    at = 16 + TT * h + t
                    ins = pe.matmul(ps_a[:, 1, at:at + 1], q_sq[:, h, t * P:(t + 1) * P], ones[:, 0:1], start=True, stop=True)
            ins.then_inc(qstat_done, 1)

            pe.wait_ge(k_ready, 2)
            with pe.Fori(0, 4) as p:
                for j in range(2):
                    kg = FIRST["gates"] + j
                    unit(p, kg, from_x(S))
                    if j == 0:
                        pe.wait_ge(drained, FIRST["gates"] + 2)
                    pe.matmul(ps_a[:, 2 + j, 0:S], swap1, q_rows[:, 2 * p + j, :], start=True, stop=True)\
                      .then_inc(q_swapped, 1)

            pe.wait_ge(q_scaled, 1)
            pe.wait_ge(v_ready, 2)

            def scores1(h, j, g, first=False):
                pe.wait_ge(qcur_ready, h + 1)
                if not first:
                    pe.wait_ge(exp_done, 2 * h)
                for qt in range(TT):
                    ins = pe.matmul(ps_a[:, qt, :], q_cur[:, j, qt * P:(qt + 1) * P], k_all[:, g, :], start=True, stop=True)
                ins.then_inc(qk_done, 1)

            def turns1(h):
                pe.wait_ge(o1_done, h + 1)
                for qt in range(TT):
                    pe.wait_ge(p_ready, 2 * h + (qt + 1))
                    for c in range(4):
                        ins = turn(ps_a[:, 2 + qt, c * P:(c + 1) * P], probs[:, qt, c * P:(c + 1) * P])
                    ins.then_inc(t_done, 1)

            def weighted1(h, g):
                pe.wait_ge(pta_ready, h + 1)
                pe.wait_ge(ptd_ready, h + 1)
                for c in range(4):
                    ins = pe.matmul(ps_a[:, 2, 0:S], v_tok[:, c, g, :], probs_t[:, c, :], start=(c == 0), stop=(c == 3))
                ins.then_inc(pv_done, 1)

            def head1(pr, i, g, g_before):
                h = 2 * pr + i
                scores1(h, i % 2, g)
                turns1(h - 1)
                unit(pr, FIRST["conv"] + i, from_x(S))
                weighted1(h - 1, g_before)

            scores1(0, 0, 0, first=True)
            unit(0, FIRST["conv"], from_x(S))
            with pe.Fori(0, 2) as p:
                head1(p, 1, 0, 0)
                head1(p, 2, p, 0)
            for h in range(GROUP + 1, HQ):
                head1(0, h, 1, 1)
            turns1(HQ - 1)
            with pe.Fori(0, 2) as p:
                for j in range(2):
                    unit(p, FIRST["bg"] + j, from_x(S))
            weighted1(HQ - 1, 1)

            def branches_ready(kc):
                pe.wait_ge(drained, FIRST["bg"] + kc // 2 + 3)
                pe.wait_ge(o1_done, kc + 2)

            with pe.Fori(0, 4) as p:
                for j in range(2):
                    unit(p, FIRST["merge"] + j, both_h, ready=branches_ready)
            with pe.Fori(0, 2) as p:
                for j in range(2):
                    unit(p, FIRST["wout"] + j, from_x(S), ready=drained_at(0, FIRST["merge"]))

            stat(2, 2)
            spread(2, 2)
            swiglu(FIRST["ffn2"], 2, S)
            stat(3, 4)
            spread(3, 4)

            k = FIRST["kcvc"]
            unit(0, k, from_x(S), ready=normed(3))
            pe.wait_ge(wg_ready, 1)
            dst = ps_a[0:3 * H2, 1, 0:S]
            for kc in range(KD):
                pe.matmul(dst, wg_hi[:, kc, :], x_hi[:, kc, 0:S], start=(kc == 0), stop=False)
                pe.matmul(dst, wg_hi[:, kc, :], x_lo[:, kc, 0:S], start=False, stop=False)
                ins = pe.matmul(dst, wg_lo[:, kc, :], x_hi[:, kc, 0:S], start=False, stop=(kc == KD - 1))
            ins.then_inc(gt_done, 1)

            def hidden(i):
                pe.wait_ge(cmp_landed[i], 32)
                if i == 0:
                    pe.wait_ge(cmp_ready, 1)
                else:
                    pe.wait_ge(drained, k + 3)
                    pe.wait_ge(gelu_done, 1)
                for l in range(CS):
                    ins = pe.matmul(ps_a[0:G2 * NC, 0, i * CH:(i + 1) * CH], cmp_in[i][:, l, :, :].rearrange("p g c -> p (g c)"),
                                    cmp_w[i][:, l // 8, (l % 8) * CH:(l % 8 + 1) * CH], start=(l == 0), stop=(l == CS - 1))
                ins.then_inc(hid_done, 1)

            def swap_rows(rows, b):
                pe.matmul(ps_a[:, b, 0:rows.shape[-1]], swap2, rows, start=True, stop=True).then_inc(rope2_swapped, 1)

            unit(0, k + 1, from_x(S))
            pe.wait_ge(gt_sig, 1)
            for t in range(TT):
                ins = turn(ps_a[:, 1, t * 3 * H2:(t + 1) * 3 * H2], g_feat[:, t * P:(t + 1) * P], 3 * H2)
            ins.then_inc(gt_turned, 1)
            hidden(0)
            unit(0, k + 2, from_x(S))
            hidden(1)
            unit(0, k + 3, from_x(S))
            pe.wait_ge(drained, k + 5)
            pe.wait_ge(x_scaled, 1)
            for b in range(2):
                swap_rows(kk2[:, b * S:(b + 1) * S], 2 + b)
            pe.wait_ge(gt_ready, 1)
            for b in range(2):
                for c in range(2):
                    ins = turn(ps_a[:, 1, (2 * b + c) * P:(2 * b + c + 1) * P], v2_feat[:, b, c * P:(c + 1) * P])
            ins.then_inc(v2_turned, 1)
            pe.wait_ge(gelu_done, 2)
            for i in range(2):
                for half in range(2):
                    c = (2 * i + half) * G2 * NC
                    ins = turn(ps_a[:, 0, c:c + G2 * NC], hid_rows[:, i, half * P:(half + 1) * P], G2 * NC)
            ins.then_inc(hid_turned, 1)
            unit(0, k + 4, from_x(S))
            pe.wait_ge(hid_copied, 1)
            for g in range(G2):
                for half in range(2):
                    ins = pe.matmul(ps_a[g * DH:(g + 1) * DH, 0, 128:128 + NC], w2c[:, 0, half, :],
                                    hid[:, 0, half, g * NC:(g + 1) * NC], start=(half == 0), stop=(half == 1))
            ins.then_inc(cmp_done, 1)
            for g in range(G2):
                for half in range(2):
                    ins = pe.matmul(ps_a[0:NC, 0, 256 + g * DH:256 + (g + 1) * DH], hid[:, 1, half, g * NC:(g + 1) * NC],
                                    w2c[:, 1, half, :], start=(half == 0), stop=(half == 1))
            ins.then_inc(cmp_done, 1)
            unit(0, k + 5, from_x(S))
            pe.wait_ge(kv2_copied, 2)
            for r in range(2):
                pe.wait_ge(rope2_done, r + 1)
                swap_rows(q2[:, r, :], 2 + r % 2)
            pe.wait_ge(v2_ready, 1)
            pe.wait_ge(kc_raw, 2)
            swap_rows(kc_r[:, 0, :], 1)
            unit(0, k + 6, from_x(S))
            for r in range(2, 4):
                pe.wait_ge(rope2_done, r + 1)
                swap_rows(q2[:, r, :], 2 + r % 2)
            pe.wait_ge(rope2_done, 5)

            def scores(h, r, g, first=False):
                rows = slice(g * DH, (g + 1) * DH)
                if g == 0:
                    pe.wait_ge(qcur_ready, HQ + r + 1)
                if not first:
                    pe.wait_ge(exp_done, 2 * HQ + h)
                q = [q_cur[rows, 0, qt * P:(qt + 1) * P] for qt in range(TT)]
                own = kk2[rows, :].rearrange("p (b n) -> p b n", b=2)[:, :, 0:P]
                pe.matmul(ps_a[:, 1, 0:2 * P].rearrange("p (b n) -> p b n", b=2), q[0], own, start=True, stop=True)
                for qt in range(TT):
                    pe.matmul(ps_a[:, 1, 2 * P + qt * 16:2 * P + qt * 16 + NC], q[qt], kc_r[rows, 1, :], start=True, stop=True)
                pe.matmul(ps_a[:, 0, :], q[1], kk2[rows, :], start=True, stop=True).then_inc(qk_done, 1)

            def turns(h, first=False):
                pe.wait_ge(p_ready, 2 * HQ + h + 1)
                if first:
                    pe.wait_ge(rope2_done, 7)
                else:
                    pe.wait_ge(o2_done, h)
                for b in range(2):
                    for kt in range(2):
                        c = 2 * b + kt
                        turn(ps_a[:, 2, c * P:(c + 1) * P], probs_hi[:, b, kt * P:(kt + 1) * P])
                for b in range(2):
                    turn(ps_a[:, 3, b * P:(b + 1) * P], probs_lo[:, b, :])
                for qt in range(TT):
                    ins = turn(ps_a[:, 3, (2 + qt) * P:(3 + qt) * P], pc[:, qt, :])
                ins.then_inc(t_done, 1)

            def weighted(h, g):
                rows = slice(g * DH, (g + 1) * DH)
                pe.wait_ge(pta_ready, HQ + h + 1)
                pe.wait_ge(ptd_ready, HQ + h + 1)
                for b in range(2):
                    pe.matmul(ps_a[rows, 2, 0:S], v2_tok[:, b, 0, rows], probs_t[:, 2 * b, :], start=(b == 0), stop=False)
                    pe.matmul(ps_a[rows, 2, P:S], v2_tok[:, b, 1, rows], probs_t[:, 2 * b + 1, P:S], start=False, stop=False)
                pe.matmul(ps_a[rows, 2, 0:S], vc_tok[:, g, :], q_cur[:, 1, :], start=False, stop=True).then_inc(pv_done, 1)

            def head(h, r, g, second=False):
                scores(h, r, g)
                turns(h - 1, second)
                unit(r, FIRST["gates2"] + g, from_x(S))
                weighted(h - 1, 1 - g)

            scores(0, 0, 0, first=True)
            unit(0, FIRST["gates2"], from_x(S))
            head(1, 0, 1, second=True)
            head(2, 1, 0)
            with pe.Fori(1, 3) as p:
                head(2 * p + 1, p, 1)
                head(2 * p + 2, p + 1, 0)
            head(7, 3, 1)
            turns(7)
            for i in range(4):
                pe.wait_ge(pooled_ready, i + 1)
                pe.wait_ge(ph_done, 2 * i - 3) if i >= 2 else pe.wait_ge(exp_done, 2 * HQ + H2)
                pe.matmul(ps_a[:, i % 2, 0:S], w_pool[:, i, :], pooled[:, i, :], start=True, stop=True).then_inc(mixed_done, 1)
            weighted(7, 1)
            pe.wait_ge(pl_done, 4)

            def rows_done(kc):
                pe.wait_ge(o2_done, 2 * kc + 2)

            with pe.Fori(0, 2) as p:
                for j in range(2):
                    unit(p, FIRST["merge2"] + j, both_h, ready=rows_done, parts=2)
            with pe.Fori(0, 2) as p:
                for j in range(2):
                    unit(p, FIRST["wout2"] + j, from_x(S), ready=drained_at(0, FIRST["merge2"], 2))
            stat(4, 2)
            spread(4, 2)
            with pe.Fori(0, SLABS2) as s:
                with pe.Fori(0, 2) as p:
                    for j in range(2):
                        unit(s * 4 + p, FIRST["ff"] + j, from_x(S), ready=normed(4))
                with pe.Fori(0, 2) as p:
                    for j in range(2):
                        unit(s * 4 + p, FIRST["ff"] + 4 + j, from_h(S), ready=drained_at(s * 4, FIRST["ff"], 2))
            stat(5, 2)
            spread(5, 2)


def constants():
    import numpy as np
    f = np.float32
    t = np.zeros((P, K_END), f)
    t[:, K_ID:K_ID + P] = np.eye(P, dtype=f)
    n = HD // 4
    for ax in range(2):
        for i in range(n):
            lo, hi = ax * 2 * n + i, ax * 2 * n + n + i
            t[hi, K_R1 + lo] = -1.0
            t[lo, K_R1 + hi] = 1.0
    inv = (f(10000.0) ** (-np.arange(n, dtype=f) / f(n))).astype(f)
    tok = np.arange(S)
    for ax, pos in enumerate((tok // 64, tok % 64)):
        ang = (pos.astype(f)[:, None] * inv).astype(f).T
        for half in range(2):
            rows = slice(ax * 2 * n + half * n, ax * 2 * n + (half + 1) * n)
            t[rows, K_C1:K_C1 + S] = np.cos(ang)
            t[rows, K_S1:K_S1 + S] = np.sin(ang)
    rot = DH // 4
    inv = (f(500000.0) ** (-np.arange(0, rot, 2, dtype=f) / f(rot))).astype(f)
    ang = (tok.astype(f)[:, None] * inv).astype(f).T
    t[:, K_C2:K_C2 + S] = 1.0
    for g in range(G2):
        for i in range(rot // 2):
            lo, hi = g * DH + i, g * DH + rot // 2 + i
            t[hi, K_R2 + lo] = -1.0
            t[lo, K_R2 + hi] = 1.0
            for row in (lo, hi):
                t[row, K_C2:K_C2 + S] = np.cos(ang[i])
                t[row, K_S2:K_S2 + S] = np.sin(ang[i])
    last = np.arange(NC) * CS + CB - 1
    t[:, K_MASK:K_MASK + P] = np.where(tok[None, :P] <= tok[:P, None], 0.0, -1e30)
    for qt in range(TT):
        q = qt * P + np.arange(P)
        seen = last[None, :] <= q[:, None]
        t[:, K_CADD + qt * NC:K_CADD + (qt + 1) * NC] = np.where(seen, 0.0, -1e30)
        t[:, K_CMUL + qt * NC:K_CMUL + (qt + 1) * NC] = seen
    for i, w in enumerate(POOLS):
        t[:, K_CNT + i * PAD:K_CNT + (i + 1) * PAD] = f(1.0) / np.minimum(np.arange(PAD) + 1, w).astype(f)
    t[:, K_EPS] = EPS
    return t


def lay_out(i):
    import numpy as np
    f = np.float32

    def rows(w, kc0=0, kcs=KD):
        return np.asarray(w)[kc0 * P:(kc0 + kcs) * P].reshape(kcs, P, -1).transpose(1, 0, 2)

    def feature_major(v):
        return np.asarray(v, f).reshape(-1, P).T

    stream = np.zeros((UNITS, P, SLOT), f)
    unit = iter(range(UNITS))

    def put(tile0, tile1):
        u = np.concatenate([tile0, tile1], axis=2)
        stream[next(unit), :, :u.shape[1] * 2 * P] = u.reshape(P, -1)

    def wide(w, col, kc0=0, kcs=KD):
        tiles = rows(w, kc0, kcs)[:, :, col:col + 2 * P]
        put(tiles[:, :, :P], tiles[:, :, P:])

    def pair(w0, col0, w1, col1):
        put(rows(w0)[:, :, col0:col0 + P], rows(w1)[:, :, col1:col1 + P])

    def swiglu(w_in, w_out, ride):
        m = MOD_FRONT
        for s, chunks in enumerate(SLABS):
            for c in range(chunks):
                col = (8 * s + c) * P
                pair(w_in, col, w_in, col + D_FF)
                if ride:
                    wide(w_mod, m * 2 * P)
                    m += 1
            for o in range(4):
                wide(w_out, o * 2 * P, 8 * s, chunks)
                if ride and o < 2:
                    wide(w_mod, m * 2 * P)
                    m += 1

    w_mod, w_in, w_in2 = i["w_mod"][0], i["w_in"][0], i["w_in_2"][0]
    for m in range(MOD_FRONT):
        wide(w_mod, m * 2 * P)
    swiglu(i["ffn1_w_in"][0], i["ffn1_w_out"][0], True)
    for col in (C_K, C_V, *range(C_Q, C_K, 2 * P)):
        wide(w_in, col)
    for m in range(KD):
        pair(w_in, C_GATE + m * P, w_in, C_GATE + D + m * P)
    for m in range(KD):
        pair(w_in, C_CG + m * P, w_in, C_VC + m * P)
    for col in range(C_BG, C_CG, 2 * P):
        wide(w_in, col)
    for m in range(KD):
        pair(i["w_branch_conv"][0], m * P, i["w_branch_attn"][0], m * P)
    for col in range(0, D, 2 * P):
        wide(i["w_out"][0], col)
    swiglu(i["ffn2_w_in"][0], i["ffn2_w_out"][0], False)
    for col in (C2_KC, C2_KS, C2_KW, 0, 2 * P, C2_POOL, C2_POOL + 2 * P):
        wide(w_in2, col)
    for m in range(KD):
        pair(w_in2, C2_MERGE + m * P, w_in2, C2_MERGE + D + m * P)
    w_ba2 = np.asarray(i["w_branch_attn_2"][0]).reshape(G2, R2H, DH, D).transpose(0, 2, 1, 3).reshape(P, R2H, D)
    w_bp2 = rows(i["w_branch_pool_2"][0], 0, 4)
    for m in range(0, KD, 2):
        cols = [slice((m + j) * P, (m + j + 1) * P) for j in range(2)]
        put(*(np.concatenate([w[:, :, c] for c in cols], axis=1) for w in (w_ba2, w_bp2)))
    for col in range(0, D, 2 * P):
        wide(i["w_out_2"][0], col)
    for s in range(SLABS2):
        for o in range(4):
            wide(i["w_ff1_2"][0], s * 8 * P + o * 2 * P)
        for o in range(4):
            wide(i["w_ff2_2"][0], o * 2 * P, 8 * s)

    cmp_w = np.concatenate([np.asarray(i[name][0]).reshape(2, 2, CS // 2, DH, CH).transpose(1, 0, 3, 2, 4).reshape(2, P, SLOT)
                            for name in ("cmp_k_w1_2", "cmp_v_w1_2")])
    pe = np.concatenate([np.tile(np.asarray(i[name][0]).T, (2, 1)) for name in ("cmp_pe_k_2", "cmp_pe_v_2")], axis=1)
    vectors = np.concatenate([feature_major(i[name]) for name in (
        "c", "c_ctx", "norm1_g", "norm2_g", "norm3_g", "final_g", "norm_mix_2", "norm_mlp_2", "norm_final_2", "conv_w",
        "pool_scale_2", "q_norm_g", "k_norm_g", "b_mod")] + [pe], axis=1)
    late = np.concatenate(
        [rows(w_in2)[:, :, C2_GATE:C2_POOL].reshape(P, -1),
         np.asarray(i["pool_w_2"][0]).transpose(1, 0, 2).reshape(P, -1)]
        + [np.asarray(i[name][0]).reshape(2, P, DH).transpose(1, 0, 2).reshape(P, -1) for name in ("cmp_k_w2_2", "cmp_v_w2_2")],
        axis=1)
    tokens = np.concatenate([np.asarray(i["x"][0]), np.asarray(i["ctx"][0])]).T.reshape(KD, P, NB).transpose(1, 0, 2)
    return {"stream": stream, "cmp_w": cmp_w, "vectors": vectors, "late": late, "tokens": tokens, "consts": constants()}


def kernel(**inputs):
    import numpy as np
    import concourse.bacc as bacc
    from concourse.bass_utils import run_bass_kernel_spmd as run

    nc = bacc.Bacc("TRN2", target_bir_lowering=False, num_devices=1)
    arrays = {f"in_{name}": np.ascontiguousarray(arr) for name, arr in lay_out(inputs).items()}
    args = {name[3:]: nc.dram_tensor(name, arr.shape, mybir.dt.from_np(arr.dtype), kind="ExternalInput").ap()
            for name, arr in arrays.items()}
    out = nc.dram_tensor("out", (P, KD, S), F32, kind="ExternalOutput").ap()
    program(nc, args, out)
    r = run(nc, [arrays], core_ids=[0])
    return r.results[0]["out"].transpose(2, 1, 0).reshape(1, S, D)
```
